# Optimizing a Trainium2 kernel written in Bass

```python
import jax, jax.numpy as jnp
from jax import lax
import numpy as np

D_MODEL = 2048
BATCH = 1
SEQ = 256
DEPTH = 2

GRID_W = 64
EPS = 1e-6
ATT_HEADS = 8
ATT_KV_HEADS = 2
ATT_HEAD_DIM = D_MODEL // 16
ROPE_THETA = 10000.0
Q_BLOCK = 128
ML_HEADS = 4
ML_HEAD_DIM = D_MODEL // 8
ML_CHUNK = 128
CONV_W = 5
POOL_WINDOWS = (2, 4, 8, 16)
POOL_GROUPS = 4
POOL_DIM = D_MODEL // POOL_GROUPS
PEER_HEADS = 8
PEER_NKEYS = 128
PEER_EXPERTS = PEER_NKEYS * PEER_NKEYS
PEER_TOPK = 16
PEER_DKEY = 256
PEER_BLOCK = 128

N_EVEN = (DEPTH + 1) // 2
N_ODD = DEPTH // 2

ATT_Q = ATT_HEADS * ATT_HEAD_DIM
ATT_KV = ATT_KV_HEADS * ATT_HEAD_DIM
ML_W = ML_HEADS * ML_HEAD_DIM
N_GATE_COLS = 4 * ML_HEADS
MIX_W = ATT_Q + ML_W
IN_SPLITS = [ATT_Q, ATT_Q + ATT_KV, ATT_Q + 2 * ATT_KV, ATT_Q + 2 * ATT_KV + 2 * ML_W,
             ATT_Q + 2 * ATT_KV + 3 * ML_W, ATT_Q + 2 * ATT_KV + 4 * ML_W]
IN_WIDTH = ATT_Q + 2 * ATT_KV + 4 * ML_W + N_GATE_COLS

kernel_name = 'hybrid_gqa_mlstm_pool_peer_encoder'

def rmsnorm(x, g):
    xf = x.astype(jnp.float32)
    y = xf * lax.rsqrt(jnp.mean(xf * xf, axis=-1, keepdims=True) + EPS)
    return (y * g.astype(jnp.float32)).astype(x.dtype)

def axial_rope_tables(seq):
    rows = seq // GRID_W
    r, c = jnp.meshgrid(jnp.arange(rows), jnp.arange(GRID_W), indexing='ij')
    pos = jnp.stack([r.reshape(-1), c.reshape(-1)], axis=-1).astype(jnp.float32)
    nf = ATT_HEAD_DIM // 4
    inv = ROPE_THETA ** (-jnp.arange(nf, dtype=jnp.float32) / nf)
    ang = pos[:, :, None] * inv
    return jnp.cos(ang), jnp.sin(ang)

def apply_rope(x, cos, sin):
    b, h, s, d = x.shape
    xr = x.reshape(b, h, s, 2, 2, d // 4)
    x1, x2 = xr[..., 0, :], xr[..., 1, :]
    c, sn = cos.astype(x.dtype), sin.astype(x.dtype)
    out = jnp.stack([x1 * c - x2 * sn, x2 * c + x1 * sn], axis=-2)
    return out.reshape(b, h, s, d)

def gqa_attention(q, k, v):
    b, hq, s, d = q.shape
    g = hq // ATT_KV_HEADS
    nb = s // Q_BLOCK
    qb = q.reshape(b, ATT_KV_HEADS, g, nb, Q_BLOCK, d).transpose(3, 0, 1, 2, 4, 5)
    scale = d ** -0.5

    def block(qi):
        sc = jnp.einsum('bkgqd,bksd->bkgqs', qi, k).astype(jnp.float32) * scale
        p = jax.nn.softmax(sc, axis=-1).astype(v.dtype)
        return jnp.einsum('bkgqs,bksd->bkgqd', p, v)

    o = lax.map(block, qb)
    return o.transpose(1, 0, 4, 2, 3, 5).reshape(b, s, hq * d)

def centred_dwconv(x, w):
    s = x.shape[1]
    p = CONV_W // 2
    xp = jnp.pad(x, ((0, 0), (p, p), (0, 0)))
    return sum(xp[:, j:j + s] * w[j] for j in range(CONV_W))

def mlstm_chunkwise(q, k, v, i_pre, logf):
    b, h, s, d = q.shape
    L = ML_CHUNK
    nc = s // L
    q, k, v = (t.reshape(b, h, nc, L, d) for t in (q, k, v))
    i_pre = i_pre.reshape(b, h, nc, L)
    logf = logf.reshape(b, h, nc, L)
    bcum = jnp.cumsum(logf, axis=-1)
    g = bcum[..., -1]
    a = g[..., None] - bcum + i_pre
    a_max = jnp.max(a, axis=-1)
    w = jnp.exp(a - a_max[..., None])
    C_loc = jnp.einsum('bhcl,bhcld,bhcle->bhcde', w, k, v)
    n_loc = jnp.einsum('bhcl,bhcld->bhcd', w, k)

    def step(carry, xs):
        C, n, m = carry
        g_c, am_c, Cl, nl = xs
        m_new = jnp.maximum(g_c + m, am_c)
        dec = jnp.exp(g_c + m - m_new)
        add = jnp.exp(am_c - m_new)
        C_new = dec[..., None, None] * C + add[..., None, None] * Cl
        n_new = dec[..., None] * n + add[..., None] * nl
        return (C_new, n_new, m_new), (C, n, m)

    init = (jnp.zeros((b, h, d, d), jnp.float32), jnp.zeros((b, h, d), jnp.float32),
            jnp.zeros((b, h), jnp.float32))
    xs = (jnp.moveaxis(g, 2, 0), jnp.moveaxis(a_max, 2, 0),
          jnp.moveaxis(C_loc, 2, 0), jnp.moveaxis(n_loc, 2, 0))
    _, (C_prev, n_prev, m_prev) = lax.scan(step, init, xs)
    C_prev = jnp.moveaxis(C_prev, 0, 2)
    n_prev = jnp.moveaxis(n_prev, 0, 2)
    m_prev = jnp.moveaxis(m_prev, 0, 2)

    lower = jnp.tril(jnp.ones((L, L), bool))
    Dlog = bcum[..., :, None] - bcum[..., None, :] + i_pre[..., None, :]
    Dlog = jnp.where(lower, Dlog, -jnp.inf)
    inter_log = bcum + m_prev[..., None]
    m_j = jnp.maximum(inter_log, jnp.max(Dlog, axis=-1))
    Sqk = jnp.einsum('bhcjd,bhcrd->bhcjr', q, k) * jnp.exp(Dlog - m_j[..., None])
    inter_w = jnp.exp(inter_log - m_j)
    num = (inter_w[..., None] * jnp.einsum('bhcjd,bhcde->bhcje', q, C_prev)
           + jnp.einsum('bhcjr,bhcre->bhcje', Sqk, v))
    den = inter_w * jnp.einsum('bhcjd,bhcd->bhcj', q, n_prev) + jnp.sum(Sqk, axis=-1)
    out = num / jnp.maximum(jnp.abs(den), jnp.exp(-m_j))[..., None]
    return out.reshape(b, h, s, d)

def mlstm_bidir(q, k, v, i_f, f_f, i_b, f_b):
    h_fwd = mlstm_chunkwise(q, k, v, i_f, jax.nn.log_sigmoid(f_f))
    rev = lambda t: jnp.flip(t, axis=2)
    h_bwd = rev(mlstm_chunkwise(rev(q), rev(k), rev(v), rev(i_b), jax.nn.log_sigmoid(rev(f_b))))
    return h_fwd + h_bwd

def attn_mlstm_mixer(xn, w_in, b_gate, conv_w, q_gain, k_gain, ml_gain, w_out):
    b, s, _ = xn.shape
    f32 = jnp.float32
    proj = xn @ w_in
    aq, ak, av, mqk, mv, mo, gates = jnp.split(proj, IN_SPLITS, axis=-1)
    heads = lambda t, nh: t.reshape(b, s, nh, -1).transpose(0, 2, 1, 3)

    cos, sin = axial_rope_tables(s)
    q = apply_rope(rmsnorm(heads(aq, ATT_HEADS), q_gain), cos, sin)
    k = apply_rope(rmsnorm(heads(ak, ATT_KV_HEADS), k_gain), cos, sin)
    v = heads(av, ATT_KV_HEADS)
    y_att = gqa_attention(q, k, v)

    mqk = jax.nn.silu(centred_dwconv(mqk, conv_w))
    mq, mk = jnp.split(mqk, 2, axis=-1)
    mq = heads(mq, ML_HEADS).astype(f32)
    mk = heads(mk, ML_HEADS).astype(f32) * (ML_HEAD_DIM ** -0.5)
    mvh = heads(mv, ML_HEADS).astype(f32)
    gates = (gates + b_gate).astype(f32).transpose(0, 2, 1)
    i_f, f_f, i_b, f_b = jnp.split(gates, 4, axis=1)
    hm = mlstm_bidir(mq, mk, mvh, i_f, f_f, i_b, f_b)
    hm = rmsnorm(hm, ml_gain.reshape(ML_HEADS, 1, ML_HEAD_DIM))
    hm = hm.transpose(0, 2, 1, 3).reshape(b, s, ML_W)
    y_ml = (hm * jax.nn.sigmoid(mo.astype(f32))).astype(xn.dtype)

    return jnp.concatenate([y_att, y_ml], axis=-1) @ w_out

def multiscale_pool_mixer(xn, pool_w, layer_scale):
    b, s, d = xn.shape
    xf = xn.astype(jnp.float32)
    cs = jnp.concatenate([jnp.zeros((b, 1, d), jnp.float32), jnp.cumsum(xf, axis=1)], axis=1)
    cs = cs.reshape(b, s + 1, POOL_GROUPS, POOL_DIM)
    t = jnp.arange(s)[:, None]
    half = jnp.array([w // 2 for w in POOL_WINDOWS], jnp.int32)[None, :]
    lo = jnp.clip(t - half, 0, s)
    hi = jnp.clip(t + half, 0, s)
    grp = jnp.arange(POOL_GROUPS)[None, :]
    win_sum = cs[:, hi, grp] - cs[:, lo, grp]
    count = (hi - lo).astype(jnp.float32)[..., None]
    pooled = win_sum / count - xf.reshape(b, s, POOL_GROUPS, POOL_DIM)
    y = jnp.einsum('bsgc,gcd->bsgd', pooled.astype(xn.dtype), pool_w).reshape(b, s, d)
    return y * layer_scale

def peer_ffn(xn, w_query, sub_keys, u, v):
    b, s, d = xn.shape
    K = PEER_TOPK
    q = (xn @ w_query).reshape(b, s, PEER_HEADS, 2, PEER_DKEY // 2)
    sc = jnp.einsum('bshpc,hpnc->bshpn', q, sub_keys).astype(jnp.float32)
    s_top, i_top = lax.top_k(sc, K)
    cand = (s_top[..., 0, :, None] + s_top[..., 1, None, :]).reshape(b, s, PEER_HEADS, K * K)
    cand_idx = (i_top[..., 0, :, None] * PEER_NKEYS + i_top[..., 1, None, :]).reshape(b, s, PEER_HEADS, K * K)
    best, pos = lax.top_k(cand, K)
    expert = jnp.take_along_axis(cand_idx, pos, axis=-1)
    gate = jax.nn.softmax(best, axis=-1).astype(xn.dtype)
    nb = (b * s) // PEER_BLOCK
    xs = (xn.reshape(nb, PEER_BLOCK, d),
          expert.reshape(nb, PEER_BLOCK, PEER_HEADS * K),
          gate.reshape(nb, PEER_BLOCK, PEER_HEADS * K))

    def block(args):
        xt, e, g = args
        act = jax.nn.gelu(jnp.einsum('tkd,td->tk', u[e], xt), approximate=False)
        return jnp.einsum('tk,tkd->td', g * act, v[e])

    return lax.map(block, xs).reshape(b, s, d)

def setup_inputs(seed: int = 0) -> dict:
    key = jax.random.key(seed)
    ks = jax.random.split(key, 20)
    f32 = jnp.float32
    nrm = lambda k, shape, scale: jax.random.normal(k, shape, f32) * scale
    gain = lambda k, shape: 1.0 + 0.02 * jax.random.normal(k, shape, f32)
    f_bias = jnp.linspace(3.0, 6.0, ML_HEADS, dtype=f32)
    zeros_h = jnp.zeros((ML_HEADS,), f32)
    gate_base = jnp.concatenate([zeros_h, f_bias, zeros_h, f_bias])
    return {
        'x': nrm(ks[0], (BATCH, SEQ, D_MODEL), 1.0),
        'norm_mix_g': gain(ks[1], (DEPTH, D_MODEL)),
        'norm_ffn_g': gain(ks[2], (DEPTH, D_MODEL)),
        'w_in': nrm(ks[3], (N_EVEN, D_MODEL, IN_WIDTH), D_MODEL ** -0.5),
        'b_gate': gate_base[None, :] + nrm(ks[4], (N_EVEN, N_GATE_COLS), 0.1),
        'conv_w': nrm(ks[5], (N_EVEN, CONV_W, 2 * ML_W), CONV_W ** -0.5),
        'q_gain': gain(ks[6], (N_EVEN, ATT_HEAD_DIM)),
        'k_gain': gain(ks[7], (N_EVEN, ATT_HEAD_DIM)),
        'ml_gain': gain(ks[8], (N_EVEN, ML_W)),
        'w_out': nrm(ks[9], (N_EVEN, MIX_W, D_MODEL), MIX_W ** -0.5),
        'pool_w': nrm(ks[10], (N_ODD, POOL_GROUPS, POOL_DIM, POOL_DIM), POOL_DIM ** -0.5),
        'layer_scale': gain(ks[11], (N_ODD, D_MODEL)),
        'peer_wq': nrm(ks[12], (DEPTH, D_MODEL, PEER_HEADS * PEER_DKEY), D_MODEL ** -0.5),
        'peer_keys': nrm(ks[13], (DEPTH, PEER_HEADS, 2, PEER_NKEYS, PEER_DKEY // 2), (PEER_DKEY // 2) ** -0.5),
        'peer_u': nrm(ks[14], (DEPTH, PEER_EXPERTS, D_MODEL), D_MODEL ** -0.5),
        'peer_v': nrm(ks[15], (DEPTH, PEER_EXPERTS, D_MODEL), PEER_HEADS ** -0.5),
        'norm_f': gain(ks[16], (D_MODEL,)),
    }

def reference(x, norm_mix_g, norm_ffn_g, w_in, b_gate, conv_w, q_gain, k_gain, ml_gain,
              w_out, pool_w, layer_scale, peer_wq, peer_keys, peer_u, peer_v, norm_f):
    h = x
    for layer in range(DEPTH):
        hn = rmsnorm(h, norm_mix_g[layer])
        if layer % 2 == 0:
            e = layer // 2
            h = h + attn_mlstm_mixer(hn, w_in[e], b_gate[e], conv_w[e], q_gain[e], k_gain[e],
                                     ml_gain[e], w_out[e])
        else:
            o = layer // 2
            h = h + multiscale_pool_mixer(hn, pool_w[o], layer_scale[o])
        h = h + peer_ffn(rmsnorm(h, norm_ffn_g[layer]), peer_wq[layer], peer_keys[layer],
                         peer_u[layer], peer_v[layer])
    return rmsnorm(h, norm_f)


_drawn_inputs = setup_inputs


def setup_inputs(seed=0):
    import zlib

    import numpy as np

    out = dict(_drawn_inputs(seed))
    spreads = {}
    factors = {'q_gain': 4.66,
     'k_gain': 4.803,
     'layer_scale': 26.133,
     'norm_f': 24.415,
     'ml_gain': 10.47,
     'norm_ffn_g': 2.932}
    for name, (base, spread) in spreads.items():
        noise = np.random.default_rng([zlib.crc32(name.encode()), seed]).standard_normal(out[name].shape)
        drawn = base * np.exp(spread * noise) if base else spread * noise
        out[name] = __import__('jax').numpy.asarray(drawn.astype(out[name].dtype))
    for name, factor in factors.items():
        out[name] = (out[name] * factor).astype(out[name].dtype)
    return out
```

```python
from contextlib import ExitStack

import concourse.bass as bass
from concourse import mybir

fp32 = mybir.dt.float32
u32 = mybir.dt.uint32
ALU = mybir.AluOpType
ACT = mybir.ActivationFunctionType
X = mybir.AxisListType.X

P = 128
D = 2048
TB = 2
S = TB * P
KC = D // P
LAYERS = 2
EPS = 1e-6
AH, AKV, AD = 8, 2, 128
MH, MD = 4, 256
CW = 5
PAD = CW // 2
PH, PK, NK = 8, 16, 128
EXPERTS = NK * NK
NEG = -3.0e38
ARENA = 41344
BANK = 512

NT = 2 * MH * MD // BANK
R_MV = 0
R_AK = R_MV + MH * MD
R_AQ = R_AK + AKV * AD
R_AV = R_AQ + AH * AD
R_MO = R_AV + AKV * AD
RAW = R_MO + MH * MD
NR = RAW // BANK
NO = D // BANK

UR, VR = 4, 4
DR = 4
GROUPS = TB * PH
POOLW = (2, 4, 8, 16)


def hybrid_encoder(nc, x, consts, poolm, w_proj, w_gates, w_out, b_gate, conv_w, q_gain, k_gain,
                   ml_gain, gains, layer_scale, pool_w, wq, keys, pu0, pv0, pu1, pv1, out):
    pu, pv = [pu0, pu1], [pv0, pv1]
    with ExitStack() as ctx:
        def sb(name, shape, dt=fp32):
            return ctx.enter_context(nc.sbuf_tensor(name, shape, dt))

        def sem(name):
            return ctx.enter_context(nc.semaphore(name))

        h = sb("h", [P, TB, D])
        xnT = sb("xnT", [P, KC, S])
        gB = sb("gB", [P, D])
        cst = sb("cst", [P, 1040])
        ident, tri_f, tri_b, ones, mask_f, mask_b = (cst[:, i * P:(i + 1) * P] for i in range(6))
        masks = cst[:, 4 * P:6 * P].rearrange("p (d r) -> p d r", d=2)
        rope_c = cst[:, 6 * P:7 * P].rearrange("p (t a f) -> p t a f", t=TB, a=2)
        rope_s = cst[:, 7 * P:8 * P].rearrange("p (t a f) -> p t a f", t=TB, a=2)
        iota16 = cst[:, 8 * P:8 * P + PK]
        stat = sb("stat", [P, 8])
        ss, ms, rt, rs = (stat[:, 2 * i:2 * i + 2] for i in range(4))
        arena = sb("arena", [P, ARENA])
        psum = [ctx.enter_context(nc.psum_tensor(f"bank{i}", [P, BANK], fp32)) for i in range(8)]

        def carver(at=0):
            place = [at]

            def carve(*shape):
                n = 1
                for d in shape:
                    n *= d
                v = arena[:, place[0]:place[0] + n]
                place[0] += n
                assert place[0] <= ARENA, place[0]
                if len(shape) == 1:
                    return v
                names = "abcd"[:len(shape)]
                return v.rearrange(f"p ({' '.join(names)}) -> p {' '.join(names)}",
                                   **{c: d for c, d in zip(names[:-1], shape[:-1])})
            return carve

        carve = carver()
        wbuf = carve(2, KC // 2, BANK)
        raw = carve(TB, RAW)
        mqkT = carve(2 * MH * 2, S + 2 * PAD)
        yT = carve(KC, S)
        cv = carve(2, S)
        Em = carve(TB, 2, MH, P)
        kw = carve(TB, MH, MD)
        hm = carve(TB, MH, MD)
        Csb = carve(2, 2, MD + 1)
        Isb = carve(2, MD + 1)
        num2 = carve(MD + 1)
        A = carve(2, 2, P)
        AT = carve(2, 2, P)
        qkr = carve(1 + 1, 10 * AD // 2)
        aT = carve(AKV + AH, S)
        Pb = carve(2, S)
        PT = carve(2, 2, P)
        mlg = carve(MH * MD)
        gB_q, gB_k = carve(AD), carve(AD)
        cvw = carve(2 * MH * 2 * CW)
        wg = carve(KC, 4 * MH)
        bgB = carve(4 * MH)
        gsb = carve(TB, 2, 2, MH)
        lf, bc, scol, Mx, mprev = (carve(TB, 2, MH) for _ in range(5))
        G = carve(TB, 2, MH)
        smax, c1 = carve(2, MH), carve(2, MH)
        eabs, elog = carve(TB, 2, MH), carve(TB, 2, MH)
        expi = carve(2 * 2 * TB * MH + 2 * MH)
        expo = carve(2 * 2 * TB * MH + 2 * MH)
        dd, dr = carve(2), carve(2)
        sq1, sq2 = carve(TB, 10), carve(TB, MH)
        sqt = carve(MD)
        mxs, nmx, psm, prc = carve(2), carve(2), carve(2), carve(2)
        nrm0 = yT.rearrange("p a b -> p (a b)").rearrange("p (t d) -> p t d", t=TB)
        rtmp = hm.rearrange("p t m c -> p (t m c)")[:, 0:10 * AD].rearrange("p (a b) -> p a b", a=2)

        carve = carver()
        U = carve(UR, D)
        V = carve(VR, D)
        wqb = carve(KC, 2 * P)
        xn1 = carve(D)
        xcur = carve(D)
        keysT = carve(2 * PH, NK)
        qT = carve(2, S)
        poolw = carve(4, 4, BANK)
        diag = carve(DR, P)
        act = carve(2, PK)
        ga = carve(PK)
        wk = carve(2, PK)
        gates = carve(GROUPS, PK)
        s16 = carve(4, PK)
        i16f = carve(4, PK)
        stmp = carve(4, NK)
        cand, cand2 = carve(TB, PK, PK), carve(TB, PK, PK)
        b16, bd, ex = carve(TB, PK), carve(TB, PK), carve(TB, PK)
        abf = carve(4, PK)
        eq = carve(4, PK, PK)
        ev = carve(TB, 2, PK)
        exs, exr = carve(TB), carve(TB)
        flat = U.rearrange("p a b -> p (a b)")
        PM = flat[:, 0:2048].rearrange("p (g t s) -> p g t s", g=4, t=TB)
        lsB = flat[:, 2048:4096]
        ytmp = flat[:, 4096:4096 + 2 * BANK].rearrange("p (a b) -> p a b", a=2)
        xns = [xcur, xn1]
        idx_all = sb("idx_all", [P, GROUPS, PK], u32)
        idxU = [sb(f"idxU{i}", [P, PK], u32) for i in range(2)]
        idxV = [sb(f"idxV{i}", [P, PK], u32) for i in range(2)]
        i16 = sb("i16", [P, 4, PK], u32)
        pos = sb("pos", [P, TB, PK], u32)
        ab = sb("ab", [P, TB, 2, PK], u32)

        ld_x, ld_c, ld_small, ld_gain, ld_keys, ld_wq, ld_pool, ld_pm = (
            sem(n) for n in ("ld_x", "ld_c", "ld_small", "ld_gain", "ld_keys", "ld_wq", "ld_pool", "ld_pm"))
        w_got = [sem("w_got0"), sem("w_got1")]
        u_got = [sem(f"u_got{i}") for i in range(UR)]
        v_got = [sem(f"v_got{i}") for i in range(VR)]
        out_done = sem("out_done")
        dve = sem("dve")
        names = """sq_done root_done ms_done xn_ready tp_done xt_act xt_dve gain_used gates_mm gsum
            abs_done lf_ready w_used mqk_done mqk_evac conv_done silu_done raw_done raw_evac cum_done
            scol_ready srow_done kscaled ktp_done expi_ready expo_done em_sub em_ready kw_ready s_mm a_ready at_mm
            at_ready c_mm c_ready i_mm i_ready n_mm comb_done y_sq y_ms y_root q_sq q_ms q_root
            rope_done atp_mm atp_ready sc_mm nmax p_exp p_ready pt_mm pt_ready pv_mm yt_ready mo_sig
            hm_ready ymt_mm ymt_ready h_ready act_self act_passed dve_passed
            keys_used wq_used q_mm q_ready sc_done sc_free bd_ready ex_done idxu_ready idxv_ready
            dot_done gelu_done wk_ready diag_ready v_mm acc_evac u_go v_go
            pool_mm pool_ev py_mm h1_ready fin_ready pmix_done""".split()
        s = {n: sem(n) for n in names}

        def hold(eng, semaphore, value, passed):
            eng.wait_ge(semaphore, value)
            eng.sem_inc(passed, 1)

        class Steps:

            def __init__(self):
                self.base, self.n = 0, 0

            def link(self, eng, ins):
                self.n += 1
                ins.then_inc(dve, 1)
                if isinstance(self.base, int):
                    eng.wait_ge(dve, self.base + self.n)
                else:
                    hold(eng, dve, self.base + self.n, s["dve_passed"])

        block = ctx.enter_context(nc.Block())

        NORM_T = {0: 0, 1: 1, 3: 2}

        @block.sync
        def _(sp):
            sp.dma_start(h[:, 0, :], x[0:P, :]).then_inc(ld_x, 16)
            sp.dma_start(h[:, 1, :], x[P:S, :]).then_inc(ld_x, 16)
            sp.dma_start(gB[:], gains[0].partition_broadcast(P)).then_inc(ld_gain, 16)
            sp.dma_start(cst[:], consts).then_inc(ld_c, 16)
            sp.dma_start(wg, w_gates.rearrange("p (k c) -> p k c", k=KC)).then_inc(ld_small, 16)
            sp.dma_start(bgB, b_gate.partition_broadcast(P)).then_inc(ld_small, 16)
            sp.dma_start(cvw, conv_w).then_inc(ld_small, 16)
            for hf in range(2):
                sp.dma_start(wbuf[:, hf].rearrange("p k c -> p (k c)"), w_proj[0, hf]).then_inc(w_got[hf], 16)
            sp.dma_start(mlg, ml_gain.partition_broadcast(P)).then_inc(ld_small, 16)
            sp.dma_start(gB_q, q_gain.partition_broadcast(P)).then_inc(ld_small, 16)
            sp.dma_start(gB_k, k_gain.partition_broadcast(P)).then_inc(ld_small, 16)
            with sp.Fori(1, NT + NR) as n:
                for hf in range(2):
                    sp.wait_ge(s["w_used"], 2 * n + hf - 1)
                    sp.dma_start(wbuf[:, hf].rearrange("p k c -> p (k c)"),
                                 w_proj[bass.ds(n, 1), hf].rearrange("a p c -> (a p) c")).then_inc(w_got[hf], 16)
            sp.wait_ge(s["xn_ready"], 2)
            sp.dma_start(gB[:], gains[1].partition_broadcast(P)).then_inc(ld_gain, 16)
            with sp.Fori(0, NO) as n:
                for hf in range(2):
                    sp.wait_ge(s["w_used"], 2 * (NT + NR) - 1 + 2 * n + hf)
                    sp.dma_start(wbuf[:, hf].rearrange("p k c -> p (k c)"),
                                 w_out[bass.ds(n, 1), hf].rearrange("a p c -> (a p) c")).then_inc(w_got[hf], 16)
            sp.wait_ge(s["h_ready"], TB * NO)
            sp.dma_start(poolw, pool_w.rearrange("p (g k c) -> p g k c", g=4, k=4)).then_inc(ld_pool, 16)
            for L in range(LAYERS):
                if L:
                    sp.wait_ge(s["sc_done"], PH)
                sp.dma_start(keysT, keys[L].rearrange("p (a n) -> p a n", a=2 * PH)).then_inc(ld_keys, 16)
                if L:
                    sp.wait_ge(s["q_mm"], PH * L)
                sp.dma_start(wqb.rearrange("p k c -> p (k c)"), wq[L, 0]).then_inc(ld_wq, 16)
                if L == 0:
                    sp.wait_ge(s["xn_ready"], 4)
                    sp.dma_start(gB[:], gains[2].partition_broadcast(P)).then_inc(ld_gain, 16)
                else:
                    sp.wait_ge(s["xn_ready"], 8)
                    sp.dma_start(gB[:], gains[4].partition_broadcast(P)).then_inc(ld_gain, 16)
                with sp.Fori(1, PH) as hd:
                    sp.wait_ge(s["q_mm"], hd + PH * L)
                    sp.dma_start(wqb.rearrange("p k c -> p (k c)"),
                                 wq[L, bass.ds(hd, 1)].rearrange("a p c -> (a p) c")).then_inc(ld_wq, 16)
                if L == 0:
                    sp.wait_ge(s["dot_done"], GROUPS * PK)
                    sp.dma_start(PM.rearrange("p g t s -> p (g t s)"), poolm).then_inc(ld_pm, 16)
                    sp.dma_start(lsB, layer_scale.partition_broadcast(P)).then_inc(ld_pm, 16)
                    sp.wait_ge(s["xn_ready"], 6)
                    sp.dma_start(gB[:], gains[3].partition_broadcast(P)).then_inc(ld_gain, 16)
            for t in range(TB):
                sp.wait_ge(s["fin_ready"], t + 1)
                sp.dma_start(out[t * P:(t + 1) * P, :], h[:, t, :]).then_inc(out_done, 16)
            sp.wait_ge(out_done, 16 * TB)

        @block.gpsimd
        def _(pool):
            def gather_u(L, g, par, k, first=False):
                n = g * PK + k
                if L or not first or k >= UR:
                    pool.wait_ge(s["dot_done"], L * GROUPS * PK + n - UR + 1)
                pool.sem_inc(s["u_go"], 1)
                if k == 0:
                    pool.wait_ge(s["idxu_ready"], L * GROUPS + g + 1)
                    pool.sem_inc(s["u_go"], 1)
                nc.gpsimd.indirect_dma_start(
                    U[:, k % UR], None, pu[L], bass.IndirectOffsetOnAxis(idxU[par][:, k:k + 1], 0)
                ).then_inc(u_got[k % UR], 16)

            def gather_v(L, g, par, k, first=False):
                n = g * PK + k
                if L or not first or k >= VR:
                    pool.wait_ge(s["v_mm"], L * GROUPS * PK + n - VR + 1)
                pool.sem_inc(s["v_go"], 1)
                if k == 0:
                    pool.wait_ge(s["idxv_ready"], L * GROUPS + g + 1)
                    pool.sem_inc(s["v_go"], 1)
                nc.gpsimd.indirect_dma_start(
                    V[:, k % VR], None, pv[L], bass.IndirectOffsetOnAxis(idxV[par][:, k:k + 1], 0)
                ).then_inc(v_got[k % VR], 16)

            def step(L, j, par, first=False):
                for k in range(PK):
                    gather_u(L, j + 1, 1 - par, k)
                    gather_v(L, j, par, k, first=first)

            for L in range(LAYERS):
                if L:
                    pool.wait_ge(s["pmix_done"], 1)
                for k in range(PK):
                    gather_u(L, 0, 0, k, first=True)
                step(L, 0, 0, first=True)
                step(L, 1, 1)
                with pool.Fori(1, 3) as jj:
                    step(L, 2 * jj, 0)
                    step(L, 2 * jj + 1, 1)
                with pool.Fori(3, 7) as jj:
                    step(L, 2 * jj, 0)
                    step(L, 2 * jj + 1, 1)
                step(L, 14, 0)
                for k in range(PK):
                    gather_v(L, 15, 1, k)

        @block.scalar
        def _(act_e):
            e = act_e

            def norm(o):
                dst = [nrm0[:, 0], nrm0[:, 1]] if o == 0 else xns
                if o:
                    e.wait_ge(s["xt_act"], 4 * NORM_T.get(min(o, 3), 2) if o < 4 else 12)
                for t in range(TB):
                    if o == 0:
                        e.wait_ge(ld_x, 32)
                    elif o == 1:
                        e.wait_ge(s["h_ready"], TB * NO)
                    elif o == 3:
                        e.wait_ge(s["h1_ready"], 8)
                    else:
                        e.wait_ge(s["acc_evac"], 8 * (o // 2))
                        e.wait_ge(s["dot_done"], GROUPS * PK * (o // 2))
                        e.wait_ge(s["v_mm"], GROUPS * PK * (o // 2))
                    nc.scalar.activation(dst[t], h[:, t, :], ACT.Square, accum_out=ss[:, t:t + 1]).then_inc(s["sq_done"], 1)
                e.wait_ge(s["ms_done"], o + 1)
                nc.scalar.activation(rt, ms, ACT.Sqrt).then_inc(s["root_done"], 1)

            def evac_xt(o):
                for t in range(TB):
                    for q in (0, 2):
                        n = 8 * o + 4 * t + q
                        e.wait_ge(s["tp_done"], n + 1)
                        nc.scalar.activation(xnT[:, 4 * q:4 * q + 4, t * P:(t + 1) * P],
                                             psum[4 + q % 4][:, :].rearrange("p (a b) -> p a b", a=4), ACT.Copy
                                             ).then_inc(s["xt_act"], 1)

            norm(0)
            evac_xt(0)
            e.wait_ge(s["gsum"], 1)
            nc.scalar.activation(eabs, gsb[:, :, :, 1], ACT.Abs).then_inc(s["act_self"], 1)
            e.wait_ge(s["act_self"], 1)
            nc.scalar.activation(elog, eabs, ACT.Exp, scale=-1.0).then_inc(s["act_self"], 1)
            e.wait_ge(s["act_self"], 2)
            nc.scalar.activation(eabs, elog, ACT.Ln, bias=1.0).then_inc(s["abs_done"], 1)
            e.sem_inc(s["mqk_evac"], 4)
            e.sem_inc(s["raw_evac"], 2)
            with e.Fori(0, NT) as n:
                for i in range(4):
                    hold(e, s["mqk_done"], 4 * n + i + 1, s["act_passed"])
                    nc.scalar.activation(mqkT[:, bass.ds(4 * n + i, 1), PAD:PAD + S].rearrange("p a b -> p (a b)"),
                                         psum[i][:, 0:S], ACT.Copy).then_inc(s["mqk_evac"], 1)
                for i in range(4):
                    hold(e, s["conv_done"], 4 * n + i + 1, s["act_passed"])
                    nc.scalar.activation(mqkT[:, bass.ds(4 * n + i, 1), PAD:PAD + S].rearrange("p a b -> p (a b)"),
                                         cv[:, i % 2], ACT.Silu).then_inc(s["silu_done"], 1)

            def evac_raw(n0, n1):
                with e.Fori(n0, n1) as n:
                    for t in range(TB):
                        hold(e, s["raw_done"], 2 * n + t + 1, s["act_passed"])
                        nc.scalar.activation(raw[:, t, bass.ds(n * BANK, BANK)], psum[4 + t][:, :], ACT.Copy
                                             ).then_inc(s["raw_evac"], 1)

            evac_raw(0, 2)
            e.wait_ge(s["expi_ready"], 1)
            nc.scalar.activation(expo, expi, ACT.Exp).then_inc(s["expo_done"], 1)
            e.wait_ge(s["em_sub"], 1)
            nc.scalar.activation(Em.rearrange("p a b c d -> p (a b c d)"), Em.rearrange("p a b c d -> p (a b c d)"),
                                 ACT.Exp).then_inc(s["em_ready"], 1)
            e.wait_ge(s["expo_done"], 1)
            for t in range(TB):
                for hp in range(2):
                    e.wait_ge(s["ktp_done"], 2 * t + hp + 1)
                    for i in range(2):
                        hd = 2 * hp + i
                        nc.scalar.activation(kw[:, t, hd], psum[6 + hp][:, i * MD:(i + 1) * MD], ACT.Copy,
                                             scale=expo[:, 32 + 4 * t + hd:33 + 4 * t + hd]).then_inc(s["kw_ready"], 1)
            evac_raw(2, NR)
            e.wait_ge(s["raw_evac"], 2 + 2 * NR)
            nc.scalar.activation(raw[:, :, R_MO:RAW], raw[:, :, R_MO:RAW], ACT.Sigmoid).then_inc(s["mo_sig"], 1)
            for t in range(TB):
                for i in range(10):
                    n = 10 * t + i
                    if n:
                        e.wait_ge(s["q_sq"], n)
                    nc.scalar.activation(sqt[:, 0:AD], raw[:, t, R_AK + i * AD:R_AK + (i + 1) * AD], ACT.Square,
                                         accum_out=sq1[:, t, i:i + 1]).then_inc(s["q_sq"], 1)
            e.wait_ge(s["q_ms"], 1)
            nc.scalar.activation(sq1, sq1, ACT.Sqrt).then_inc(s["q_root"], 1)
            for n in range(6):
                t, q = n // 3, n % 3
                m = 4 if q < 2 else 2
                e.wait_ge(s["atp_mm"], n + 1)
                nc.scalar.activation(aT[:, 4 * q:4 * q + m, t * P:(t + 1) * P],
                                     psum[n % 2][:, 0:m * P].rearrange("p (a b) -> p a b", a=m), ACT.Copy
                                     ).then_inc(s["atp_ready"], 1)
            for i in range(9):
                if i < 8:
                    hd, t = i // 2, i % 2
                    for c in range(2):
                        e.wait_ge(s["c_mm"], 2 * i + c + 1)
                        if i >= 2:
                            e.wait_ge(s["i_mm"], i - 1)
                        nc.scalar.activation(Csb[:, i % 2, c], psum[3 + c][:, 0:MD + 1], ACT.Copy).then_inc(s["c_ready"], 1)
                if i:
                    u = i - 1
                    hd, t = u // 2, u % 2
                    e.wait_ge(s["at_mm"], u + 1)
                    if u >= 2:
                        e.wait_ge(s["n_mm"], 2 * (u - 1))
                    nc.scalar.activation(AT[:, u % 2], psum[2][:, 0:2 * P].rearrange("p (a b) -> p a b", a=2),
                                         ACT.Copy).then_inc(s["at_ready"], 1)
                    e.wait_ge(s["i_mm"], u + 1)
                    if u >= 2:
                        e.wait_ge(s["comb_done"], u - 1)
                    w = (t * 2 + (1 - t)) * MH + hd
                    nc.scalar.activation(Isb[:, u % 2], psum[5][:, 0:MD + 1], ACT.Copy,
                                         scale=expo[:, w:w + 1]).then_inc(s["i_ready"], 1)
            e.wait_ge(s["comb_done"], 8)
            for t in range(TB):
                for hd in range(MH):
                    e.wait_ge(s["y_sq"], 4 * t + hd) if t + hd else None
                    if t + hd == 0:
                        e.wait_ge(s["q_sq"], 20)
                    nc.scalar.activation(sqt, hm[:, t, hd], ACT.Square, accum_out=sq2[:, t, hd:hd + 1]).then_inc(s["y_sq"], 1)
            e.wait_ge(s["y_ms"], 1)
            nc.scalar.activation(sq2, sq2, ACT.Sqrt).then_inc(s["y_root"], 1)
            for i in range(16 + 2):
                if i < 16:
                    e.wait_ge(s["nmax"], i + 1)
                    if i >= 2:
                        e.wait_ge(s["pt_mm"], i - 1)
                    nc.scalar.activation(Pb[:, i % 2], psum[i % 2][:, 0:S], ACT.Exp, bias=nmx[:, i % 2:i % 2 + 1],
                                         scale=AD ** -0.5, accum_out=psm[:, i % 2:i % 2 + 1]).then_inc(s["p_exp"], 1)
                if 1 <= i <= 16:
                    u = i - 1
                    e.wait_ge(s["pt_mm"], u + 1)
                    if u >= 2:
                        e.wait_ge(s["pv_mm"], u - 1)
                    nc.scalar.activation(PT[:, u % 2], psum[2 + u % 2][:, 0:2 * P].rearrange("p (a b) -> p a b", a=2),
                                         ACT.Copy).then_inc(s["pt_ready"], 1)
                if i >= 2:
                    u = i - 2
                    hd, t = u // 2, u % 2
                    e.wait_ge(s["pv_mm"], u + 1)
                    nc.scalar.activation(yT[:, hd, t * P:(t + 1) * P], psum[4 + u % 2][:, 0:P], ACT.Copy
                                         ).then_inc(s["yt_ready"], 1)
            for n in range(4):
                t, q = n // 2, n % 2
                e.wait_ge(s["ymt_mm"], n + 1)
                nc.scalar.activation(yT[:, 8 + 4 * q:12 + 4 * q, t * P:(t + 1) * P],
                                     psum[6 + q][:, :].rearrange("p (a b) -> p a b", a=4), ACT.Copy
                                     ).then_inc(s["ymt_ready"], 1)

            def route_q(L, hd):
                e.wait_ge(s["q_mm"], L * PH + hd + 1)
                nc.scalar.activation(qT, psum[6][:, :].rearrange("p (a b) -> p a b", a=2), ACT.Copy
                                     ).then_inc(s["q_ready"], 1)

            def route_exp(L, hd):
                e.wait_ge(s["bd_ready"], L * PH + hd + 1)
                nc.scalar.activation(ex, bd, ACT.Exp).then_inc(s["ex_done"], 1)

            def step(L, j, par, route=None, first=False):
                N = L * GROUPS * PK
                e.wait_ge(s["dot_done"], N + j * PK + PK)
                nc.scalar.activation(ga, act[:, par], ACT.Gelu).then_inc(s["gelu_done"], 1)
                for k in range(PK):
                    if k == 0:
                        e.wait_ge(s["wk_ready"], L * GROUPS + j + 1)
                    if L or not first or k >= DR:
                        e.wait_ge(s["v_mm"], N + j * PK + k - DR + 1)
                    nc.scalar.activation(diag[:, k % DR], ident, ACT.Copy, scale=wk[:, par, k:k + 1]
                                         ).then_inc(s["diag_ready"], 1)
                    if route is not None and k == 5:
                        route_q(L, route)
                    if route is not None and k == 10:
                        route_exp(L, route)

            def evac_acc(L, b):
                e.wait_ge(s["v_mm"], L * GROUPS * PK + (b + 1) * PH * PK)
                for n in range(NO):
                    nc.scalar.activation(h[:, b, n * BANK:(n + 1) * BANK], psum[n][:, :], ACT.Copy
                                         ).then_inc(s["acc_evac"], 1)

            for L in range(LAYERS):
                if L:
                    norm(2)
                    for c in range(KC):
                        e.wait_ge(s["pool_mm"], c + 1)
                        nc.scalar.activation(xnT[:, c, :], psum[4 + c % 4][:, 0:S], ACT.Copy).then_inc(s["pool_ev"], 1)
                norm(1 + 2 * L)
                evac_xt(1 + L)
                for hd in range(2):
                    route_q(L, hd)
                    route_exp(L, hd)
                step(L, 0, 0, route=2, first=True)
                step(L, 1, 1, route=3)
                with e.Fori(1, 3) as jj:
                    step(L, 2 * jj, 0, route=2 * jj + 2)
                    step(L, 2 * jj + 1, 1, route=2 * jj + 3)
                step(L, 6, 0)
                step(L, 7, 1)
                evac_acc(L, 0)
                with e.Fori(4, 7) as jj:
                    step(L, 2 * jj, 0)
                    step(L, 2 * jj + 1, 1)
                step(L, 14, 0)
                step(L, 15, 1)
                evac_acc(L, 1)
            norm(4)

        @block.vector
        def _(v):
            st = Steps()
            vec = nc.vector

            def link(ins):
                st.link(v, ins)

            def norm(o):
                v.wait_ge(s["sq_done"], 2 * o + 2)
                vec.tensor_scalar(ms, ss, 1.0 / D, EPS, ALU.mult, ALU.add).then_inc(s["ms_done"], 1)
                v.wait_ge(s["root_done"], o + 1)
                link(vec.reciprocal(rs, rt))
                v.wait_ge(ld_gain, 16 * (o + 1))
                for t in range(TB):
                    dst = [nrm0[:, 0], nrm0[:, 1]][t] if o == 0 else h[:, t, :] if o == 4 else xns[t]
                    vec.scalar_tensor_tensor(dst, h[:, t, :], rs[:, t:t + 1], gB[:], ALU.mult, ALU.mult
                                             ).then_inc(s["fin_ready" if o == 4 else "xn_ready"], 1)

            def evac_xt(o):
                for t in range(TB):
                    for q in (1, 3):
                        n = 8 * o + 4 * t + q
                        v.wait_ge(s["tp_done"], n + 1)
                        vec.tensor_copy(xnT[:, 4 * q:4 * q + 4, t * P:(t + 1) * P],
                                        psum[4 + q % 4][:, :].rearrange("p (a b) -> p a b", a=4)
                                        ).then_inc(s["xt_dve"], 1)

            vec.memset(mqkT[:, :, 0:PAD], 0.0)
            link(vec.memset(mqkT[:, :, PAD + S:], 0.0))
            norm(0)
            evac_xt(0)
            v.wait_ge(ld_small, 6 * 16)
            v.wait_ge(s["gates_mm"], 1)
            g_ps = psum[6][:, 0:TB * 16].rearrange("p (t c) -> p t c", t=TB)
            g_v = gsb.rearrange("p t d x m -> p t (d x m)")
            vec.tensor_tensor(g_v, g_ps, bgB.unsqueeze(1).to_broadcast([P, TB, 16]), ALU.add).then_inc(s["gsum"], 1)
            v.wait_ge(s["gsum"], 1)
            v.wait_ge(s["abs_done"], 1)
            for t in range(TB):
                for d in range(2):
                    vec_f = gsb[:, t, d, 1]
                    last = vec.scalar_tensor_tensor(lf[:, t, d], vec_f, 0.0, eabs[:, t, d], ALU.min, ALU.subtract)
            last.then_inc(s["lf_ready"], 1)
            CONV = CW
            with v.Fori(0, 2 * MH * 2 // 2) as cc:
                v.wait_ge(s["mqk_evac"], 4 + 2 * cc + 2)
                v.wait_ge(s["silu_done"], 2 * cc)
                for j in range(CW):
                    for i in range(2):
                        src = mqkT[:, bass.ds(2 * cc + i, 1), j:j + S].rearrange("p a b -> p (a b)")
                        wc = cvw[:, bass.ds((2 * cc + i) * CW + j, 1)]
                        if j == 0:
                            ins = vec.tensor_scalar(cv[:, i], src, wc, None, ALU.mult)
                        else:
                            ins = vec.scalar_tensor_tensor(cv[:, i], src, wc, cv[:, i], ALU.mult, ALU.add)
                        if j == CW - 1:
                            ins.then_inc(s["conv_done"], 1)
                        elif i == 1:
                            ins.then_inc(dve, 1)
                            v.wait_ge(dve, st.n + cc * (CW - 1) + j + 1)
            st.n += (CW - 1) * 2 * MH
            v.wait_ge(s["silu_done"], 16)
            kk = mqkT[:, 2 * MH:4 * MH, PAD:PAD + S]
            vec.tensor_scalar(kk, kk, MD ** -0.5, None, ALU.mult).then_inc(s["kscaled"], 1)
            v.wait_ge(s["cum_done"], 1)
            w8 = TB * 2 * MH
            cum = psum[7][:, 0:w8].rearrange("p (t d m) -> p t d m", t=TB, d=2)
            tot = psum[7][:, w8:2 * w8].rearrange("p (t d m) -> p t d m", t=TB, d=2)
            vec.tensor_copy(bc, cum)
            vec.tensor_copy(G, tot)
            for t in range(TB):
                ins = vec.tensor_tensor(scol[:, t], gsb[:, t, :, 0], cum[:, t], ALU.subtract)
            link(ins)
            vec.memset(mprev, 0.0).then_inc(s["scol_ready"], 1)
            v.wait_ge(s["srow_done"], 4)
            for t in range(TB):
                for d in range(2):
                    row = psum[2 * t + d][:, :].rearrange("p (m r) -> p m r", m=MH)
                    vec.tensor_tensor(Em[:, t, d], row, masks[:, d].unsqueeze(1).to_broadcast([P, MH, P]), ALU.add)
                    if t == d:
                        vec.tensor_reduce(smax[:, d], row, X, ALU.max)
            link(vec.tensor_copy(elog[:, 0, 0], bc[:, 0, 0]))
            for t in range(TB):
                for d in range(2):
                    vec.tensor_reduce(Mx[:, t, d], Em[:, t, d], X, ALU.max)
            link(vec.tensor_scalar(c1, smax, 0.0, None, ALU.max))
            for d in range(2):
                ins = vec.tensor_tensor(mprev[:, 1 - d, d], G[:, d, d], c1[:, d], ALU.add)
            link(ins)
            link(vec.tensor_tensor(Mx, Mx, mprev, ALU.max))
            e16 = [expi[:, i * 16:(i + 1) * 16].rearrange("p (t d m) -> p t d m", t=TB, d=2) for i in range(2)]
            vec.tensor_tensor(e16[0], mprev, Mx, ALU.subtract)
            vec.scalar_tensor_tensor(e16[1].rearrange("p t d m -> p (t d m)"), bc.rearrange("p t d m -> p (t d m)"),
                                     -1.0, Mx.rearrange("p t d m -> p (t d m)"), ALU.mult, ALU.subtract)
            for d in range(2):
                ins = vec.tensor_tensor(expi[:, 32 + 4 * d:36 + 4 * d], scol[:, d, d], c1[:, d], ALU.subtract)
            ins.then_inc(s["expi_ready"], 1)
            em = Em.rearrange("p t d m r -> p (t d m) r")
            vec.tensor_tensor(em, em, Mx.rearrange("p t d m -> p (t d m)").unsqueeze(2).to_broadcast([P, 16, P]),
                              ALU.subtract).then_inc(s["em_sub"], 1)
            v.wait_ge(s["q_sq"], 20)
            vec.tensor_scalar(sq1, sq1, 1.0 / AD, EPS, ALU.mult, ALU.add).then_inc(s["q_ms"], 1)
            v.wait_ge(s["q_root"], 1)
            link(vec.reciprocal(sq1, sq1))
            for t in range(TB):
                for i in range(10):
                    hv = raw[:, t, R_AK + i * AD:R_AK + (i + 1) * AD]
                    ins = vec.scalar_tensor_tensor(hv, hv, sq1[:, t, i:i + 1], gB_k if i < AKV else gB_q,
                                                   ALU.mult, ALU.mult)
            link(ins)
            qkf = qkr.rearrange("p a b -> p (a b)")
            for t in range(TB):
                src = raw[:, t, R_AK:R_AK + 10 * AD].rearrange("p (n a x f) -> p n a x f", n=10, a=2, x=2)
                dst = qkf.rearrange("p (n a x f) -> p n a x f", n=10, a=2, x=2)
                t1, t2 = (rtmp[:, i].rearrange("p (n a f) -> p n a f", n=10, a=2) for i in range(2))
                if t:
                    v.wait_ge(s["atp_mm"], 3)
                for a in range(2):
                    cb = rope_c[:, t, a].unsqueeze(1).to_broadcast([P, 10, 32])
                    sn = rope_s[:, t, a].unsqueeze(1).to_broadcast([P, 10, 32])
                    vec.tensor_tensor(t1[:, :, a], src[:, :, a, 0], cb, ALU.mult)
                    link(vec.tensor_tensor(t2[:, :, a], src[:, :, a, 1], sn, ALU.mult))
                    link(vec.tensor_tensor(dst[:, :, a, 0], t1[:, :, a], t2[:, :, a], ALU.subtract))
                    vec.tensor_tensor(t1[:, :, a], src[:, :, a, 1], cb, ALU.mult)
                    link(vec.tensor_tensor(t2[:, :, a], src[:, :, a, 0], sn, ALU.mult))
                    ins = vec.tensor_tensor(dst[:, :, a, 1], t1[:, :, a], t2[:, :, a], ALU.add)
                    if a == 0:
                        link(ins)
                    else:
                        ins.then_inc(s["rope_done"], 1)
                v.wait_ge(s["rope_done"], t + 1)
            v.wait_ge(s["em_ready"], 1)
            for i in range(9):
                if i < 8:
                    hd, t = i // 2, i % 2
                    v.wait_ge(s["s_mm"], i + 1)
                    if i >= 2:
                        v.wait_ge(s["at_mm"], i - 1)
                    vec.tensor_tensor(A[:, i % 2], psum[i % 2][:, 0:P].unsqueeze(1).to_broadcast([P, 2, P]),
                                      Em[:, t, :, hd], ALU.mult).then_inc(s["a_ready"], 1)
                if i:
                    u = i - 1
                    hd, t = u // 2, u % 2
                    first, second = 6 + t, 6 + (1 - t)
                    v.wait_ge(s["i_ready"], u + 1)
                    v.wait_ge(s["n_mm"], 2 * (u + 1))
                    link(vec.tensor_tensor(num2, Isb[:, u % 2], psum[second][:, 0:MD + 1], ALU.add))
                    for x_, (srcd, d) in enumerate(((psum[first][:, MD:MD + 1], t), (num2[:, MD:MD + 1], 1 - t))):
                        w = 16 + (t * 2 + d) * MH + hd
                        ins = vec.scalar_tensor_tensor(dd[:, x_:x_ + 1], srcd, -1.0, expo[:, w:w + 1], ALU.mult, ALU.max)
                    link(ins)
                    vec.tensor_tensor(dd[:, 0:1], psum[first][:, MD:MD + 1], dd[:, 0:1], ALU.max)
                    link(vec.tensor_tensor(dd[:, 1:2], num2[:, MD:MD + 1], dd[:, 1:2], ALU.max))
                    link(vec.reciprocal(dr, dd))
                    link(vec.tensor_scalar(hm[:, t, hd], psum[first][:, 0:MD], dr[:, 0:1], None, ALU.mult))
                    vec.scalar_tensor_tensor(hm[:, t, hd], num2[:, 0:MD], dr[:, 1:2], hm[:, t, hd], ALU.mult, ALU.add
                                             ).then_inc(s["comb_done"], 1)
                    v.wait_ge(s["comb_done"], u + 1)
            v.wait_ge(s["y_sq"], 8)
            vec.tensor_scalar(sq2, sq2, 1.0 / MD, EPS, ALU.mult, ALU.add).then_inc(s["y_ms"], 1)
            v.wait_ge(s["y_root"], 1)
            link(vec.reciprocal(sq2, sq2))
            for t in range(TB):
                for hd in range(MH):
                    ins = vec.scalar_tensor_tensor(hm[:, t, hd], hm[:, t, hd], sq2[:, t, hd:hd + 1],
                                                   mlg[:, hd * MD:(hd + 1) * MD], ALU.mult, ALU.mult)
            link(ins)
            v.wait_ge(s["mo_sig"], 1)
            for t in range(TB):
                hf_ = hm[:, t].rearrange("p m c -> p (m c)")
                vec.tensor_tensor(hf_, hf_, raw[:, t, R_MO:RAW], ALU.mult).then_inc(s["hm_ready"], 1)
            for i in range(17):
                if i < 16:
                    v.wait_ge(s["sc_mm"], i + 1)
                    if i >= 2:
                        v.wait_ge(s["p_exp"], i - 1)
                    link(vec.tensor_reduce(mxs[:, i % 2:i % 2 + 1], psum[i % 2][:, 0:S], X, ALU.max))
                    vec.tensor_scalar(nmx[:, i % 2:i % 2 + 1], mxs[:, i % 2:i % 2 + 1], -(AD ** -0.5), None, ALU.mult
                                      ).then_inc(s["nmax"], 1)
                if i:
                    u = i - 1
                    v.wait_ge(s["p_exp"], u + 1)
                    link(vec.reciprocal(prc[:, u % 2:u % 2 + 1], psm[:, u % 2:u % 2 + 1]))
                    vec.tensor_scalar(Pb[:, u % 2], Pb[:, u % 2], prc[:, u % 2:u % 2 + 1], None, ALU.mult
                                      ).then_inc(s["p_ready"], 1)
            with v.Fori(0, NO) as n:
                for t in range(TB):
                    v.wait_ge(s["raw_done"], 2 * NR + 2 * n + t + 1)
                    hv = h[:, t, bass.ds(n * BANK, BANK)]
                    vec.tensor_tensor(hv, psum[4 + t][:, :], hv, ALU.add).then_inc(s["h_ready"], 1)

            ROUTE = 15

            def route(L, hd, exp_wait):
                n0 = L * PH + hd
                hold(v, s["sc_done"], n0 + 1, s["dve_passed"])
                sc = psum[7][:, :].rearrange("p (q n) -> p q n", q=4)
                for q in range(4):
                    ins = vec.max(s16[:, q, 0:8], sc[:, q])
                link(ins)
                for q in range(4):
                    vec.match_replace(stmp[:, q], s16[:, q, 0:8], sc[:, q], NEG)
                for q in range(4):
                    ins = vec.max_index(i16[:, q, 0:8], s16[:, q, 0:8], sc[:, q])
                ins.then_inc(s["sc_free"], 1)
                hold(v, s["sc_free"], n0 + 1, s["dve_passed"])
                for q in range(4):
                    ins = vec.max(s16[:, q, 8:16], stmp[:, q])
                link(ins)
                for q in range(4):
                    vec.max_index(i16[:, q, 8:16], s16[:, q, 8:16], stmp[:, q])
                for t in range(TB):
                    ins = vec.tensor_tensor(cand[:, t], s16[:, 2 * t].unsqueeze(2).to_broadcast([P, PK, PK]),
                                            s16[:, 2 * t + 1].unsqueeze(1).to_broadcast([P, PK, PK]), ALU.add)
                link(ins)
                vec.tensor_copy(i16f, i16[:])
                cf = cand.rearrange("p t a b -> p t (a b)")
                c2 = cand2.rearrange("p t a b -> p t (a b)")
                for t in range(TB):
                    ins = vec.max(b16[:, t, 0:8], cf[:, t])
                link(ins)
                for t in range(TB):
                    vec.match_replace(c2[:, t], b16[:, t, 0:8], cf[:, t], NEG)
                for t in range(TB):
                    ins = vec.max_index(pos[:, t, 0:8], b16[:, t, 0:8], cf[:, t])
                link(ins)
                for t in range(TB):
                    ins = vec.max(b16[:, t, 8:16], c2[:, t])
                link(ins)
                for t in range(TB):
                    vec.max_index(pos[:, t, 8:16], b16[:, t, 8:16], c2[:, t])
                vec.tensor_tensor(bd, b16, b16[:, :, 0:1].to_broadcast([P, TB, PK]), ALU.subtract
                                  ).then_inc(s["bd_ready"], 1)
                v.wait_ge(s["bd_ready"], n0 + 1)
                vec.tensor_scalar(ab[:, :, 0], pos[:], 4, None, ALU.logical_shift_right)
                link(vec.tensor_scalar(ab[:, :, 1], pos[:], PK - 1, None, ALU.bitwise_and))
                link(vec.tensor_copy(abf, ab[:].rearrange("p t x k -> p (t x) k")))
                e64 = eq.rearrange("p q k a -> p (q k) a")
                link(vec.tensor_tensor(e64, abf.rearrange("p q k -> p (q k)").unsqueeze(2).to_broadcast([P, 64, PK]),
                                       iota16.unsqueeze(1).to_broadcast([P, 64, PK]), ALU.is_equal))
                link(vec.tensor_tensor(eq, eq, i16f.unsqueeze(2).to_broadcast([P, 4, PK, PK]), ALU.mult))
                link(vec.tensor_reduce(ev.rearrange("p t x k -> p (t x k)"), e64, X, ALU.add))
                link(vec.scalar_tensor_tensor(idx_all[:, :, :].rearrange("p (t g) k -> p t g k", t=TB)[:, :, bass.ds(hd, 1)]
                                              .rearrange("p t g k -> p t (g k)"),
                                              ev[:, :, 0], float(NK), ev[:, :, 1], ALU.mult, ALU.add))
                exp_wait()
                v.wait_ge(s["ex_done"], n0 + 1)
                link(vec.tensor_reduce(exs, ex, X, ALU.add))
                link(vec.reciprocal(exr, exs))
                link(vec.tensor_tensor(gates.rearrange("p (t g) k -> p t g k", t=TB)[:, :, bass.ds(hd, 1)]
                                       .rearrange("p t g k -> p t (g k)"),
                                       ex, exr.unsqueeze(2).to_broadcast([P, TB, PK]), ALU.mult))

            def copy_idx(L, g, par, buf, name):
                vec.tensor_copy(buf[par][:], idx_all[:, bass.ds(g, 1)].rearrange("p g k -> p (g k)")
                                ).then_inc(s[name], 1)

            def dot(L, g, par, k):
                n = g * PK + k
                v.wait_ge(u_got[k % UR], 16 * (L * GROUPS * PK // UR + g * (PK // UR) + k // UR + 1))
                u = U[:, k % UR]
                vec.tensor_tensor_reduce(out=u, in0=u, in1=xcur, scale=1.0, scalar=0.0, op0=ALU.mult, op1=ALU.add,
                                         accum_out=act[:, par, k:k + 1]).then_inc(s["dot_done"], 1)

            def weigh(L, g, par):
                v.wait_ge(s["gelu_done"], L * GROUPS + g + 1)
                vec.tensor_tensor(wk[:, par], ga, gates[:, bass.ds(g, 1)].rearrange("p g k -> p (g k)"), ALU.mult
                                  ).then_inc(s["wk_ready"], 1)

            def step(L, j, par, route_head=None, last=False, switch=False):
                if switch:
                    v.wait_ge(s["dot_done"], L * GROUPS * PK + PH * PK)
                    link(vec.tensor_copy(xcur, xn1))
                for k in range(PK):
                    dot(L, j + 1, 1 - par, k)
                    if k == 0:
                        weigh(L, j, par)
                    if k == 4:
                        hold(v, s["v_mm"], L * GROUPS * PK + j * PK, s["dve_passed"])
                        copy_idx(L, j + 1, 1 - par, idxV, "idxv_ready")
                    if k == 6 and route_head is not None:
                        route(L, route_head, lambda: None)
                    if k == 7 and not last:
                        hold(v, s["dot_done"], L * GROUPS * PK + j * PK + PK, s["dve_passed"])
                        copy_idx(L, j + 2, par, idxU, "idxu_ready")

            for L in range(LAYERS):
                if L:
                    norm(2)
                    v.wait_ge(ld_pm, 32)
                    for g in range(4):
                        for t in range(TB):
                            n = 2 * g + t
                            v.wait_ge(s["py_mm"], n + 1)
                            cols = slice(g * BANK, (g + 1) * BANK)
                            link(vec.tensor_tensor(ytmp[:, t], psum[n % 4][:, :], lsB[:, cols], ALU.mult))
                            vec.tensor_tensor(h[:, t, cols], h[:, t, cols], ytmp[:, t], ALU.add).then_inc(s["h1_ready"], 1)
                    v.wait_ge(s["h1_ready"], 8)
                    v.sem_inc(s["pmix_done"], 1)
                norm(1 + 2 * L)
                evac_xt(1 + L)
                for hd in range(2):
                    route(L, hd, lambda: None)
                    copy_idx(L, hd, hd, idxU, "idxu_ready")
                copy_idx(L, 0, 0, idxV, "idxv_ready")
                for k in range(PK):
                    dot(L, 0, 0, k)
                step(L, 0, 0, route_head=2)
                step(L, 1, 1, route_head=3)
                n0 = st.n
                with v.Fori(1, 3) as jj:
                    st.base, st.n = n0 + (jj - 1) * (2 * ROUTE), 0
                    step(L, 2 * jj, 0, route_head=2 * jj + 2)
                    step(L, 2 * jj + 1, 1, route_head=2 * jj + 3)
                    assert st.n == 2 * ROUTE, st.n
                st.base, st.n = 0, n0 + 2 * 2 * ROUTE
                step(L, 6, 0)
                step(L, 7, 1, switch=True)
                with v.Fori(4, 7) as jj:
                    step(L, 2 * jj, 0)
                    step(L, 2 * jj + 1, 1)
                step(L, 14, 0, last=True)
                weigh(L, 15, 1)
            norm(4)

        @block.tensor
        def _(pe):
            mm = nc.tensor.matmul
            tr = nc.tensor.transpose

            def transpose_xn(o, norm_o, src):
                for t in range(TB):
                    pe.wait_ge(s["xn_ready"], 2 * norm_o + t + 1)
                    for q in range(4):
                        n = 8 * o + 4 * t + q
                        if t:
                            pe.wait_ge(s["xt_act" if q % 2 == 0 else "xt_dve"], 4 * o + 2 * (t - 1) + q // 2 + 1)
                        for i in range(4):
                            k = 4 * q + i
                            ins = tr(psum[4 + q][:, i * P:(i + 1) * P], src[t][:, k * P:(k + 1) * P], ident)
                        ins.then_inc(s["tp_done"], 1)

            pe.wait_ge(ld_c, 16)
            transpose_xn(0, 0, [nrm0[:, 0], nrm0[:, 1]])
            pe.wait_ge(s["xt_act"], 4)
            pe.wait_ge(s["xt_dve"], 4)
            pe.wait_ge(ld_small, 6 * 16)
            for t in range(TB):
                for k in range(KC):
                    ins = mm(psum[6][:, 16 * t:16 * t + 16], xnT[:, k, t * P:(t + 1) * P], wg[:, k], start=k == 0, stop=k == KC - 1)
            ins.then_inc(s["gates_mm"], 1)
            with pe.Fori(0, NT) as n:
                for hf in range(2):
                    pe.wait_ge(w_got[hf], 16 * (n + 1))
                    for i in range(4):
                        if hf == 0:
                            pe.wait_ge(s["mqk_evac"], 4 * n + i + 1)
                        for k in range(8):
                            ins = mm(psum[i][:, 0:S], wbuf[:, hf, k, i * P:(i + 1) * P], xnT[:, 8 * hf + k, :],
                                     start=hf == 0 and k == 0, stop=hf == 1 and k == 7)
                        if hf == 1:
                            ins.then_inc(s["mqk_done"], 1)
                    if hf == 0:
                        ins.then_inc(s["w_used"], 1)
                    else:
                        pe.wait_ge(s["mqk_done"], 4 * n + 4)
                        pe.sem_inc(s["w_used"], 1)
            pe.wait_ge(s["lf_ready"], 1)
            for t in range(TB):
                for d, tri in enumerate((tri_f, tri_b)):
                    c = (2 * t + d) * MH
                    mm(psum[7][:, c:c + MH], tri, lf[:, t, d], start=True, stop=True)
                    ins = mm(psum[7][:, 16 + c:16 + c + MH], ones, lf[:, t, d], start=True, stop=True)
            ins.then_inc(s["cum_done"], 1)

            def straight(src, n0, n1, base_w, base_r):
                with pe.Fori(n0, n1) as n:
                    for hf in range(2):
                        pe.wait_ge(w_got[hf], 16 * (base_w + n + 1))
                        for t in range(TB):
                            if hf == 0 and base_r == 0:
                                pe.wait_ge(s["raw_evac"], 2 * n + t + 1)
                            elif hf == 0:
                                pe.wait_ge(s["h_ready"], 2 * n + t - 1 + 0) if False else None
                            for k in range(8):
                                ins = mm(psum[4 + t][:, :], src[:, 8 * hf + k, t * P:(t + 1) * P], wbuf[:, hf, k],
                                         start=hf == 0 and k == 0, stop=hf == 1 and k == 7)
                            if hf == 1:
                                ins.then_inc(s["raw_done"], 1)
                        if hf == 0:
                            ins.then_inc(s["w_used"], 1)
                        else:
                            pe.wait_ge(s["raw_done"], base_r + 2 * n + 2)
                            pe.sem_inc(s["w_used"], 1)

            straight(xnT, 0, 2, NT, 0)
            pe.wait_ge(s["scol_ready"], 1)
            pe.wait_ge(s["mqk_evac"], 4 + 4 * NT)
            for t in range(TB):
                for d in range(2):
                    for m in range(MH):
                        ins = mm(psum[2 * t + d][:, m * P:(m + 1) * P], scol[:, t, d, m:m + 1].to_broadcast([P, P]), ident,
                                 start=True, stop=True)
                    ins.then_inc(s["srow_done"], 1)
            pe.wait_ge(s["kscaled"], 1)
            for t in range(TB):
                for hp in range(2):
                    if t:
                        pe.wait_ge(s["kw_ready"], 2 * hp + 2)
                    for i in range(4):
                        c = 2 * MH + 4 * hp + i
                        ins = tr(psum[6 + hp][:, i * P:(i + 1) * P], mqkT[:, c, PAD + t * P:PAD + (t + 1) * P], ident)
                    ins.then_inc(s["ktp_done"], 1)
            straight(xnT, 2, NR, NT, 0)
            for n in range(6):
                t, q = n // 3, n % 3
                pe.wait_ge(s["rope_done"], t + 1)
                if n >= 2:
                    pe.wait_ge(s["atp_ready"], n - 1)
                for i in range(4 if q < 2 else 2):
                    c = 4 * q + i
                    ins = tr(psum[n % 2][:, i * P:(i + 1) * P], qkr.rearrange("p a b -> p (a b)")[:, c * P:(c + 1) * P], ident)
                ins.then_inc(s["atp_mm"], 1)
            pe.wait_ge(s["atp_ready"], 6)
            pe.wait_ge(s["kw_ready"], 8)
            pe.wait_ge(s["raw_evac"], 2 + 2 * NR)
            pe.wait_ge(s["em_sub"], 1)
            for i in range(9):
                if i < 8:
                    hd, t = i // 2, i % 2
                    if i >= 2:
                        pe.wait_ge(s["a_ready"], i - 1)
                    for c in range(2):
                        ins = mm(psum[i % 2][:, 0:P], mqkT[:, 2 * hd + c, PAD + t * P:PAD + (t + 1) * P],
                                 mqkT[:, 2 * MH + 2 * hd + c, PAD + t * P:PAD + (t + 1) * P], start=c == 0, stop=c == 1)
                    ins.then_inc(s["s_mm"], 1)
                    d = 1 - t
                    for c in range(2):
                        if i:
                            pe.wait_ge(s["c_ready"], 2 * (i - 1) + c + 1)
                        mm(psum[3 + c][:, 0:MD], kw[:, d, hd, c * P:(c + 1) * P], raw[:, d, R_MV + hd * MD:R_MV + (hd + 1) * MD],
                           start=True, stop=True)
                        mm(psum[3 + c][:, MD:MD + 1], kw[:, d, hd, c * P:(c + 1) * P], ones[:, 0:1],
                           start=True, stop=True).then_inc(s["c_mm"], 1)
                if i:
                    u = i - 1
                    hd, t = u // 2, u % 2
                    pe.wait_ge(s["a_ready"], u + 1)
                    if u:
                        pe.wait_ge(s["at_ready"], u)
                    for d in range(2):
                        ins = tr(psum[2][:, d * P:(d + 1) * P], A[:, u % 2, d], ident)
                    ins.then_inc(s["at_mm"], 1)
                    pe.wait_ge(s["c_ready"], 2 * (u + 1))
                    if u:
                        pe.wait_ge(s["i_ready"], u)
                    for c in range(2):
                        ins = mm(psum[5][:, 0:MD + 1], mqkT[:, 2 * hd + c, PAD + t * P:PAD + (t + 1) * P],
                                 Csb[:, u % 2, c], start=c == 0, stop=c == 1)
                    ins.then_inc(s["i_mm"], 1)
                    pe.wait_ge(s["at_ready"], u + 1)
                    if u:
                        pe.wait_ge(s["comb_done"], u)
                    for d in range(2):
                        mm(psum[6 + d][:, 0:MD], AT[:, u % 2, d], raw[:, t, R_MV + hd * MD:R_MV + (hd + 1) * MD],
                           start=True, stop=True)
                        mm(psum[6 + d][:, MD:MD + 1], AT[:, u % 2, d], ones[:, 0:1], start=True, stop=True
                           ).then_inc(s["n_mm"], 1)
            for i in range(18):
                if i < 16:
                    hd, t = i // 2, i % 2
                    if i >= 2:
                        pe.wait_ge(s["p_exp"], i - 1)
                    mm(psum[i % 2][:, 0:S], aT[:, AKV + hd, t * P:(t + 1) * P], aT[:, hd // (AH // AKV)],
                       start=True, stop=True).then_inc(s["sc_mm"], 1)
                if 1 <= i <= 16:
                    u = i - 1
                    pe.wait_ge(s["p_ready"], u + 1)
                    if u >= 2:
                        pe.wait_ge(s["pt_ready"], u - 1)
                    for c in range(2):
                        ins = tr(psum[2 + u % 2][:, c * P:(c + 1) * P], Pb[:, u % 2, c * P:(c + 1) * P], ident)
                    ins.then_inc(s["pt_mm"], 1)
                if i >= 2:
                    u = i - 2
                    hd = u // 2
                    kv = hd // (AH // AKV)
                    pe.wait_ge(s["pt_ready"], u + 1)
                    if u >= 2:
                        pe.wait_ge(s["yt_ready"], u - 1)
                    for c in range(2):
                        ins = mm(psum[4 + u % 2][:, 0:P], raw[:, c, R_AV + kv * AD:R_AV + (kv + 1) * AD], PT[:, u % 2, c],
                                 start=c == 0, stop=c == 1)
                    ins.then_inc(s["pv_mm"], 1)
            for n in range(4):
                t, q = n // 2, n % 2
                pe.wait_ge(s["hm_ready"], t + 1)
                if t:
                    pe.wait_ge(s["ymt_ready"], q + 1)
                for i in range(4):
                    c = 4 * q + i
                    ins = tr(psum[6 + q][:, i * P:(i + 1) * P], hm[:, t].rearrange("p m c -> p (m c)")[:, c * P:(c + 1) * P], ident)
                ins.then_inc(s["ymt_mm"], 1)
            pe.wait_ge(s["yt_ready"], 16)
            pe.wait_ge(s["ymt_ready"], 4)
            for n in range(NO):
                for hf in range(2):
                    pe.wait_ge(w_got[hf], 16 * (NT + NR + n + 1))
                    for t in range(TB):
                        if hf == 0 and n:
                            pe.wait_ge(s["h_ready"], 2 * (n - 1) + t + 1)
                        for k in range(8):
                            ins = mm(psum[4 + t][:, :], yT[:, 8 * hf + k, t * P:(t + 1) * P], wbuf[:, hf, k],
                                     start=hf == 0 and k == 0, stop=hf == 1 and k == 7)
                        if hf == 1:
                            ins.then_inc(s["raw_done"], 1)
                    if hf == 0:
                        ins.then_inc(s["w_used"], 1)
                    else:
                        pe.wait_ge(s["raw_done"], 2 * NR + 2 * n + 2)
                        pe.sem_inc(s["w_used"], 1)

            def queries(L, hd):
                n0 = L * PH + hd
                pe.wait_ge(ld_wq, 16 * (n0 + 1))
                pe.wait_ge(s["q_ready"], n0)
                for p_ in range(2):
                    for k in range(KC):
                        ins = mm(psum[6][:, p_ * S:(p_ + 1) * S], wqb[:, k, p_ * P:(p_ + 1) * P], xnT[:, k, :],
                                 start=k == 0, stop=k == KC - 1)
                ins.then_inc(s["q_mm"], 1)

            def scores(L, hd):
                n0 = L * PH + hd
                pe.wait_ge(s["q_ready"], n0 + 1)
                pe.wait_ge(s["sc_free"], n0)
                for t in range(TB):
                    for p_ in range(2):
                        ins = mm(psum[7][:, (2 * t + p_) * P:(2 * t + p_ + 1) * P], qT[:, p_, t * P:(t + 1) * P],
                                 keysT[:, bass.ds(2 * hd + p_, 1)].rearrange("p a n -> p (a n)"), start=True, stop=True)
                ins.then_inc(s["sc_done"], 1)

            def step(L, j, route_head=None, last=False):
                N = L * GROUPS * PK
                for k in range(PK):
                    pe.wait_ge(v_got[k % VR], 16 * (N // VR + j * (PK // VR) + k // VR + 1))
                    pe.wait_ge(s["diag_ready"], N + j * PK + k + 1)
                    for n in range(NO):
                        ins = mm(psum[n][:, :], diag[:, k % DR], V[:, k % VR, n * BANK:(n + 1) * BANK],
                                 start=False, stop=last and k == PK - 1)
                    ins.then_inc(s["v_mm"], 1)
                    if route_head is not None and k == 3:
                        queries(L, route_head)
                    if route_head is not None and k == 5:
                        scores(L, route_head)

            def seed(L, b):
                for n in range(NO):
                    mm(psum[n][:, :], ident, h[:, b, n * BANK:(n + 1) * BANK], start=True, stop=False)

            for L in range(LAYERS):
                if L:
                    pe.wait_ge(s["xn_ready"], 6)
                    pe.wait_ge(ld_pm, 32)
                    for c in range(KC):
                        if c >= 4:
                            pe.wait_ge(s["pool_ev"], c - 3)
                        for t in range(TB):
                            ins = mm(psum[4 + c % 4][:, 0:S], xns[t][:, c * P:(c + 1) * P], PM[:, c // 4, t], start=t == 0, stop=t == 1)
                        ins.then_inc(s["pool_mm"], 1)
                    pe.wait_ge(ld_pool, 16)
                    for g in range(4):
                        pe.wait_ge(s["pool_ev"], 4 * g + 4)
                        for t in range(TB):
                            n = 2 * g + t
                            if n >= 4:
                                pe.wait_ge(s["h1_ready"], n - 3)
                            for c in range(4):
                                ins = mm(psum[n % 4][:, :], xnT[:, 4 * g + c, t * P:(t + 1) * P], poolw[:, g, c],
                                         start=c == 0, stop=c == 3)
                            ins.then_inc(s["py_mm"], 1)
                transpose_xn(1 + L, 1 + 2 * L, xns)
                pe.wait_ge(s["xt_act"], 4 * (2 + L))
                pe.wait_ge(s["xt_dve"], 4 * (2 + L))
                pe.wait_ge(ld_keys, 16 * (L + 1))
                for hd in range(2):
                    queries(L, hd)
                    scores(L, hd)
                seed(L, 0)
                step(L, 0, route_head=2)
                step(L, 1, route_head=3)
                with pe.Fori(1, 3) as jj:
                    step(L, 2 * jj, route_head=2 * jj + 2)
                    step(L, 2 * jj + 1, route_head=2 * jj + 3)
                step(L, 6)
                step(L, 7, last=True)
                pe.wait_ge(s["acc_evac"], 8 * L + 4)
                seed(L, 1)
                with pe.Fori(4, 7) as jj:
                    step(L, 2 * jj)
                    step(L, 2 * jj + 1)
                step(L, 14)
                step(L, 15, last=True)


def _constants(np):
    i = np.arange(P)
    tri = (i[:, None] <= i[None, :]).astype(np.float32)
    ropes = []
    tok = np.arange(S)
    posn = np.stack([tok // 64, tok % 64], -1).astype(np.float32)
    nf = AD // 4
    inv = (10000.0 ** (-np.arange(nf, dtype=np.float32) / nf)).astype(np.float32)
    ang = posn[:, :, None] * inv
    for f in (np.cos, np.sin):
        ropes.append(f(ang).astype(np.float32).reshape(TB, P, 2 * nf).transpose(1, 0, 2).reshape(P, TB * 2 * nf))
    mask = np.where(i[None, :] <= i[:, None], np.float32(0), np.float32(NEG))
    consts = np.concatenate([np.eye(P), tri, tri.T, np.ones((P, P)), mask, mask.T, *ropes,
                             np.broadcast_to(np.arange(PK), (P, PK))], 1).astype(np.float32)
    pool = np.zeros((4, S, S), np.float32)
    for g, w in enumerate(POOLW):
        for t in range(S):
            lo, hi = max(t - w // 2, 0), min(t + w // 2, S)
            pool[g, lo:hi, t] = np.float32(1.0) / np.float32(hi - lo)
            pool[g, t, t] -= 1.0
    pool = pool.reshape(4, TB, P, S).transpose(2, 0, 1, 3).reshape(P, 4 * TB * S)
    return np.ascontiguousarray(consts), np.ascontiguousarray(pool)


def kernel(**inputs):
    import numpy as np
    import concourse.bacc as bacc
    from concourse.bass_utils import run_bass_kernel_spmd

    a = {k: np.asarray(v) for k, v in inputs.items()}

    def tiles(w, halves):
        n = w.shape[1] // BANK
        return w.reshape(halves, KC // halves, P, n, BANK).transpose(3, 0, 2, 1, 4).reshape(n, halves, P, -1)

    w_in = a["w_in"][0]
    aq, ak, av = AH * AD, AH * AD + AKV * AD, AH * AD + 2 * AKV * AD
    mq, mv = av + 2 * MH * MD, av + 3 * MH * MD
    mo = mv + MH * MD
    cols = [w_in[:, av:mq], w_in[:, mq:mv], w_in[:, aq:ak], w_in[:, :aq], w_in[:, ak:av], w_in[:, mv:mo]]
    w_proj = np.concatenate(cols, 1)
    consts, poolm = _constants(np)
    arrays = {
        "x": a["x"][0],
        "consts": consts,
        "poolm": poolm,
        "w_proj": tiles(w_proj, 2),
        "w_gates": w_in[:, mo:].reshape(KC, P, 4 * MH).transpose(1, 0, 2).reshape(P, -1),
        "w_out": tiles(a["w_out"][0], 2),
        "b_gate": a["b_gate"][0],
        "conv_w": a["conv_w"][0].reshape(CW, 4 * MH, P).transpose(2, 1, 0).reshape(P, -1),
        "q_gain": a["q_gain"][0],
        "k_gain": a["k_gain"][0],
        "ml_gain": a["ml_gain"][0],
        "gains": np.stack([a["norm_mix_g"][0], a["norm_ffn_g"][0], a["norm_mix_g"][1], a["norm_ffn_g"][1], a["norm_f"]]),
        "layer_scale": a["layer_scale"][0],
        "pool_w": a["pool_w"][0].reshape(4, 4, P, BANK).transpose(2, 0, 1, 3).reshape(P, -1),
        "wq": a["peer_wq"].reshape(LAYERS, KC, P, PH, 2 * P).transpose(0, 3, 2, 1, 4).reshape(LAYERS, PH, P, -1),
        "keys": a["peer_keys"].reshape(LAYERS, 2 * PH, NK, P).transpose(0, 3, 1, 2).reshape(LAYERS, P, -1),
        "pu0": a["peer_u"][0], "pv0": a["peer_v"][0], "pu1": a["peer_u"][1], "pv1": a["peer_v"][1],
    }
    nc = bacc.Bacc("TRN2", target_bir_lowering=False, num_devices=1)
    args = []
    for name in list(arrays):
        arrays[name] = np.ascontiguousarray(arrays[name])
        args.append(nc.dram_tensor(name, arrays[name].shape, mybir.dt.from_np(arrays[name].dtype),
                                   kind="ExternalInput").ap())
    args.append(nc.dram_tensor("out", (S, D), fp32, kind="ExternalOutput").ap())
    hybrid_encoder(nc, *args)
    r = run_bass_kernel_spmd(nc, [arrays], core_ids=[0])
    return r.results[0]["out"].reshape(1, S, D)
```

```python
from contextlib import ExitStack

import concourse.bass as bass
from concourse import mybir

fp32 = mybir.dt.float32
u32 = mybir.dt.uint32
ALU = mybir.AluOpType
ACT = mybir.ActivationFunctionType
X = mybir.AxisListType.X

P = 128
D = 2048
TB = 2
S = TB * P
KC = D // P
LAYERS = 2
EPS = 1e-6
AH, AKV, AD = 8, 2, 128
MH, MD = 4, 256
CW = 5
PAD = CW // 2
PH, PK, NK = 8, 16, 128
EXPERTS = NK * NK
NEG = -3.0e38
BANK = 512

R_AK = 0
R_AQ = R_AK + AKV * AD
R_AV = R_AQ + AH * AD
R_MV = R_AV + AKV * AD
R_MO = R_MV + MH * MD
RAW = R_MO + MH * MD
N_QKV = R_MV // BANK
N_MQK = 2 * MH * MD // BANK
N_MV = MH * MD // BANK
N_IN = N_QKV + N_MQK + 2 * N_MV
NO = D // BANK
MC = MD // P
HALF = KC // 2

WR = 3
UR, VR = 4, 4
DR = 4
GROUPS = TB * PH
ROWS = GROUPS * PK
EVENTS = PH + 2
ROUTE = 15
POOLW = (2, 4, 8, 16)
ARENA = 41344
OUT_AT = 33152


def hybrid_encoder(nc, x, consts, poolm, w_proj, w_gates, w_out, b_gate, conv_w, q_gain, k_gain,
                   ml_gain, gains, layer_scale, pool_w, wq, keys, pu0, pv0, pu1, pv1, out):
    pu, pv = [pu0, pu1], [pv0, pv1]
    with ExitStack() as ctx:
        def sb(name, shape, dt=fp32):
            return ctx.enter_context(nc.sbuf_tensor(name, shape, dt))

        h = sb("h", [P, TB, D])
        xnT = sb("xnT", [P, KC, S])
        gB = sb("gB", [P, D])
        cst = sb("cst", [P, 8 * P + PK])
        ident, tri_f, tri_b, ones = (cst[:, i * P:(i + 1) * P] for i in range(4))
        masks = cst[:, 4 * P:6 * P].rearrange("p (d r) -> p d r", d=2)
        rope_c = cst[:, 6 * P:7 * P].rearrange("p (t a f) -> p t a f", t=TB, a=2)
        rope_s = cst[:, 7 * P:8 * P].rearrange("p (t a f) -> p t a f", t=TB, a=2)
        iota16 = cst[:, 8 * P:8 * P + PK]
        stat = sb("stat", [P, 8])
        ss, ms, rt, rs = (stat[:, 2 * i:2 * i + 2] for i in range(4))
        arena = sb("arena", [P, ARENA])
        psum = [ctx.enter_context(nc.psum_tensor(f"bank{i}", [P, BANK], fp32)) for i in range(8)]

        def carver(at, end):
            place = [at]

            def carve(*shape):
                if not shape:
                    return place[0]
                n = 1
                for d in shape:
                    n *= d
                v = arena[:, place[0]:place[0] + n]
                place[0] += n
                assert place[0] <= end, (place[0], end)
                if len(shape) == 1:
                    return v
                names = "abcd"[:len(shape)]
                return v.rearrange(f"p ({' '.join(names)}) -> p {' '.join(names)}",
                                   **{c: d for c, d in zip(names[:-1], shape[:-1])})
            return carve

        U = carver(0, ARENA)(UR, D)
        vring = carver(UR * D, ARENA)
        V = vring(VR, D)
        carve = vring
        wqb = carve(2, KC, 2 * P)
        xn0 = carve(D)
        keysT = carve(2 * PH, NK)
        qT = carve(2, S)
        diag = carve(DR, P)
        act = carve(2, PK)
        ga = carve(PK)
        wk = carve(2, PK)
        gates = carve(GROUPS, PK)
        s16 = carve(4, PK)
        i16f = carve(4, PK)
        stmp = carve(4, NK)
        cand, cand2 = carve(TB, PK, PK), carve(TB, PK, PK)
        b16, bd, ex = carve(TB, PK), carve(TB, PK), carve(TB, PK)
        abf = carve(4, PK)
        eq = carve(4, PK, PK)
        ev = carve(TB, 2, PK)
        exs, exr = carve(TB), carve(TB)
        xn1 = carver(OUT_AT, ARENA)(D)
        xns = [xn0, xn1]
        poolw = U.rearrange("p a b -> p (a b)").rearrange("p (g k c) -> p g k c", g=4, k=4)
        slot1 = wqb[:, 1].rearrange("p k c -> p (k c)")
        PM = slot1[:, 0:D].rearrange("p (g t s) -> p g t s", g=4, t=TB)
        lsB = slot1[:, D:2 * D]
        ytmp = eq.rearrange("p q k a -> p (q k a)").rearrange("p (a b) -> p a b", a=2)
        idx_all = sb("idx_all", [P, GROUPS, PK], u32)
        idxU = [sb(f"idxU{i}", [P, PK], u32) for i in range(2)]
        idxV = [sb(f"idxV{i}", [P, PK], u32) for i in range(2)]
        i16 = sb("i16", [P, 4, PK], u32)
        pos = sb("pos", [P, TB, PK], u32)
        ab = sb("ab", [P, TB, 2, PK], u32)

        yT = carver(UR * D, ARENA)(KC, S)
        nrm0 = yT.rearrange("p a b -> p (a b)").rearrange("p (t d) -> p t d", t=TB)
        wslot = [carver(a, ARENA)(HALF, BANK) for a in (UR * D + KC * S, OUT_AT, OUT_AT + HALF * BANK)]
        raw = carver(0, UR * D)(TB, RAW)
        carve = carver((UR + VR) * D, OUT_AT)
        mqkT = carve(2 * MH * MC, S + 2 * PAD)
        cv = carve(2, S)
        Em = carve(TB, 2, MH, P)
        hm = carve(TB, MH, MD)
        rtmp = hm.rearrange("p t m c -> p (t m c)")[:, 0:10 * AD].rearrange("p (a b) -> p a b", a=2)
        mlg = carve(MH * MD)
        gB_q, gB_k = carve(AD), carve(AD)
        cvw = carve(2 * MH * MC * CW)
        wg = carve(KC, 4 * MH)
        bgB = carve(4 * MH)
        gsb = carve(TB, 2, 2, MH)
        lf, bc, scol, Mx, mprev, G, eabs, elog = (carve(TB, 2, MH) for _ in range(8))
        smax, c1 = carve(2, MH), carve(2, MH)
        expi = carve(2 * 2 * TB * MH + 2 * MH)
        expo = carve(2 * 2 * TB * MH + 2 * MH)
        dd, dr = carve(2), carve(2)
        sq1, sq2 = carve(TB, AKV + AH), carve(TB, MH)
        sqt = carve(MD)
        mxs, nmx, psm, prc = carve(2), carve(2), carve(2), carve(2)
        at = carve()
        carve = carver(at, OUT_AT)
        qkr = carve((AKV + AH) * AD)
        aT = carve(AKV + AH, S)
        Pb = carve(2, S)
        PT = carve(2, 2, P)
        carve = carver(at, OUT_AT)
        kw = carve(TB, MH, MD)
        Csb = carve(2, MC, MD + 1)
        Isb = carve(2, MD + 1)
        num2 = carve(MD + 1)
        A = carve(2, 2, P)
        AT = carve(2, 2, P)

        names = """ld_x ld_c ld_small ld_gain ld_keys ld_wq0 ld_wq1 ld_pool ld_pm out_done
            w_got0 w_got1 w_got2 w_used
            sq_done ms_done root_done xn_ready tp_done xt_act xt_dve
            gates_mm gsum eabs_done elog_done ln_done lf_ready cum_done scol_ready srow_done
            expi_ready expo_done em_sub em_ready
            raw_done raw_evac mqk_done mqk_evac conv_done silu_done kscaled ktp_done kw_ready
            q_sq q_ms q_root rope_done atp_mm atp_ready sc_mm nmax p_exp p_ready pt_mm pt_ready pv_mm yt_ready
            s_mm a_ready at_mm at_ready c_mm c_ready i_mm i_ready n_mm comb_done
            y_sq y_ms y_root mo_sig hm_ready ymt_mm ymt_ready wo_done h_ready
            q_mm q_ready sc_done sc_free bd_ready ex_done idxu_ready idxv_ready
            dot_done gelu_done wk_ready diag_ready v_mm acc_evac
            pool_mm pool_ev py_mm h1_ready fin_ready
            dve dve_passed act_passed pool_passed""".split()
        s = {n: ctx.enter_context(nc.semaphore(n)) for n in names}
        w_got = [s["w_got0"], s["w_got1"], s["w_got2"]]
        ld_wq = [s["ld_wq0"], s["ld_wq1"]]
        u_got = [ctx.enter_context(nc.semaphore(f"u_got{i}")) for i in range(UR)]
        v_got = [ctx.enter_context(nc.semaphore(f"v_got{i}")) for i in range(VR)]

        def hold(eng, name, value, passed):
            eng.wait_ge(s[name], value)
            eng.sem_inc(s[passed], 1)

        class Steps:

            def __init__(self):
                self.base, self.n = 0, 0

            def link(self, eng, ins):
                self.n += 1
                ins.then_inc(s["dve"], 1)
                if isinstance(self.base, int):
                    eng.wait_ge(s["dve"], self.base + self.n)
                else:
                    hold(eng, "dve", self.base + self.n, "dve_passed")

        NORM_T = {0: 0, 1: 1, 3: 2}

        SC_BANK = (0, 3)
        AU, AT0 = 2 * AH, 10
        MU = 2 * MH

        def w_half(i):
            return i % WR, 16 * (i // WR + 1)

        block = ctx.enter_context(nc.Block())

        @block.sync
        def _(sp):
            def load_half(i, src):
                if i >= WR:
                    sp.wait_ge(s["w_used"], i - WR + 1)
                sp.dma_start(wslot[i % WR].rearrange("p k c -> p (k c)"), src).then_inc(w_got[i % WR], 16)

            def gain(o):
                if o:
                    sp.wait_ge(s["xn_ready"], TB * o)
                sp.dma_start(gB[:], gains[o].partition_broadcast(P)).then_inc(s["ld_gain"], 16)

            sp.dma_start(h[:, 0, :], x[0:P, :]).then_inc(s["ld_x"], 16)
            gain(0)
            sp.dma_start(cst[:], consts).then_inc(s["ld_c"], 16)
            sp.wait_ge(s["ld_x"], 16)
            sp.dma_start(h[:, 1, :], x[P:S, :]).then_inc(s["ld_x"], 16)
            for i in range(2):
                load_half(i, w_proj[i // 2, i % 2])
            sp.dma_start(wg, w_gates.rearrange("p (k c) -> p k c", k=KC)).then_inc(s["ld_small"], 16)
            sp.dma_start(bgB, b_gate.partition_broadcast(P)).then_inc(s["ld_small"], 16)
            sp.dma_start(cvw, conv_w).then_inc(s["ld_small"], 16)
            sp.dma_start(gB_q, q_gain.partition_broadcast(P)).then_inc(s["ld_small"], 16)
            sp.dma_start(gB_k, k_gain.partition_broadcast(P)).then_inc(s["ld_small"], 16)
            sp.dma_start(mlg, ml_gain.partition_broadcast(P)).then_inc(s["ld_small"], 16)
            for i in range(2, 2 * N_IN):
                load_half(i, w_proj[i // 2, i % 2])
                if i == 4:
                    gain(1)
            for m in range(2 * 2 * NO):
                load_half(2 * N_IN + m, w_out[m % (2 * NO)])
                if m == 2 * NO:
                    sp.wait_ge(s["ymt_ready"], 2 * TB)
                    sp.wait_ge(s["yt_ready"], AU)
                    sp.dma_start(keysT, keys[0].rearrange("p (a n) -> p a n", a=2 * PH)).then_inc(s["ld_keys"], 16)
                    for hd in range(2):
                        sp.dma_start(wqb[:, hd].rearrange("p k c -> p (k c)"), wq[0, hd]).then_inc(ld_wq[hd], 16)
            for L in range(LAYERS):
                gain(2 + 2 * L)
                for hd in range(2, PH):
                    sp.wait_ge(s["q_mm"], EVENTS * L + hd + 1)
                    sp.dma_start(wqb[:, hd % 2].rearrange("p k c -> p (k c)"), wq[L, hd]).then_inc(ld_wq[hd % 2], 16)
                if L == 0:
                    sp.wait_ge(s["q_mm"], EVENTS)
                    sp.dma_start(PM.rearrange("p g t s -> p (g t s)"), poolm).then_inc(s["ld_pm"], 16)
                    sp.dma_start(lsB, layer_scale.partition_broadcast(P)).then_inc(s["ld_pm"], 16)
                    sp.dma_start(wqb[:, 0].rearrange("p k c -> p (k c)"), wq[1, 0]).then_inc(ld_wq[0], 16)
                    sp.wait_ge(s["sc_done"], EVENTS)
                    sp.dma_start(keysT, keys[1].rearrange("p (a n) -> p a n", a=2 * PH)).then_inc(s["ld_keys"], 16)
                    sp.wait_ge(s["dot_done"], ROWS)
                    sp.dma_start(poolw, pool_w.rearrange("p (g k c) -> p g k c", g=4, k=4)).then_inc(s["ld_pool"], 16)
                    gain(3)
                    sp.wait_ge(s["h1_ready"], 4 * TB)
                    sp.dma_start(wqb[:, 1].rearrange("p k c -> p (k c)"), wq[1, 1]).then_inc(ld_wq[1], 16)
            for t in range(TB):
                sp.wait_ge(s["fin_ready"], t + 1)
                sp.dma_start(out[t * P:(t + 1) * P, :], h[:, t, :]).then_inc(s["out_done"], 16)
            sp.wait_ge(s["out_done"], 16 * TB)

        @block.gpsimd
        def _(pool):
            def gather(L, g, par, k, first, ring, R, table, idx, used, listed, got):
                if L or not first or k >= R:
                    hold(pool, used, L * ROWS + g * PK + k - R + 1, "pool_passed")
                if k == 0:
                    hold(pool, listed, L * GROUPS + g + 1, "pool_passed")
                nc.gpsimd.indirect_dma_start(
                    ring[:, k % R], None, table[L], bass.IndirectOffsetOnAxis(idx[par][:, k:k + 1], 0)
                ).then_inc(got[k % R], 16)

            def gather_u(L, g, par, k, first=False):
                gather(L, g, par, k, first, U, UR, pu, idxU, "dot_done", "idxu_ready", u_got)

            def gather_v(L, g, par, k, first=False):
                gather(L, g, par, k, first, V, VR, pv, idxV, "v_mm", "idxv_ready", v_got)

            def step(L, j, par, first=False):
                for k in range(PK):
                    gather_u(L, j + 1, 1 - par, k)
                    if first and L == 0 and k == 0:
                        pool.wait_ge(s["wo_done"], 1)
                    gather_v(L, j, par, k, first=first)

            for L in range(LAYERS):
                if L:
                    pool.wait_ge(s["py_mm"], 4 * TB)
                for k in range(PK):
                    gather_u(L, 0, 0, k, first=True)
                step(L, 0, 0, first=True)
                step(L, 1, 1)
                with pool.Fori(1, PH - 1) as jj:
                    step(L, 2 * jj, 0)
                    step(L, 2 * jj + 1, 1)
                step(L, GROUPS - 2, 0)
                for k in range(PK):
                    gather_v(L, GROUPS - 1, 1, k)

        @block.scalar
        def _(e):
            activation = nc.scalar.activation

            def norm(o, t):
                dst = nrm0[:, t] if o == 0 else xns[t]
                if o == 0:
                    e.wait_ge(s["ld_x"], 16 * (t + 1))
                elif o == 1:
                    e.wait_ge(s["h_ready"], NO * (t + 1))
                elif o == 3:
                    e.wait_ge(s["h1_ready"], 4 * (t + 1))
                    e.wait_ge(s["pool_mm"], KC)
                else:
                    e.wait_ge(s["acc_evac"], NO * (TB * (o // 2 - 1) + t + 1))
                    e.wait_ge(s["dot_done"], ROWS * (o // 2 - 1) + ROWS // 2 * (t + 1))
                activation(dst, h[:, t, :], ACT.Square, accum_out=ss[:, t:t + 1]).then_inc(s["sq_done"], 1)
                e.wait_ge(s["ms_done"], TB * o + t + 1)
                activation(rt[:, t:t + 1], ms[:, t:t + 1], ACT.Sqrt).then_inc(s["root_done"], 1)

            def evac_xt(o, t):
                for q in (0, 2):
                    e.wait_ge(s["tp_done"], 8 * o + 4 * t + q + 1)
                    activation(xnT[:, 4 * q:4 * q + 4, t * P:(t + 1) * P],
                               psum[4 + q][:, :].rearrange("p (a b) -> p a b", a=4), ACT.Copy
                               ).then_inc(s["xt_act"], 1)

            def evac_raw(r):
                for t in range(TB):
                    e.wait_ge(s["raw_done"], TB * r + t + 1)
                    activation(raw[:, t, r * BANK:(r + 1) * BANK], psum[4 + t][:, :], ACT.Copy
                               ).then_inc(s["raw_evac"], 1)

            for t in range(TB):
                norm(0, t)
            for t in range(TB):
                evac_xt(0, t)
            e.wait_ge(s["gsum"], 1)
            activation(eabs, gsb[:, :, :, 1], ACT.Abs).then_inc(s["eabs_done"], 1)
            e.wait_ge(s["eabs_done"], 1)
            activation(elog, eabs, ACT.Exp, scale=-1.0).then_inc(s["elog_done"], 1)
            e.wait_ge(s["elog_done"], 1)
            activation(eabs, elog, ACT.Ln, bias=1.0).then_inc(s["ln_done"], 1)
            evac_raw(0)
            evac_raw(1)
            e.wait_ge(s["expi_ready"], 1)
            activation(expo, expi, ACT.Exp).then_inc(s["expo_done"], 1)
            e.wait_ge(s["em_sub"], 1)
            em = Em.rearrange("p a b c d -> p (a b c d)")
            activation(em, em, ACT.Exp).then_inc(s["em_ready"], 1)
            evac_raw(2)
            e.wait_ge(s["raw_evac"], TB * N_QKV)
            for t in range(TB):
                for i in range(AKV + AH):
                    if t + i:
                        e.wait_ge(s["q_sq"], (AKV + AH) * t + i)
                    activation(sqt[:, 0:AD], raw[:, t, R_AK + i * AD:R_AK + (i + 1) * AD], ACT.Square,
                               accum_out=sq1[:, t, i:i + 1]).then_inc(s["q_sq"], 1)
            e.wait_ge(s["q_ms"], 1)
            activation(sq1, sq1, ACT.Sqrt).then_inc(s["q_root"], 1)

            def silu(c):
                e.wait_ge(s["conv_done"], c + 1)
                activation(mqkT[:, c, PAD:PAD + S], cv[:, c % 2], ACT.Silu).then_inc(s["silu_done"], 1)

            def attention(i):
                if i < AU:
                    e.wait_ge(s["nmax"], i + 1)
                    if i >= 2:
                        e.wait_ge(s["pt_mm"], i - 1)
                    activation(Pb[:, i % 2], psum[SC_BANK[i % 2]][:, 0:S], ACT.Exp,
                               bias=nmx[:, i % 2:i % 2 + 1], scale=AD ** -0.5,
                               accum_out=psm[:, i % 2:i % 2 + 1]).then_inc(s["p_exp"], 1)
                if 1 <= i <= AU:
                    u = i - 1
                    e.wait_ge(s["pt_mm"], u + 1)
                    if u >= 2:
                        e.wait_ge(s["pv_mm"], u - 1)
                    activation(PT[:, u % 2], psum[1][:, 0:S].rearrange("p (a b) -> p a b", a=2),
                               ACT.Copy).then_inc(s["pt_ready"], 1)
                if i >= 2:
                    u = i - 2
                    hd, t = u // 2, u % 2
                    e.wait_ge(s["pv_mm"], u + 1)
                    activation(yT[:, hd, t * P:(t + 1) * P], psum[2][:, 0:P], ACT.Copy
                               ).then_inc(s["yt_ready"], 1)

            for g in range(8 * N_MQK):
                n, hf, i = g // 8, g // 4 % 2, g % 4
                if g == AT0 - 1:
                    for m in range(3 * TB):
                        t, q = m // 3, m % 3
                        w = 4 if q < 2 else 2
                        e.wait_ge(s["atp_mm"], m + 1)
                        activation(aT[:, 4 * q:4 * q + w, t * P:(t + 1) * P],
                                   psum[2 + m % 2][:, 0:w * P].rearrange("p (a b) -> p a b", a=w), ACT.Copy
                                   ).then_inc(s["atp_ready"], 1)
                if hf == 1:
                    e.wait_ge(s["mqk_done"], 4 * n + i + 1)
                    activation(mqkT[:, 4 * n + i, PAD:PAD + S], psum[4 + i][:, 0:S], ACT.Copy).then_inc(s["mqk_evac"], 1)
                elif n and i % 2 == 1:
                    silu(4 * (n - 1) + i - 1)
                    silu(4 * (n - 1) + i)
                if 0 <= g - AT0 < AU + 2:
                    attention(g - AT0)
            for c in range(4 * (N_MQK - 1), 4 * N_MQK):
                silu(c)
            evac_raw(N_QKV)
            e.wait_ge(s["expo_done"], 1)
            for t in range(TB):
                for hp in range(2):
                    e.wait_ge(s["ktp_done"], 2 * t + hp + 1)
                    for i in range(2):
                        hd = 2 * hp + i
                        activation(kw[:, t, hd], psum[6 + hp][:, i * MD:(i + 1) * MD], ACT.Copy,
                                   scale=expo[:, 32 + 4 * t + hd:33 + 4 * t + hd]).then_inc(s["kw_ready"], 1)
            evac_raw(N_QKV + 1)

            def mlstm(i):
                if i < MU:
                    for c in range(MC):
                        e.wait_ge(s["c_mm"], MC * i + c + 1)
                        if i >= 2:
                            e.wait_ge(s["i_mm"], i - 1)
                        activation(Csb[:, i % 2, c], psum[2 + c][:, 0:MD + 1], ACT.Copy).then_inc(s["c_ready"], 1)
                if i:
                    u = i - 1
                    hd, t = u // 2, u % 2
                    e.wait_ge(s["at_mm"], u + 1)
                    if u >= 2:
                        e.wait_ge(s["n_mm"], 2 * (u - 1))
                    activation(AT[:, u % 2], psum[1][:, 0:2 * P].rearrange("p (a b) -> p a b", a=2),
                               ACT.Copy).then_inc(s["at_ready"], 1)
                    e.wait_ge(s["i_mm"], u + 1)
                    if u >= 2:
                        e.wait_ge(s["comb_done"], u - 1)
                    w = (t * 2 + (1 - t)) * MH + hd
                    activation(Isb[:, u % 2], psum[2][:, 0:MD + 1], ACT.Copy,
                               scale=expo[:, w:w + 1]).then_inc(s["i_ready"], 1)

            for g in range(4 * N_MV):
                if g % 4 == 3:
                    evac_raw(N_QKV + N_MV + g // 4)
                mlstm(g)
            mlstm(MU)
            e.wait_ge(s["raw_evac"], TB * RAW // BANK)
            activation(raw[:, :, R_MO:RAW], raw[:, :, R_MO:RAW], ACT.Sigmoid).then_inc(s["mo_sig"], 1)
            e.wait_ge(s["comb_done"], MU)
            for t in range(TB):
                for hd in range(MH):
                    e.wait_ge(*((s["y_sq"], MH * t + hd) if t + hd else (s["q_sq"], TB * (AKV + AH))))
                    activation(sqt, hm[:, t, hd], ACT.Square, accum_out=sq2[:, t, hd:hd + 1]).then_inc(s["y_sq"], 1)
            e.wait_ge(s["y_ms"], 1)
            activation(sq2, sq2, ACT.Sqrt).then_inc(s["y_root"], 1)
            for m in range(2 * TB):
                t, q = m // 2, m % 2
                e.wait_ge(s["ymt_mm"], m + 1)
                activation(yT[:, AH + 4 * q:AH + 4 + 4 * q, t * P:(t + 1) * P],
                           psum[6 + q][:, :].rearrange("p (a b) -> p a b", a=4), ACT.Copy
                           ).then_inc(s["ymt_ready"], 1)

            def route_q(L, ev_, t0, t1):
                n0 = EVENTS * L + ev_
                hold(e, "q_mm", n0 + 1, "act_passed")
                activation(qT[:, :, t0 * P:t1 * P],
                           psum[6][:, :].rearrange("p (a b) -> p a b", a=2)[:, :, t0 * P:t1 * P], ACT.Copy
                           ).then_inc(s["q_ready"], 1)

            def route_exp(L, ev_, t0, t1):
                hold(e, "bd_ready", EVENTS * L + ev_ + 1, "act_passed")
                activation(ex[:, t0:t1], bd[:, t0:t1], ACT.Exp).then_inc(s["ex_done"], 1)

            def gelu(L, j, par):
                hold(e, "dot_done", L * ROWS + j * PK + PK, "act_passed")
                activation(ga, act[:, par], ACT.Gelu).then_inc(s["gelu_done"], 1)

            def diagonal(L, j, par, k, first=False):
                if k == 0:
                    hold(e, "wk_ready", L * GROUPS + j + 1, "act_passed")
                if L or not first or k >= DR:
                    hold(e, "v_mm", L * ROWS + j * PK + k - DR + 1, "act_passed")
                activation(diag[:, k % DR], ident, ACT.Copy, scale=wk[:, par, k:k + 1]).then_inc(s["diag_ready"], 1)

            def first_step(L):
                gelu(L, 0, 0)
                norm(1 + 2 * L, 1)
                for k in range(PK):
                    diagonal(L, 0, 0, k, first=True)
                    if k == 2:
                        evac_xt(1 + L, 1)
                    if k == 4:
                        route_q(L, 2, 1, 2)
                    if k == 6:
                        route_exp(L, 2, 1, 2)
                        route_q(L, 3, 1, 2)
                    if k == 8:
                        route_exp(L, 3, 1, 2)
                    if k == 10:
                        route_q(L, 4, 0, 2)
                    if k == 13:
                        route_exp(L, 4, 0, 2)

            def step(L, j, par, route_head=None):
                gelu(L, j, par)
                for k in range(PK):
                    diagonal(L, j, par, k)
                    if route_head is not None and k == 5:
                        route_q(L, route_head + 2, 0, 2)
                    if route_head is not None and k == 10:
                        route_exp(L, route_head + 2, 0, 2)

            def evac_acc(L, b):
                e.wait_ge(s["v_mm"], L * ROWS + (b + 1) * PH * PK)
                for n in range(NO):
                    activation(h[:, b, n * BANK:(n + 1) * BANK], psum[n][:, :], ACT.Copy).then_inc(s["acc_evac"], 1)

            for L in range(LAYERS):
                if L:
                    norm(2, 1)
                    for c in range(KC):
                        e.wait_ge(s["pool_mm"], c + 1)
                        activation(xnT[:, c, :], psum[4 + c % 4][:, 0:S], ACT.Copy).then_inc(s["pool_ev"], 1)
                norm(1 + 2 * L, 0)
                evac_xt(1 + L, 0)
                for hd in range(2):
                    route_q(L, hd, 0, 1)
                    route_exp(L, hd, 0, 1)
                first_step(L)
                step(L, 1, 1, route_head=3)
                with e.Fori(1, 3) as jj:
                    step(L, 2 * jj, 0, route_head=2 * jj + 2)
                    step(L, 2 * jj + 1, 1, route_head=2 * jj + 3)
                step(L, PH - 2, 0)
                step(L, PH - 1, 1)
                evac_acc(L, 0)
                norm(2 + 2 * L, 0)
                with e.Fori(PH // 2, PH - 1) as jj:
                    step(L, 2 * jj, 0)
                    step(L, 2 * jj + 1, 1)
                step(L, GROUPS - 2, 0)
                step(L, GROUPS - 1, 1)
                evac_acc(L, 1)
            norm(4, 1)

        @block.vector
        def _(v):
            st = Steps()
            vec = nc.vector

            def link(ins):
                st.link(v, ins)

            def norm(o, t):
                one = slice(t, t + 1)
                v.wait_ge(s["sq_done"], TB * o + t + 1)
                vec.tensor_scalar(ms[:, one], ss[:, one], 1.0 / D, EPS, ALU.mult, ALU.add).then_inc(s["ms_done"], 1)
                v.wait_ge(s["root_done"], TB * o + t + 1)
                link(vec.reciprocal(rs[:, one], rt[:, one]))
                v.wait_ge(s["ld_gain"], 16 * (o + 1))
                dst = nrm0[:, t] if o == 0 else h[:, t, :] if o == 4 else xns[t]
                vec.scalar_tensor_tensor(dst, h[:, t, :], rs[:, one], gB[:], ALU.mult, ALU.mult
                                         ).then_inc(s["fin_ready" if o == 4 else "xn_ready"], 1)

            def evac_xt(o, t):
                for q in (1, 3):
                    v.wait_ge(s["tp_done"], 8 * o + 4 * t + q + 1)
                    vec.tensor_copy(xnT[:, 4 * q:4 * q + 4, t * P:(t + 1) * P],
                                    psum[4 + q][:, :].rearrange("p (a b) -> p a b", a=4)).then_inc(s["xt_dve"], 1)

            vec.memset(mqkT[:, :, 0:PAD], 0.0)
            link(vec.memset(mqkT[:, :, PAD + S:], 0.0))
            for t in range(TB):
                norm(0, t)
            for t in range(TB):
                evac_xt(0, t)
            v.wait_ge(s["ld_small"], 6 * 16)
            v.wait_ge(s["gates_mm"], 1)
            g_ps = psum[6][:, 0:TB * 4 * MH].rearrange("p (t c) -> p t c", t=TB)
            vec.tensor_tensor(gsb.rearrange("p t d x m -> p t (d x m)"), g_ps,
                              bgB.unsqueeze(1).to_broadcast([P, TB, 4 * MH]), ALU.add).then_inc(s["gsum"], 1)
            v.wait_ge(s["gsum"], 1)
            v.wait_ge(s["ln_done"], 1)
            for t in range(TB):
                for d in range(2):
                    last = vec.scalar_tensor_tensor(lf[:, t, d], gsb[:, t, d, 1], 0.0, eabs[:, t, d], ALU.min, ALU.subtract)
            last.then_inc(s["lf_ready"], 1)
            v.wait_ge(s["cum_done"], 1)
            w8 = TB * 2 * MH
            cum = psum[7][:, 0:w8].rearrange("p (t d m) -> p t d m", t=TB, d=2)
            tot = psum[7][:, w8:2 * w8].rearrange("p (t d m) -> p t d m", t=TB, d=2)
            vec.tensor_copy(bc, cum)
            vec.tensor_copy(G, tot)
            vec.memset(mprev, 0.0)
            for t in range(TB):
                ins = vec.tensor_tensor(scol[:, t], gsb[:, t, :, 0], cum[:, t], ALU.subtract)
            ins.then_inc(s["scol_ready"], 1)
            v.wait_ge(s["srow_done"], 4)
            for t in range(TB):
                for d in range(2):
                    row = psum[2 * t + d][:, :].rearrange("p (m r) -> p m r", m=MH)
                    ins = vec.tensor_tensor(Em[:, t, d], row, masks[:, d].unsqueeze(1).to_broadcast([P, MH, P]), ALU.add)
                    if t == d:
                        ins = vec.tensor_reduce(smax[:, d], row, X, ALU.max)
            link(ins)
            for t in range(TB):
                for d in range(2):
                    vec.tensor_reduce(Mx[:, t, d], Em[:, t, d], X, ALU.max)
            link(vec.tensor_scalar(c1, smax, 0.0, None, ALU.max))
            for d in range(2):
                ins = vec.tensor_tensor(mprev[:, 1 - d, d], G[:, d, d], c1[:, d], ALU.add)
            link(ins)
            link(vec.tensor_tensor(Mx, Mx, mprev, ALU.max))
            e16 = [expi[:, i * 16:(i + 1) * 16] for i in range(2)]
            vec.tensor_tensor(e16[0], mprev.rearrange("p t d m -> p (t d m)"), Mx.rearrange("p t d m -> p (t d m)"), ALU.subtract)
            vec.scalar_tensor_tensor(e16[1], bc.rearrange("p t d m -> p (t d m)"), -1.0,
                                     Mx.rearrange("p t d m -> p (t d m)"), ALU.mult, ALU.subtract)
            for d in range(2):
                ins = vec.tensor_tensor(expi[:, 32 + 4 * d:36 + 4 * d], scol[:, d, d], c1[:, d], ALU.subtract)
            ins.then_inc(s["expi_ready"], 1)
            em = Em.rearrange("p t d m r -> p (t d m) r")
            vec.tensor_tensor(em, em, Mx.rearrange("p t d m -> p (t d m)").unsqueeze(2).to_broadcast([P, 16, P]),
                              ALU.subtract).then_inc(s["em_sub"], 1)
            v.wait_ge(s["q_sq"], TB * (AKV + AH))
            vec.tensor_scalar(sq1, sq1, 1.0 / AD, EPS, ALU.mult, ALU.add).then_inc(s["q_ms"], 1)
            v.wait_ge(s["q_root"], 1)
            link(vec.reciprocal(sq1, sq1))
            for t in range(TB):
                for i in range(AKV + AH):
                    hv = raw[:, t, R_AK + i * AD:R_AK + (i + 1) * AD]
                    ins = vec.scalar_tensor_tensor(hv, hv, sq1[:, t, i:i + 1], gB_k if i < AKV else gB_q,
                                                   ALU.mult, ALU.mult)
            link(ins)

            def rotate(t):
                n = AKV + AH
                src = raw[:, t, R_AK:R_AK + n * AD].rearrange("p (n a x f) -> p n a x f", n=n, a=2, x=2)
                dst = qkr.rearrange("p (n a x f) -> p n a x f", n=n, a=2, x=2)
                t1, t2 = (rtmp[:, i].rearrange("p (n a f) -> p n a f", n=n, a=2) for i in range(2))
                if t:
                    v.wait_ge(s["atp_mm"], 3)
                cb, sn = ([m[:, t, a].unsqueeze(1).to_broadcast([P, n, 32]) for a in range(2)] for m in (rope_c, rope_s))
                for a in range(2):
                    vec.tensor_tensor(t1[:, :, a], src[:, :, a, 0], cb[a], ALU.mult)
                    ins = vec.tensor_tensor(t2[:, :, a], src[:, :, a, 1], sn[a], ALU.mult)
                link(ins)
                for a in range(2):
                    ins = vec.tensor_tensor(dst[:, :, a, 0], t1[:, :, a], t2[:, :, a], ALU.subtract)
                link(ins)
                for a in range(2):
                    vec.tensor_tensor(t1[:, :, a], src[:, :, a, 1], cb[a], ALU.mult)
                    ins = vec.tensor_tensor(t2[:, :, a], src[:, :, a, 0], sn[a], ALU.mult)
                link(ins)
                for a in range(2):
                    ins = vec.tensor_tensor(dst[:, :, a, 1], t1[:, :, a], t2[:, :, a], ALU.add)
                ins.then_inc(s["rope_done"], 1)
                v.wait_ge(s["rope_done"], t + 1)

            def convolve(c):
                v.wait_ge(s["mqk_evac"], c + 2)
                if c:
                    v.wait_ge(s["silu_done"], c)
                for j in range(CW):
                    for i in range(2):
                        src = mqkT[:, c + i, j:j + S]
                        wc = cvw[:, (c + i) * CW + j:(c + i) * CW + j + 1]
                        if j == 0:
                            ins = vec.tensor_scalar(cv[:, i], src, wc, None, ALU.mult)
                        else:
                            ins = vec.scalar_tensor_tensor(cv[:, i], src, wc, cv[:, i], ALU.mult, ALU.add)
                        if j == CW - 1:
                            ins.then_inc(s["conv_done"], 1)
                    if j < CW - 1:
                        link(ins)

            def attention(i):
                if i < AU:
                    v.wait_ge(s["sc_mm"], i + 1)
                    if i >= 2:
                        v.wait_ge(s["p_exp"], i - 1)
                    link(vec.tensor_reduce(mxs[:, i % 2:i % 2 + 1], psum[SC_BANK[i % 2]][:, 0:S], X, ALU.max))
                    vec.tensor_scalar(nmx[:, i % 2:i % 2 + 1], mxs[:, i % 2:i % 2 + 1], -(AD ** -0.5), None, ALU.mult
                                      ).then_inc(s["nmax"], 1)
                if 1 <= i <= AU:
                    u = i - 1
                    v.wait_ge(s["p_exp"], u + 1)
                    link(vec.reciprocal(prc[:, u % 2:u % 2 + 1], psm[:, u % 2:u % 2 + 1]))
                    vec.tensor_scalar(Pb[:, u % 2], Pb[:, u % 2], prc[:, u % 2:u % 2 + 1], None, ALU.mult
                                      ).then_inc(s["p_ready"], 1)

            for t in range(TB):
                rotate(t)
            for g in range(8 * N_MQK):
                n, hf, i = g // 8, g // 4 % 2, g % 4
                if hf == 0 and n and i % 2 == 1:
                    convolve(4 * (n - 1) + i - 1)
                if 0 <= g - AT0 < AU + 2:
                    attention(g - AT0)
            for c in range(4 * (N_MQK - 1), 4 * N_MQK, 2):
                convolve(c)
            v.wait_ge(s["silu_done"], 4 * N_MQK)
            kk = mqkT[:, MH * MC:2 * MH * MC, PAD:PAD + S]
            vec.tensor_scalar(kk, kk, MD ** -0.5, None, ALU.mult).then_inc(s["kscaled"], 1)
            v.wait_ge(s["em_ready"], 1)
            for i in range(MU + 1):
                if i < MU:
                    hd, t = i // 2, i % 2
                    v.wait_ge(s["s_mm"], i + 1)
                    if i >= 2:
                        v.wait_ge(s["at_mm"], i - 1)
                    vec.tensor_tensor(A[:, i % 2], psum[0][:, 0:P].unsqueeze(1).to_broadcast([P, 2, P]),
                                      Em[:, t, :, hd], ALU.mult).then_inc(s["a_ready"], 1)
                if i:
                    u = i - 1
                    hd, t = u // 2, u % 2
                    first, second = 6 + t, 6 + (1 - t)
                    v.wait_ge(s["i_ready"], u + 1)
                    v.wait_ge(s["n_mm"], 2 * (u + 1))
                    link(vec.tensor_tensor(num2, Isb[:, u % 2], psum[second][:, 0:MD + 1], ALU.add))
                    dens = ((psum[first][:, MD:MD + 1], t), (num2[:, MD:MD + 1], 1 - t))
                    for c, (den, d) in enumerate(dens):
                        w = 16 + (t * 2 + d) * MH + hd
                        ins = vec.scalar_tensor_tensor(dd[:, c:c + 1], den, -1.0, expo[:, w:w + 1], ALU.mult, ALU.max)
                    link(ins)
                    for c, (den, d) in enumerate(dens):
                        ins = vec.tensor_tensor(dd[:, c:c + 1], den, dd[:, c:c + 1], ALU.max)
                    link(ins)
                    link(vec.reciprocal(dr, dd))
                    link(vec.tensor_scalar(hm[:, t, hd], psum[first][:, 0:MD], dr[:, 0:1], None, ALU.mult))
                    vec.scalar_tensor_tensor(hm[:, t, hd], num2[:, 0:MD], dr[:, 1:2], hm[:, t, hd], ALU.mult, ALU.add
                                             ).then_inc(s["comb_done"], 1)
                    v.wait_ge(s["comb_done"], u + 1)
            v.wait_ge(s["y_sq"], TB * MH)
            vec.tensor_scalar(sq2, sq2, 1.0 / MD, EPS, ALU.mult, ALU.add).then_inc(s["y_ms"], 1)
            v.wait_ge(s["y_root"], 1)
            link(vec.reciprocal(sq2, sq2))
            for t in range(TB):
                for hd in range(MH):
                    ins = vec.scalar_tensor_tensor(hm[:, t, hd], hm[:, t, hd], sq2[:, t, hd:hd + 1],
                                                   mlg[:, hd * MD:(hd + 1) * MD], ALU.mult, ALU.mult)
            link(ins)
            v.wait_ge(s["mo_sig"], 1)
            for t in range(TB):
                hf_ = hm[:, t].rearrange("p m c -> p (m c)")
                vec.tensor_tensor(hf_, hf_, raw[:, t, R_MO:RAW], ALU.mult).then_inc(s["hm_ready"], 1)

            def add_mixer(t):
                for n in range(NO):
                    v.wait_ge(s["wo_done"] if t * NO + n == 2 * NO - 1 else s["raw_done"],
                              1 if t * NO + n == 2 * NO - 1 else TB * RAW // BANK + NO * t + n + 1)
                    hv = h[:, t, n * BANK:(n + 1) * BANK]
                    vec.tensor_tensor(hv, psum[n][:, :], hv, ALU.add).then_inc(s["h_ready"], 1)

            def route(L, hd, ev_, t0, t1):
                n0 = EVENTS * L + ev_
                nt = t1 - t0
                ts, qs = range(t0, t1), range(2 * t0, 2 * t1)
                tsl, qsl = slice(t0, t1), slice(2 * t0, 2 * t1)
                hold(v, "sc_done", n0 + 1, "dve_passed")
                sc = psum[7][:, :].rearrange("p (q n) -> p q n", q=4)
                for q in qs:
                    ins = vec.max(s16[:, q, 0:8], sc[:, q])
                link(ins)
                for q in qs:
                    vec.match_replace(stmp[:, q], s16[:, q, 0:8], sc[:, q], NEG)
                for q in qs:
                    ins = vec.max_index(i16[:, q, 0:8], s16[:, q, 0:8], sc[:, q])
                ins.then_inc(s["sc_free"], 1)
                hold(v, "sc_free", n0 + 1, "dve_passed")
                for q in qs:
                    ins = vec.max(s16[:, q, 8:16], stmp[:, q])
                link(ins)
                for q in qs:
                    vec.max_index(i16[:, q, 8:16], s16[:, q, 8:16], stmp[:, q])
                for t in ts:
                    ins = vec.tensor_tensor(cand[:, t], s16[:, 2 * t].unsqueeze(2).to_broadcast([P, PK, PK]),
                                            s16[:, 2 * t + 1].unsqueeze(1).to_broadcast([P, PK, PK]), ALU.add)
                link(ins)
                vec.tensor_copy(i16f[:, qsl], i16[:, qsl])
                cf = cand.rearrange("p t a b -> p t (a b)")
                c2 = cand2.rearrange("p t a b -> p t (a b)")
                for t in ts:
                    ins = vec.max(b16[:, t, 0:8], cf[:, t])
                link(ins)
                for t in ts:
                    vec.match_replace(c2[:, t], b16[:, t, 0:8], cf[:, t], NEG)
                for t in ts:
                    ins = vec.max_index(pos[:, t, 0:8], b16[:, t, 0:8], cf[:, t])
                link(ins)
                for t in ts:
                    ins = vec.max(b16[:, t, 8:16], c2[:, t])
                link(ins)
                for t in ts:
                    vec.max_index(pos[:, t, 8:16], b16[:, t, 8:16], c2[:, t])
                vec.tensor_tensor(bd[:, tsl], b16[:, tsl], b16[:, tsl, 0:1].to_broadcast([P, nt, PK]), ALU.subtract
                                  ).then_inc(s["bd_ready"], 1)
                hold(v, "bd_ready", n0 + 1, "dve_passed")
                vec.tensor_scalar(ab[:, tsl, 0], pos[:, tsl], 4, None, ALU.logical_shift_right)
                link(vec.tensor_scalar(ab[:, tsl, 1], pos[:, tsl], PK - 1, None, ALU.bitwise_and))
                link(vec.tensor_copy(abf[:, qsl], ab[:, tsl].rearrange("p t x k -> p (t x) k")))
                e64 = eq[:, qsl].rearrange("p q k a -> p (q k) a")
                link(vec.tensor_tensor(e64, abf[:, qsl].rearrange("p q k -> p (q k)").unsqueeze(2).to_broadcast([P, 32 * nt, PK]),
                                       iota16.unsqueeze(1).to_broadcast([P, 32 * nt, PK]), ALU.is_equal))
                link(vec.tensor_tensor(eq[:, qsl], eq[:, qsl], i16f[:, qsl].unsqueeze(2).to_broadcast([P, 2 * nt, PK, PK]), ALU.mult))
                link(vec.tensor_reduce(ev[:, tsl].rearrange("p t x k -> p (t x k)"), e64, X, ALU.add))
                link(vec.scalar_tensor_tensor(idx_all[:, :, :].rearrange("p (t g) k -> p t g k", t=TB)[:, tsl, bass.ds(hd, 1)]
                                              .rearrange("p t g k -> p t (g k)"),
                                              ev[:, tsl, 0], float(NK), ev[:, tsl, 1], ALU.mult, ALU.add))
                hold(v, "ex_done", n0 + 1, "dve_passed")
                link(vec.tensor_reduce(exs[:, tsl], ex[:, tsl], X, ALU.add))
                link(vec.reciprocal(exr[:, tsl], exs[:, tsl]))
                link(vec.tensor_tensor(gates.rearrange("p (t g) k -> p t g k", t=TB)[:, tsl, bass.ds(hd, 1)]
                                       .rearrange("p t g k -> p t (g k)"),
                                       ex[:, tsl], exr[:, tsl].unsqueeze(2).to_broadcast([P, nt, PK]), ALU.mult))

            def copy_idx(g, buf, name):
                vec.tensor_copy(buf[:], idx_all[:, bass.ds(g, 1)].rearrange("p g k -> p (g k)")).then_inc(s[name], 1)

            def dot(L, g, par, k, xn):
                v.wait_ge(u_got[k % UR], 16 * (L * ROWS // UR + g * (PK // UR) + k // UR + 1))
                u = U[:, k % UR]
                vec.tensor_tensor_reduce(out=u, in0=u, in1=xn, scale=1.0, scalar=0.0, op0=ALU.mult, op1=ALU.add,
                                         accum_out=act[:, par, k:k + 1]).then_inc(s["dot_done"], 1)

            def weigh(L, g, par):
                hold(v, "gelu_done", L * GROUPS + g + 1, "dve_passed")
                vec.tensor_tensor(wk[:, par], ga, gates[:, bass.ds(g, 1)].rearrange("p g k -> p (g k)"), ALU.mult
                                  ).then_inc(s["wk_ready"], 1)

            def next_v(L, j, par):
                hold(v, "v_mm", L * ROWS + j * PK, "dve_passed")
                copy_idx(j + 1, idxV[1 - par], "idxv_ready")

            def next_u(L, j, par):
                hold(v, "dot_done", L * ROWS + j * PK + PK, "dve_passed")
                copy_idx(j + 2, idxU[par], "idxu_ready")

            def first_step(L):
                norm(1 + 2 * L, 1)
                for k in range(PK):
                    dot(L, 1, 1, k, xn0)
                    if k == 0:
                        weigh(L, 0, 0)
                        evac_xt(1 + L, 1)
                        copy_idx(1, idxV[1], "idxv_ready")
                    if k == 3:
                        route(L, 0, 2, 1, 2)
                    if k == 6:
                        route(L, 1, 3, 1, 2)
                    if k == 10:
                        route(L, 2, 4, 0, 2)
                    if k == 11:
                        next_u(L, 0, 0)

            def step(L, j, par, xn, route_head=None, last=False):
                for k in range(PK):
                    dot(L, j + 1, 1 - par, k, xn)
                    if k == 0:
                        weigh(L, j, par)
                    if k == 4:
                        next_v(L, j, par)
                    if k == 6 and route_head is not None:
                        route(L, route_head, route_head + 2, 0, 2)
                    if k == 7 and not last:
                        next_u(L, j, par)

            add_mixer(0)
            for L in range(LAYERS):
                if L:
                    norm(2, 1)
                    v.wait_ge(s["ld_pm"], 32)
                    for n in range(4 * TB):
                        t, g = n // 4, n % 4
                        v.wait_ge(s["py_mm"], n + 1)
                        cols = slice(g * BANK, (g + 1) * BANK)
                        link(vec.tensor_tensor(ytmp[:, n % 2], psum[g][:, :], lsB[:, cols], ALU.mult))
                        vec.tensor_tensor(h[:, t, cols], h[:, t, cols], ytmp[:, n % 2], ALU.add).then_inc(s["h1_ready"], 1)
                        if n == 4:
                            norm(3, 0)
                    v.wait_ge(s["h1_ready"], 4 * TB)
                else:
                    norm(1, 0)
                evac_xt(1 + L, 0)
                route(L, 0, 0, 0, 1)
                copy_idx(0, idxU[0], "idxu_ready")
                copy_idx(0, idxV[0], "idxv_ready")
                for k in range(PK):
                    dot(L, 0, 0, k, xn0)
                    if k == 2:
                        route(L, 1, 1, 0, 1)
                        copy_idx(1, idxU[1], "idxu_ready")
                    if k == 12 and L == 0:
                        add_mixer(1)
                first_step(L)
                step(L, 1, 1, xn0, route_head=3)
                n0 = st.n
                with v.Fori(1, 3) as jj:
                    st.base, st.n = n0 + (jj - 1) * (2 * ROUTE), 0
                    step(L, 2 * jj, 0, xn0, route_head=2 * jj + 2)
                    step(L, 2 * jj + 1, 1, xn0, route_head=2 * jj + 3)
                    assert st.n == 2 * ROUTE, st.n
                st.base, st.n = 0, n0 + 2 * 2 * ROUTE
                step(L, PH - 2, 0, xn0)
                step(L, PH - 1, 1, xn1)
                norm(2 + 2 * L, 0)
                with v.Fori(PH // 2, PH - 1) as jj:
                    step(L, 2 * jj, 0, xn1)
                    step(L, 2 * jj + 1, 1, xn1)
                step(L, GROUPS - 2, 0, xn1, last=True)
                weigh(L, GROUPS - 1, 1)
            norm(4, 1)

        @block.tensor
        def _(pe):
            mm = nc.tensor.matmul
            tr = nc.tensor.transpose

            def transpose_xn(o, norm_o, t, src):
                pe.wait_ge(s["xn_ready"], TB * norm_o + t + 1)
                for q in range(4):
                    if 4 * o + 2 * t:
                        pe.wait_ge(s["xt_act" if q % 2 == 0 else "xt_dve"], 4 * o + 2 * t)
                    for i in range(4):
                        k = 4 * q + i
                        ins = tr(psum[4 + q][:, i * P:(i + 1) * P], src[:, k * P:(k + 1) * P], ident)
                    ins.then_inc(s["tp_done"], 1)

            def straight_half(i, r, hf, after=None):
                slot, got = w_half(i)
                pe.wait_ge(w_got[slot], got)
                for t in range(TB):
                    if hf == 0 and r:
                        pe.wait_ge(s["raw_evac"], TB * (r - 1) + t + 1)
                    for k in range(HALF):
                        ins = mm(psum[4 + t][:, :], xnT[:, HALF * hf + k, t * P:(t + 1) * P], wslot[slot][:, k],
                                 start=hf == 0 and k == 0, stop=hf == 1 and k == HALF - 1)
                    if hf == 1:
                        ins.then_inc(s["raw_done"], 1)
                    elif t == 1:
                        ins.then_inc(s["w_used"], 1)
                    if hf == 1 and t == 1:
                        pe.wait_ge(s["raw_done"], TB * (r + 1))
                        pe.sem_inc(s["w_used"], 1)
                    if after is not None:
                        after(t)

            pe.wait_ge(s["ld_c"], 16)
            for t in range(TB):
                transpose_xn(0, 0, t, nrm0[:, t])
            pe.wait_ge(s["xt_act"], 4)
            pe.wait_ge(s["xt_dve"], 4)
            pe.wait_ge(s["ld_small"], 6 * 16)
            for t in range(TB):
                for k in range(KC):
                    ins = mm(psum[6][:, 4 * MH * t:4 * MH * (t + 1)], xnT[:, k, t * P:(t + 1) * P], wg[:, k],
                             start=k == 0, stop=k == KC - 1)
            ins.then_inc(s["gates_mm"], 1)
            straight_half(0, 0, 0)
            straight_half(1, 0, 1)
            pe.wait_ge(s["lf_ready"], 1)
            for t in range(TB):
                for d, tri in enumerate((tri_f, tri_b)):
                    c = (2 * t + d) * MH
                    mm(psum[7][:, c:c + MH], tri, lf[:, t, d], start=True, stop=True)
                    ins = mm(psum[7][:, 16 + c:16 + c + MH], ones, lf[:, t, d], start=True, stop=True)
            ins.then_inc(s["cum_done"], 1)
            straight_half(2, 1, 0)
            pe.wait_ge(s["scol_ready"], 1)
            for t in range(TB):
                for d in range(2):
                    for m in range(MH):
                        ins = mm(psum[2 * t + d][:, m * P:(m + 1) * P], scol[:, t, d, m:m + 1].to_broadcast([P, P]), ident,
                                 start=True, stop=True)
                    ins.then_inc(s["srow_done"], 1)
            straight_half(3, 1, 1)
            straight_half(4, 2, 0)
            straight_half(5, 2, 1)

            def attention(i):
                if i < AU:
                    hd, t = i // 2, i % 2
                    if i >= 2:
                        pe.wait_ge(s["p_exp"], i - 1)
                    mm(psum[SC_BANK[i % 2]][:, 0:S], aT[:, AKV + hd, t * P:(t + 1) * P], aT[:, hd // (AH // AKV)],
                       start=True, stop=True).then_inc(s["sc_mm"], 1)
                if 1 <= i <= AU:
                    u = i - 1
                    pe.wait_ge(s["p_ready"], u + 1)
                    if u:
                        pe.wait_ge(s["pt_ready"], u)
                    for c in range(2):
                        ins = tr(psum[1][:, c * P:(c + 1) * P], Pb[:, u % 2, c * P:(c + 1) * P], ident)
                    ins.then_inc(s["pt_mm"], 1)
                if i >= 2:
                    u = i - 2
                    kv = u // 2 // (AH // AKV)
                    pe.wait_ge(s["pt_ready"], u + 1)
                    if u:
                        pe.wait_ge(s["yt_ready"], u)
                    for c in range(2):
                        ins = mm(psum[2][:, 0:P], raw[:, c, R_AV + kv * AD:R_AV + (kv + 1) * AD],
                                 PT[:, u % 2, c], start=c == 0, stop=c == 1)
                    ins.then_inc(s["pv_mm"], 1)

            for g in range(8 * N_MQK):
                n, hf, i = g // 8, g // 4 % 2, g % 4
                slot, got = w_half(2 * N_QKV + 2 * n + hf)
                if i == 0:
                    pe.wait_ge(w_got[slot], got)
                if hf == 0:
                    if n == 0:
                        pe.wait_ge(s["raw_evac"], TB * N_QKV)
                        pe.wait_ge(s["scol_ready"], 1)
                    else:
                        pe.wait_ge(s["mqk_evac"], 4 * (n - 1) + i + 1)
                for k in range(HALF):
                    ins = mm(psum[4 + i][:, 0:S], wslot[slot][:, k, i * P:(i + 1) * P], xnT[:, HALF * hf + k, :],
                             start=hf == 0 and k == 0, stop=hf == 1 and k == HALF - 1)
                if hf == 1:
                    ins.then_inc(s["mqk_done"], 1)
                elif i == 3:
                    ins.then_inc(s["w_used"], 1)
                if hf == 1 and i == 3:
                    pe.wait_ge(s["mqk_done"], 4 * n + 4)
                    pe.sem_inc(s["w_used"], 1)
                if g == AT0 - 1:
                    for m in range(3 * TB):
                        t, q = m // 3, m % 3
                        pe.wait_ge(s["rope_done"], t + 1)
                        if m >= 2:
                            pe.wait_ge(s["atp_ready"], m - 1)
                        for c in range(4 * q, min(4 * q + 4, AKV + AH)):
                            ins = tr(psum[2 + m % 2][:, c % 4 * P:(c % 4 + 1) * P], qkr[:, c * P:(c + 1) * P], ident)
                        ins.then_inc(s["atp_mm"], 1)
                    pe.wait_ge(s["atp_ready"], 3 * TB)
                if 0 <= g - AT0 < AU + 2:
                    attention(g - AT0)
            w0 = 2 * (N_QKV + N_MQK)
            pe.wait_ge(s["mqk_evac"], 4 * N_MQK)
            straight_half(w0, N_QKV, 0)
            straight_half(w0 + 1, N_QKV, 1)
            pe.wait_ge(s["kscaled"], 1)
            for t in range(TB):
                for hp in range(2):
                    if t:
                        pe.wait_ge(s["kw_ready"], 2 * hp + 2)
                    for i in range(4):
                        c = MH * MC + 4 * hp + i
                        ins = tr(psum[6 + hp][:, i * P:(i + 1) * P], mqkT[:, c, PAD + t * P:PAD + (t + 1) * P], ident)
                    ins.then_inc(s["ktp_done"], 1)
                if t == 0:
                    straight_half(w0 + 2, N_QKV + 1, 0)
            straight_half(w0 + 3, N_QKV + 1, 1)

            def mlstm(i):
                if i < MU:
                    hd, t = i // 2, i % 2
                    if i:
                        pe.wait_ge(s["a_ready"], i)
                    for c in range(MC):
                        ins = mm(psum[0][:, 0:P], mqkT[:, MC * hd + c, PAD + t * P:PAD + (t + 1) * P],
                                 mqkT[:, MC * (MH + hd) + c, PAD + t * P:PAD + (t + 1) * P], start=c == 0, stop=c == MC - 1)
                    ins.then_inc(s["s_mm"], 1)
                    d = 1 - t
                    if i >= 2:
                        pe.wait_ge(s["i_ready"], i - 1)
                    for c in range(MC):
                        if i:
                            pe.wait_ge(s["c_ready"], MC * (i - 1) + c + 1)
                        kwc = kw[:, d, hd, c * P:(c + 1) * P]
                        mm(psum[2 + c][:, 0:MD], kwc, raw[:, d, R_MV + hd * MD:R_MV + (hd + 1) * MD], start=True, stop=True)
                        mm(psum[2 + c][:, MD:MD + 1], kwc, ones[:, 0:1], start=True, stop=True).then_inc(s["c_mm"], 1)
                if i:
                    u = i - 1
                    hd, t = u // 2, u % 2
                    pe.wait_ge(s["a_ready"], u + 1)
                    if u:
                        pe.wait_ge(s["at_ready"], u)
                    for d in range(2):
                        ins = tr(psum[1][:, d * P:(d + 1) * P], A[:, u % 2, d], ident)
                    ins.then_inc(s["at_mm"], 1)
                    pe.wait_ge(s["c_ready"], MC * (u + 1))
                    if i < MU:
                        pe.wait_ge(s["c_ready"], MC * i + 1)
                    else:
                        pe.wait_ge(s["i_ready"], u)
                    for c in range(MC):
                        ins = mm(psum[2][:, 0:MD + 1], mqkT[:, MC * hd + c, PAD + t * P:PAD + (t + 1) * P],
                                 Csb[:, u % 2, c], start=c == 0, stop=c == MC - 1)
                    ins.then_inc(s["i_mm"], 1)
                    pe.wait_ge(s["at_ready"], u + 1)
                    if u:
                        pe.wait_ge(s["comb_done"], u)
                    for d in range(2):
                        mm(psum[6 + d][:, 0:MD], AT[:, u % 2, d], raw[:, t, R_MV + hd * MD:R_MV + (hd + 1) * MD],
                           start=True, stop=True)
                        mm(psum[6 + d][:, MD:MD + 1], AT[:, u % 2, d], ones[:, 0:1], start=True, stop=True
                           ).then_inc(s["n_mm"], 1)

            pe.wait_ge(s["kw_ready"], 2 * MH)
            pe.wait_ge(s["raw_evac"], TB * (N_QKV + N_MV))
            pe.wait_ge(s["em_sub"], 1)
            for g in range(2 * N_MV):
                straight_half(w0 + 2 * N_MV + g, N_QKV + N_MV + g // 2, g % 2, after=lambda t: mlstm(2 * g + t))
            mlstm(MU)

            def project_out(m):
                t, hf, n = m // (2 * NO), m // NO % 2, m % NO
                slot, got = w_half(2 * N_IN + m)
                pe.wait_ge(w_got[slot], got)
                if t and hf == 0:
                    pe.wait_ge(s["h_ready"], n + 1)
                for k in range(HALF):
                    ins = mm(psum[n][:, :], yT[:, HALF * hf + k, t * P:(t + 1) * P], wslot[slot][:, k],
                             start=hf == 0 and k == 0, stop=hf == 1 and k == HALF - 1)
                if m == 4 * NO - 1:
                    ins.then_inc(s["wo_done"], 1)
                elif hf == 1:
                    ins.then_inc(s["raw_done"], 1)
                    pe.wait_ge(s["raw_done"], TB * RAW // BANK + NO * t + n + 1)
                    pe.sem_inc(s["w_used"], 1)
                else:
                    ins.then_inc(s["w_used"], 1)

            pe.wait_ge(s["comb_done"], MU)
            pe.wait_ge(s["yt_ready"], AU)
            for m in range(NO):
                project_out(m)
            for m in range(2 * TB):
                t, q = m // 2, m % 2
                pe.wait_ge(s["hm_ready"], t + 1)
                if t:
                    pe.wait_ge(s["ymt_ready"], q + 1)
                for i in range(4):
                    c = 4 * q + i
                    ins = tr(psum[6 + q][:, i * P:(i + 1) * P], hm[:, t].rearrange("p m c -> p (m c)")[:, c * P:(c + 1) * P], ident)
                ins.then_inc(s["ymt_mm"], 1)
            pe.wait_ge(s["ymt_ready"], 2 * TB)
            for m in range(NO, 2 * NO):
                project_out(m)

            def queries(L, hd, par, ev_, t0, t1):
                n0 = EVENTS * L + ev_
                pe.wait_ge(ld_wq[par], 16 * (L * (PH // 2) + (hd - par) // 2 + 1) if isinstance(hd, int) else
                           16 * (L * (PH // 2) + 1) + 8 * (hd - par))
                if n0 if isinstance(n0, int) else True:
                    pe.wait_ge(s["q_ready"], n0)
                for p_ in range(2):
                    for k in range(KC):
                        ins = mm(psum[6][:, p_ * S + t0 * P:p_ * S + t1 * P], wqb[:, par, k, p_ * P:(p_ + 1) * P],
                                 xnT[:, k, t0 * P:t1 * P], start=k == 0, stop=k == KC - 1)
                ins.then_inc(s["q_mm"], 1)

            def scores(L, hd, ev_, t0, t1):
                n0 = EVENTS * L + ev_
                pe.wait_ge(s["q_ready"], n0 + 1)
                if n0 if isinstance(n0, int) else True:
                    pe.wait_ge(s["sc_free"], n0)
                for t in range(t0, t1):
                    for p_ in range(2):
                        ins = mm(psum[7][:, (2 * t + p_) * P:(2 * t + p_ + 1) * P], qT[:, p_, t * P:(t + 1) * P],
                                 keysT[:, bass.ds(2 * hd + p_, 1)].rearrange("p a n -> p (a n)"), start=True, stop=True)
                ins.then_inc(s["sc_done"], 1)

            def add_v(L, j, k, last=False):
                pe.wait_ge(v_got[k % VR], 16 * (L * ROWS // VR + j * (PK // VR) + k // VR + 1))
                pe.wait_ge(s["diag_ready"], L * ROWS + j * PK + k + 1)
                for n in range(NO):
                    ins = mm(psum[n][:, :], diag[:, k % DR], V[:, k % VR, n * BANK:(n + 1) * BANK],
                             start=False, stop=last and k == PK - 1)
                ins.then_inc(s["v_mm"], 1)

            def first_step(L):
                for k in range(PK):
                    add_v(L, 0, k)
                    if k == 0:
                        transpose_xn(1 + L, 1 + 2 * L, 1, xn1)
                        pe.wait_ge(s["xt_act"], 4 * (2 + L))
                        pe.wait_ge(s["xt_dve"], 4 * (2 + L))
                    if k == 1:
                        queries(L, 0, 0, 2, 1, 2)
                    if k == 3:
                        scores(L, 0, 2, 1, 2)
                        queries(L, 1, 1, 3, 1, 2)
                    if k == 5:
                        scores(L, 1, 3, 1, 2)
                    if k == 8:
                        queries(L, 2, 0, 4, 0, 2)
                    if k == 10:
                        scores(L, 2, 4, 0, 2)

            def step(L, j, par, route_head=None, last=False):
                for k in range(PK):
                    add_v(L, j, k, last)
                    if route_head is not None and k == 3:
                        queries(L, route_head, par, route_head + 2, 0, 2)
                    if route_head is not None and k == 5:
                        scores(L, route_head, route_head + 2, 0, 2)

            def seed(L, b):
                for n in range(NO):
                    mm(psum[n][:, :], ident, h[:, b, n * BANK:(n + 1) * BANK], start=True, stop=False)

            for L in range(LAYERS):
                if L:
                    pe.wait_ge(s["xn_ready"], 6)
                    pe.wait_ge(s["ld_pm"], 32)
                    for c in range(KC):
                        if c >= 4:
                            pe.wait_ge(s["pool_ev"], c - 3)
                        for t in range(TB):
                            ins = mm(psum[4 + c % 4][:, 0:S], xns[t][:, c * P:(c + 1) * P], PM[:, c // 4, t], start=t == 0, stop=t == 1)
                        ins.then_inc(s["pool_mm"], 1)
                    pe.wait_ge(s["ld_pool"], 16)
                    pe.wait_ge(s["pool_ev"], KC)
                    pe.wait_ge(s["acc_evac"], TB * NO)
                    for n in range(4 * TB):
                        t, g = n // 4, n % 4
                        if t:
                            pe.wait_ge(s["h1_ready"], g + 1)
                        for c in range(4):
                            ins = mm(psum[g][:, :], xnT[:, 4 * g + c, t * P:(t + 1) * P], poolw[:, g, c],
                                     start=c == 0, stop=c == 3)
                        ins.then_inc(s["py_mm"], 1)
                else:
                    for m in range(2 * NO, 3 * NO):
                        project_out(m)
                transpose_xn(1 + L, 1 + 2 * L, 0, xn0)
                pe.wait_ge(s["ld_keys"], 16 * (L + 1))
                if L == 0:
                    project_out(3 * NO)
                pe.wait_ge(s["xt_act"], 4 * (1 + L) + 2)
                pe.wait_ge(s["xt_dve"], 4 * (1 + L) + 2)
                queries(L, 0, 0, 0, 0, 1)
                if L == 0:
                    project_out(3 * NO + 1)
                scores(L, 0, 0, 0, 1)
                queries(L, 1, 1, 1, 0, 1)
                if L == 0:
                    project_out(3 * NO + 2)
                scores(L, 1, 1, 0, 1)
                if L == 0:
                    project_out(3 * NO + 3)
                    pe.wait_ge(s["h_ready"], TB * NO)
                seed(L, 0)
                first_step(L)
                step(L, 1, 1, route_head=3)
                with pe.Fori(1, 3) as jj:
                    step(L, 2 * jj, 0, route_head=2 * jj + 2)
                    step(L, 2 * jj + 1, 1, route_head=2 * jj + 3)
                step(L, PH - 2, 0)
                step(L, PH - 1, 1, last=True)
                pe.wait_ge(s["acc_evac"], TB * NO * L + NO)
                seed(L, 1)
                with pe.Fori(PH // 2, PH - 1) as jj:
                    step(L, 2 * jj, 0)
                    step(L, 2 * jj + 1, 1)
                step(L, GROUPS - 2, 0)
                step(L, GROUPS - 1, 1, last=True)


def _constants(np):
    i = np.arange(P)
    tri = (i[:, None] <= i[None, :]).astype(np.float32)
    ropes = []
    tok = np.arange(S)
    posn = np.stack([tok // 64, tok % 64], -1).astype(np.float32)
    nf = AD // 4
    inv = (10000.0 ** (-np.arange(nf, dtype=np.float32) / nf)).astype(np.float32)
    ang = posn[:, :, None] * inv
    for f in (np.cos, np.sin):
        ropes.append(f(ang).astype(np.float32).reshape(TB, P, 2 * nf).transpose(1, 0, 2).reshape(P, TB * 2 * nf))
    mask = np.where(i[None, :] <= i[:, None], np.float32(0), np.float32(NEG))
    consts = np.concatenate([np.eye(P), tri, tri.T, np.ones((P, P)), mask, mask.T, *ropes,
                             np.broadcast_to(np.arange(PK), (P, PK))], 1).astype(np.float32)
    pool = np.zeros((4, S, S), np.float32)
    for g, w in enumerate(POOLW):
        for t in range(S):
            lo, hi = max(t - w // 2, 0), min(t + w // 2, S)
            pool[g, lo:hi, t] = np.float32(1.0) / np.float32(hi - lo)
            pool[g, t, t] -= 1.0
    pool = pool.reshape(4, TB, P, S).transpose(2, 0, 1, 3).reshape(P, 4 * TB * S)
    return np.ascontiguousarray(consts), np.ascontiguousarray(pool)


def kernel(**inputs):
    import numpy as np
    import concourse.bacc as bacc
    from concourse.bass_utils import run_bass_kernel_spmd

    a = {k: np.asarray(v) for k, v in inputs.items()}

    def tiles(w, halves):
        n = w.shape[1] // BANK
        return w.reshape(halves, KC // halves, P, n, BANK).transpose(3, 0, 2, 1, 4).reshape(n, halves, P, -1)

    w_in = a["w_in"][0]
    aq, ak, av = AH * AD, AH * AD + AKV * AD, AH * AD + 2 * AKV * AD
    mq, mv = av + 2 * MH * MD, av + 3 * MH * MD
    mo = mv + MH * MD
    cols = [w_in[:, aq:ak], w_in[:, :aq], w_in[:, ak:av], w_in[:, av:mq], w_in[:, mq:mv], w_in[:, mv:mo]]
    w_proj = np.concatenate(cols, 1)
    consts, poolm = _constants(np)
    arrays = {
        "x": a["x"][0],
        "consts": consts,
        "poolm": poolm,
        "w_proj": tiles(w_proj, 2),
        "w_gates": w_in[:, mo:].reshape(KC, P, 4 * MH).transpose(1, 0, 2).reshape(P, -1),
        "w_out": tiles(a["w_out"][0], 2).transpose(1, 0, 2, 3).reshape(2 * NO, P, -1),
        "b_gate": a["b_gate"][0],
        "conv_w": a["conv_w"][0].reshape(CW, 4 * MH, P).transpose(2, 1, 0).reshape(P, -1),
        "q_gain": a["q_gain"][0],
        "k_gain": a["k_gain"][0],
        "ml_gain": a["ml_gain"][0],
        "gains": np.stack([a["norm_mix_g"][0], a["norm_ffn_g"][0], a["norm_mix_g"][1], a["norm_ffn_g"][1], a["norm_f"]]),
        "layer_scale": a["layer_scale"][0],
        "pool_w": a["pool_w"][0].reshape(4, 4, P, BANK).transpose(2, 0, 1, 3).reshape(P, -1),
        "wq": a["peer_wq"].reshape(LAYERS, KC, P, PH, 2 * P).transpose(0, 3, 2, 1, 4).reshape(LAYERS, PH, P, -1),
        "keys": a["peer_keys"].reshape(LAYERS, 2 * PH, NK, P).transpose(0, 3, 1, 2).reshape(LAYERS, P, -1),
        "pu0": a["peer_u"][0], "pv0": a["peer_v"][0], "pu1": a["peer_u"][1], "pv1": a["peer_v"][1],
    }
    nc = bacc.Bacc("TRN2", target_bir_lowering=False, num_devices=1)
    args = []
    for name in list(arrays):
        arrays[name] = np.ascontiguousarray(arrays[name])
        args.append(nc.dram_tensor(name, arrays[name].shape, mybir.dt.from_np(arrays[name].dtype),
                                   kind="ExternalInput").ap())
    args.append(nc.dram_tensor("out", (S, D), fp32, kind="ExternalOutput").ap())
    hybrid_encoder(nc, *args)
    r = run_bass_kernel_spmd(nc, [arrays], core_ids=[0])
    return r.results[0]["out"].reshape(1, S, D)
```

```python
from contextlib import ExitStack

import concourse.bass as bass
from concourse import mybir

fp32 = mybir.dt.float32
u32 = mybir.dt.uint32
ALU = mybir.AluOpType
ACT = mybir.ActivationFunctionType
X = mybir.AxisListType.X

P = 128
D = 2048
TB = 2
S = TB * P
KC = D // P
LAYERS = 2
EPS = 1e-6
AH, AKV, AD = 8, 2, 128
MH, MD = 4, 256
CW = 5
PAD = CW // 2
PH, PK, NK = 8, 16, 128
EXPERTS = NK * NK
NEG = -3.0e38
BANK = 512

R_AK = 0
R_AQ = R_AK + AKV * AD
R_AV = R_AQ + AH * AD
R_MV = R_AV + AKV * AD
R_MO = R_MV + MH * MD
RAW = R_MO + MH * MD
N_QKV = R_MV // BANK
N_MQK = 2 * MH * MD // BANK
N_MV = MH * MD // BANK
N_IN = N_QKV + N_MQK + 2 * N_MV
NO = D // BANK
MC = MD // P
HALF = KC // 2

WR = 3
UR, VR = 4, 4
DR = 4
GROUPS = TB * PH
ROWS = GROUPS * PK
EVENTS = PH + 2
ROUTE = 15
POOLW = (2, 4, 8, 16)
ARENA = 41344
OUT_AT = 33152


def hybrid_encoder(nc, x, consts, poolm, w_proj, w_gates, w_out, b_gate, conv_w, q_gain, k_gain,
                   ml_gain, gains, layer_scale, pool_w, wq, keys, pu0, pv0, pu1, pv1, out):
    pu, pv = [pu0, pu1], [pv0, pv1]
    with ExitStack() as ctx:
        def sb(name, shape, dt=fp32):
            return ctx.enter_context(nc.sbuf_tensor(name, shape, dt))

        h = sb("h", [P, TB, D])
        xnT = sb("xnT", [P, KC, S])
        gB = sb("gB", [P, D])
        cst = sb("cst", [P, 8 * P + PK])
        ident, tri_f, tri_b, ones = (cst[:, i * P:(i + 1) * P] for i in range(4))
        masks = cst[:, 4 * P:6 * P].rearrange("p (d r) -> p d r", d=2)
        rope_c = cst[:, 6 * P:7 * P].rearrange("p (t a f) -> p t a f", t=TB, a=2)
        rope_s = cst[:, 7 * P:8 * P].rearrange("p (t a f) -> p t a f", t=TB, a=2)
        iota16 = cst[:, 8 * P:8 * P + PK]
        stat = sb("stat", [P, 8])
        ss, ms, rt, rs = (stat[:, 2 * i:2 * i + 2] for i in range(4))
        arena = sb("arena", [P, ARENA])
        psum = [ctx.enter_context(nc.psum_tensor(f"bank{i}", [P, BANK], fp32)) for i in range(8)]

        def carver(at, end):
            place = [at]

            def carve(*shape):
                if not shape:
                    return place[0]
                n = 1
                for d in shape:
                    n *= d
                v = arena[:, place[0]:place[0] + n]
                place[0] += n
                assert place[0] <= end, (place[0], end)
                if len(shape) == 1:
                    return v
                names = "abcd"[:len(shape)]
                return v.rearrange(f"p ({' '.join(names)}) -> p {' '.join(names)}",
                                   **{c: d for c, d in zip(names[:-1], shape[:-1])})
            return carve

        U = carver(0, ARENA)(UR, D)
        vring = carver(UR * D, ARENA)
        V = vring(VR, D)
        carve = vring
        wqb = carve(2, KC, 2 * P)
        xn0 = carve(D)
        keysT = carve(2 * PH, NK)
        qT = carve(2, S)
        diag = carve(DR, P)
        act = carve(2, PK)
        ga = carve(PK)
        wk = carve(2, PK)
        gates = carve(GROUPS, PK)
        s16 = carve(4, PK)
        i16f = carve(4, PK)
        stmp = carve(4, NK)
        cand, cand2 = carve(TB, PK, PK), carve(TB, PK, PK)
        b16, bd, ex = carve(TB, PK), carve(TB, PK), carve(TB, PK)
        abf = carve(4, PK)
        eq = carve(4, PK, PK)
        ev = carve(TB, 2, PK)
        exs, exr = carve(TB), carve(TB)
        xn1 = carver(OUT_AT, ARENA)(D)
        xns = [xn0, xn1]
        poolw = U.rearrange("p a b -> p (a b)").rearrange("p (g k c) -> p g k c", g=4, k=4)
        slot1 = wqb[:, 1].rearrange("p k c -> p (k c)")
        PM = slot1[:, 0:D].rearrange("p (g t s) -> p g t s", g=4, t=TB)
        lsB = slot1[:, D:2 * D]
        ytmp = eq.rearrange("p q k a -> p (q k a)").rearrange("p (a b) -> p a b", a=2)
        idx_all = sb("idx_all", [P, GROUPS, PK], u32)
        idxU = [sb(f"idxU{i}", [P, PK], u32) for i in range(2)]
        idxV = [sb(f"idxV{i}", [P, PK], u32) for i in range(2)]
        i16 = sb("i16", [P, 4, PK], u32)
        pos = sb("pos", [P, TB, PK], u32)
        ab = sb("ab", [P, TB, 2, PK], u32)

        yT = carver(UR * D, ARENA)(KC, S)
        nrm0 = yT.rearrange("p a b -> p (a b)").rearrange("p (t d) -> p t d", t=TB)
        wslot = [carver(a, ARENA)(HALF, BANK) for a in (UR * D + KC * S, OUT_AT, OUT_AT + HALF * BANK)]
        raw = carver(0, UR * D)(TB, RAW)
        carve = carver((UR + VR) * D, OUT_AT)
        mqkT = carve(2 * MH * MC, S + 2 * PAD)
        cv = carve(2, S)
        Em = carve(TB, 2, MH, P)
        hm = carve(TB, MH, MD)
        rtmp = hm.rearrange("p t m c -> p (t m c)")[:, 0:10 * AD].rearrange("p (a b) -> p a b", a=2)
        mlg = carve(MH * MD)
        gB_q, gB_k = carve(AD), carve(AD)
        cvw = carve(2 * MH * MC * CW)
        wg = carve(KC, 4 * MH)
        bgB = carve(4 * MH)
        gsb = carve(TB, 2, 2, MH)
        lf, bc, scol, Mx, mprev, G, eabs, elog = (carve(TB, 2, MH) for _ in range(8))
        smax, c1 = carve(2, MH), carve(2, MH)
        expi = carve(2 * 2 * TB * MH + 2 * MH)
        expo = carve(2 * 2 * TB * MH + 2 * MH)
        dd, dr = carve(2), carve(2)
        sq1, sq2 = carve(TB, AKV + AH), carve(TB, MH)
        sqt = carve(MD)
        mxs, nmx, psm, prc = carve(2), carve(2), carve(2), carve(2)
        at = carve()
        carve = carver(at, OUT_AT)
        qkr = carve((AKV + AH) * AD)
        aT = carve(AKV + AH, S)
        Pb = carve(2, S)
        PT = carve(2, 2, P)
        carve = carver(at, OUT_AT)
        kw = carve(TB, MH, MD)
        Csb = carve(2, MC, MD + 1)
        Isb = carve(2, MD + 1)
        num2 = carve(MD + 1)
        A = carve(2, 2, P)
        AT = carve(2, 2, P)

        names = """ld_x ld_c ld_small ld_gain ld_keys ld_wq0 ld_wq1 ld_pool ld_pm ld_scale out_done
            w_got0 w_got1 w_got2 w_used
            sq_done ms_done root_done xn_ready tp_done xt_act xt_dve
            gates_mm gsum eabs_done elog_done ln_done lf_ready cum_done scol_ready srow_done
            expi_ready expo_done em_sub em_ready
            raw_done raw_evac mqk_done mqk_evac conv_done silu_done kscaled ktp_done kw_ready
            q_sq q_ms q_root rope_done atp_mm atp_ready sc_mm nmax p_exp p_ready pt_mm pt_ready pv_mm yt_ready
            s_mm a_ready at_mm at_ready c_mm c_ready i_mm i_ready n_mm comb_done
            y_sq y_ms y_root mo_sig hm_ready ymt_mm ymt_ready part_done part_added out_mm h_ready
            q_mm q_ready sc_done sc_free bd_ready ex_done idxu_ready idxv_ready
            dot_done gelu_done wk_ready diag_ready v_mm acc_evac
            v_dve pool_mm pool_ev pool_add py_mm h1_ready fin_ready
            dve dve_passed act_passed pool_passed""".split()
        s = {n: ctx.enter_context(nc.semaphore(n)) for n in names}
        w_got = [s["w_got0"], s["w_got1"], s["w_got2"]]
        ld_wq = [s["ld_wq0"], s["ld_wq1"]]
        u_got = [ctx.enter_context(nc.semaphore(f"u_got{i}")) for i in range(UR)]
        v_got = [ctx.enter_context(nc.semaphore(f"v_got{i}")) for i in range(VR)]

        def hold(eng, name, value, passed):
            eng.wait_ge(s[name], value)
            eng.sem_inc(s[passed], 1)

        class Steps:

            def __init__(self):
                self.base, self.n = 0, 0

            def link(self, eng, ins):
                self.n += 1
                ins.then_inc(s["dve"], 1)
                if isinstance(self.base, int):
                    eng.wait_ge(s["dve"], self.base + self.n)
                else:
                    hold(eng, "dve", self.base + self.n, "dve_passed")

        NORM_T = {0: 0, 1: 1, 3: 2}

        SC_BANK = (0, 3)
        AU, AT0 = 2 * AH, 10
        ATP = (AT0 - 4, AT0 - 1)
        MU = 2 * MH

        def w_half(i):
            return i % WR, 16 * (i // WR + 1)

        LAST_HALF = 2 * N_IN + 2 * NO - 1 + WR

        def half_read(i):
            c, m = i // 2, i - 2 * N_IN
            if m >= NO:
                return s["out_mm"], m - NO + 1
            if m >= 0:
                return s["part_done"], m + 1
            if i % 2 == 0:
                return s["w_used"], c + 1
            if N_QKV <= c < N_QKV + N_MQK:
                return s["mqk_done"], 4 * (c - N_QKV + 1)
            return s["raw_done"], TB * ((c if c < N_QKV else c - N_MQK) + 1)

        block = ctx.enter_context(nc.Block())

        @block.sync
        def _(sp):
            def load_half(i, src):
                if i >= WR:
                    sp.wait_ge(*half_read(i - WR))
                sp.dma_start(wslot[i % WR].rearrange("p k c -> p (k c)"), src).then_inc(w_got[i % WR], 16)

            def gain(o):
                if o:
                    sp.wait_ge(s["xn_ready"], TB * o)
                sp.dma_start(gB[:], gains[o].partition_broadcast(P)).then_inc(s["ld_gain"], 16)

            sp.dma_start(h[:, 0, :], x[0:P, :]).then_inc(s["ld_x"], 16)
            gain(0)
            sp.dma_start(cst[:], consts).then_inc(s["ld_c"], 16)
            sp.wait_ge(s["ld_x"], 16)
            sp.dma_start(h[:, 1, :], x[P:S, :]).then_inc(s["ld_x"], 16)
            for i in range(2):
                load_half(i, w_proj[i // 2, i % 2])
            sp.dma_start(wg, w_gates.rearrange("p (k c) -> p k c", k=KC)).then_inc(s["ld_small"], 16)
            sp.dma_start(bgB, b_gate.partition_broadcast(P)).then_inc(s["ld_small"], 16)
            sp.dma_start(cvw, conv_w).then_inc(s["ld_small"], 16)
            sp.dma_start(gB_q, q_gain.partition_broadcast(P)).then_inc(s["ld_small"], 16)
            sp.dma_start(gB_k, k_gain.partition_broadcast(P)).then_inc(s["ld_small"], 16)
            sp.dma_start(mlg, ml_gain.partition_broadcast(P)).then_inc(s["ld_small"], 16)
            for i in range(2, 2 * N_IN):
                load_half(i, w_proj[i // 2, i % 2])
                if i == 4:
                    gain(1)
            for m in range(2 * NO):
                load_half(2 * N_IN + m, w_out[m])
                if m == NO + 1:
                    sp.wait_ge(s["ymt_ready"], 2 * TB)
                    sp.wait_ge(s["yt_ready"], AU)
                    sp.dma_start(keysT, keys[0].rearrange("p (a n) -> p a n", a=2 * PH)).then_inc(s["ld_keys"], 16)
                    for hd in range(2):
                        sp.dma_start(wqb[:, hd].rearrange("p k c -> p (k c)"), wq[0, hd]).then_inc(ld_wq[hd], 16)
            sp.wait_ge(s["out_mm"], NO + 1)
            slot, _ = w_half(LAST_HALF)
            sp.dma_start(wslot[slot].rearrange("p k c -> p (k c)"), w_out[NO]).then_inc(w_got[slot], 16)
            for L in range(LAYERS):
                gain(2 + 2 * L)
                for hd in range(2, PH):
                    sp.wait_ge(s["q_mm"], EVENTS * L + hd + 1)
                    sp.dma_start(wqb[:, hd % 2].rearrange("p k c -> p (k c)"), wq[L, hd]).then_inc(ld_wq[hd % 2], 16)
                if L == 0:
                    sp.wait_ge(s["q_mm"], EVENTS)
                    sp.dma_start(PM.rearrange("p g t s -> p (g t s)"), poolm).then_inc(s["ld_pm"], 16)
                    sp.wait_ge(s["sc_done"], EVENTS)
                    sp.wait_ge(s["dot_done"], ROWS)
                    sp.wait_ge(v_got[VR - 1], 16 * (ROWS // VR))
                    sp.dma_start(poolw, pool_w.rearrange("p (g k c) -> p g k c", g=4, k=4)).then_inc(s["ld_pool"], 16)
                    sp.dma_start(lsB, layer_scale.partition_broadcast(P)).then_inc(s["ld_scale"], 16)
                    sp.dma_start(wqb[:, 0].rearrange("p k c -> p (k c)"), wq[1, 0]).then_inc(ld_wq[0], 16)
                    gain(3)
                    sp.dma_start(keysT, keys[1].rearrange("p (a n) -> p a n", a=2 * PH)).then_inc(s["ld_keys"], 16)
                    sp.wait_ge(s["h1_ready"], 4 * TB)
                    sp.dma_start(wqb[:, 1].rearrange("p k c -> p (k c)"), wq[1, 1]).then_inc(ld_wq[1], 16)
            for t in range(TB):
                sp.wait_ge(s["fin_ready"], t + 1)
                sp.dma_start(out[t * P:(t + 1) * P, :], h[:, t, :]).then_inc(s["out_done"], 16)
            sp.wait_ge(s["out_done"], 16 * TB)

        @block.gpsimd
        def _(pool):
            def gather(L, g, par, k, first, ring, R, table, idx, used, listed, got):
                if L or not first or k >= R:
                    hold(pool, used, L * ROWS + g * PK + k - R + 1, "pool_passed")
                if k == 0:
                    hold(pool, listed, L * GROUPS + g + 1, "pool_passed")
                nc.gpsimd.indirect_dma_start(
                    ring[:, k % R], None, table[L], bass.IndirectOffsetOnAxis(idx[par][:, k:k + 1], 0)
                ).then_inc(got[k % R], 16)

            def gather_u(L, g, par, k, first=False):
                gather(L, g, par, k, first, U, UR, pu, idxU, "dot_done", "idxu_ready", u_got)

            def gather_v(L, g, par, k, first=False):
                gather(L, g, par, k, first, V, VR, pv, idxV, "v_mm", "idxv_ready", v_got)

            def step(L, j, par, first=False):
                for k in range(PK):
                    gather_u(L, j + 1, 1 - par, k)
                    if first and L == 0 and k == 0:
                        pool.wait_ge(s["out_mm"], TB * NO)
                    gather_v(L, j, par, k, first=first)

            for L in range(LAYERS):
                for k in range(PK):
                    if L and k < 4:
                        pool.wait_ge(s["py_mm"], 4 + k + 1)
                    gather_u(L, 0, 0, k, first=True)
                step(L, 0, 0, first=True)
                step(L, 1, 1)
                with pool.Fori(1, PH - 1) as jj:
                    step(L, 2 * jj, 0)
                    step(L, 2 * jj + 1, 1)
                step(L, GROUPS - 2, 0)
                for k in range(PK):
                    gather_v(L, GROUPS - 1, 1, k)

        @block.scalar
        def _(e):
            activation = nc.scalar.activation

            def norm(o, t):
                dst = nrm0[:, t] if o == 0 else xns[t]
                if o == 0:
                    e.wait_ge(s["ld_x"], 16 * (t + 1))
                elif o == 1:
                    e.wait_ge(s["h_ready"], NO * (t + 1))
                elif o == 3:
                    e.wait_ge(s["h1_ready"], 4 * (t + 1))
                    e.wait_ge(s["pool_mm"], KC // 2 + 8 * t)
                else:
                    e.wait_ge(s["acc_evac"], NO * (TB * (o // 2 - 1) + t + 1))
                    e.wait_ge(s["dot_done"], ROWS * (o // 2 - 1) + ROWS // 2 * (t + 1))
                activation(dst, h[:, t, :], ACT.Square, accum_out=ss[:, t:t + 1]).then_inc(s["sq_done"], 1)
                e.wait_ge(s["ms_done"], TB * o + t + 1)
                activation(rt[:, t:t + 1], ms[:, t:t + 1], ACT.Sqrt).then_inc(s["root_done"], 1)

            def evac_xt(o, t):
                for q in (0, 2):
                    e.wait_ge(s["tp_done"], 8 * o + 4 * t + q + 1)
                    activation(xnT[:, 4 * q:4 * q + 4, t * P:(t + 1) * P],
                               psum[4 + q][:, :].rearrange("p (a b) -> p a b", a=4), ACT.Copy
                               ).then_inc(s["xt_act"], 1)

            def evac_raw(r):
                for t in range(TB):
                    e.wait_ge(s["raw_done"], TB * r + t + 1)
                    activation(raw[:, t, r * BANK:(r + 1) * BANK], psum[4 + t][:, :], ACT.Copy
                               ).then_inc(s["raw_evac"], 1)

            for t in range(TB):
                norm(0, t)
            for t in range(TB):
                evac_xt(0, t)
            e.wait_ge(s["gsum"], 1)
            activation(eabs, gsb[:, :, :, 1], ACT.Abs).then_inc(s["eabs_done"], 1)
            e.wait_ge(s["eabs_done"], 1)
            activation(elog, eabs, ACT.Exp, scale=-1.0).then_inc(s["elog_done"], 1)
            e.wait_ge(s["elog_done"], 1)
            activation(eabs, elog, ACT.Ln, bias=1.0).then_inc(s["ln_done"], 1)
            evac_raw(0)
            evac_raw(1)
            e.wait_ge(s["expi_ready"], 1)
            activation(expo, expi, ACT.Exp).then_inc(s["expo_done"], 1)
            e.wait_ge(s["em_sub"], 1)
            em = Em.rearrange("p a b c d -> p (a b c d)")
            activation(em, em, ACT.Exp).then_inc(s["em_ready"], 1)
            evac_raw(2)
            e.wait_ge(s["raw_evac"], TB * N_QKV)
            for t in range(TB):
                for i in range(AKV + AH):
                    if t + i:
                        e.wait_ge(s["q_sq"], (AKV + AH) * t + i)
                    activation(sqt[:, 0:AD], raw[:, t, R_AK + i * AD:R_AK + (i + 1) * AD], ACT.Square,
                               accum_out=sq1[:, t, i:i + 1]).then_inc(s["q_sq"], 1)
            e.wait_ge(s["q_ms"], 1)
            activation(sq1, sq1, ACT.Sqrt).then_inc(s["q_root"], 1)

            def silu(c):
                e.wait_ge(s["conv_done"], c + 1)
                activation(mqkT[:, c, PAD:PAD + S], cv[:, c % 2], ACT.Silu).then_inc(s["silu_done"], 1)

            def attention(i):
                if i < AU:
                    e.wait_ge(s["nmax"], i + 1)
                    if i >= 2:
                        e.wait_ge(s["pt_mm"], i - 1)
                    activation(Pb[:, i % 2], psum[SC_BANK[i % 2]][:, 0:S], ACT.Exp,
                               bias=nmx[:, i % 2:i % 2 + 1], scale=AD ** -0.5,
                               accum_out=psm[:, i % 2:i % 2 + 1]).then_inc(s["p_exp"], 1)
                if 1 <= i <= AU:
                    u = i - 1
                    e.wait_ge(s["pt_mm"], u + 1)
                    if u >= 2:
                        e.wait_ge(s["pv_mm"], u - 1)
                    activation(PT[:, u % 2], psum[1][:, 0:S].rearrange("p (a b) -> p a b", a=2),
                               ACT.Copy).then_inc(s["pt_ready"], 1)
                if i >= 2:
                    u = i - 2
                    hd, t = u // 2, u % 2
                    e.wait_ge(s["pv_mm"], u + 1)
                    activation(yT[:, hd, t * P:(t + 1) * P], psum[2][:, 0:P], ACT.Copy
                               ).then_inc(s["yt_ready"], 1)

            for g in range(8 * N_MQK):
                n, hf, i = g // 8, g // 4 % 2, g % 4
                if g in ATP:
                    t = ATP.index(g)
                    for q in range(3):
                        m = 3 * t + q
                        w = 4 if q < 2 else 2
                        e.wait_ge(s["atp_mm"], m + 1)
                        activation(aT[:, 4 * q:4 * q + w, t * P:(t + 1) * P],
                                   psum[2 + m % 2][:, 0:w * P].rearrange("p (a b) -> p a b", a=w), ACT.Copy
                                   ).then_inc(s["atp_ready"], 1)
                if hf == 1:
                    e.wait_ge(s["mqk_done"], 4 * n + i + 1)
                    activation(mqkT[:, 4 * n + i, PAD:PAD + S], psum[4 + i][:, 0:S], ACT.Copy).then_inc(s["mqk_evac"], 1)
                elif n and i % 2 == 1:
                    silu(4 * (n - 1) + i - 1)
                    silu(4 * (n - 1) + i)
                if 0 <= g - AT0 < AU + 2:
                    attention(g - AT0)
            for c in range(4 * (N_MQK - 1), 4 * N_MQK):
                silu(c)
            evac_raw(N_QKV)
            e.wait_ge(s["expo_done"], 1)
            for t in range(TB):
                for hp in range(2):
                    e.wait_ge(s["ktp_done"], 2 * t + hp + 1)
                    for i in range(2):
                        hd = 2 * hp + i
                        activation(kw[:, t, hd], psum[6 + hp][:, i * MD:(i + 1) * MD], ACT.Copy,
                                   scale=expo[:, 32 + 4 * t + hd:33 + 4 * t + hd]).then_inc(s["kw_ready"], 1)
            evac_raw(N_QKV + 1)

            def mlstm(i):
                if i < MU:
                    for c in range(MC):
                        e.wait_ge(s["c_mm"], MC * i + c + 1)
                        if i >= 2:
                            e.wait_ge(s["i_mm"], i - 1)
                        activation(Csb[:, i % 2, c], psum[2 + c][:, 0:MD + 1], ACT.Copy).then_inc(s["c_ready"], 1)
                if i:
                    u = i - 1
                    hd, t = u // 2, u % 2
                    e.wait_ge(s["at_mm"], u + 1)
                    if u >= 2:
                        e.wait_ge(s["n_mm"], 2 * (u - 1))
                    activation(AT[:, u % 2], psum[1][:, 0:2 * P].rearrange("p (a b) -> p a b", a=2),
                               ACT.Copy).then_inc(s["at_ready"], 1)
                    e.wait_ge(s["i_mm"], u + 1)
                    if u >= 2:
                        e.wait_ge(s["comb_done"], u - 1)
                    w = (t * 2 + (1 - t)) * MH + hd
                    activation(Isb[:, u % 2], psum[2][:, 0:MD + 1], ACT.Copy,
                               scale=expo[:, w:w + 1]).then_inc(s["i_ready"], 1)

            for g in range(4 * N_MV):
                if g % 4 == 3:
                    evac_raw(N_QKV + N_MV + g // 4)
                mlstm(g)
            mlstm(MU)
            e.wait_ge(s["raw_evac"], TB * RAW // BANK)
            activation(raw[:, :, R_MO:RAW], raw[:, :, R_MO:RAW], ACT.Sigmoid).then_inc(s["mo_sig"], 1)
            e.wait_ge(s["comb_done"], MU)
            for t in range(TB):
                for hd in range(MH):
                    e.wait_ge(*((s["y_sq"], MH * t + hd) if t + hd else (s["q_sq"], TB * (AKV + AH))))
                    activation(sqt, hm[:, t, hd], ACT.Square, accum_out=sq2[:, t, hd:hd + 1]).then_inc(s["y_sq"], 1)
            e.wait_ge(s["y_ms"], 1)
            activation(sq2, sq2, ACT.Sqrt).then_inc(s["y_root"], 1)
            for m in range(2 * TB):
                t, q = m // 2, m % 2
                e.wait_ge(s["ymt_mm"], m + 1)
                activation(yT[:, AH + 4 * q:AH + 4 + 4 * q, t * P:(t + 1) * P],
                           psum[4 + q][:, :].rearrange("p (a b) -> p a b", a=4), ACT.Copy
                           ).then_inc(s["ymt_ready"], 1)

            def route_q(L, ev_, t0, t1):
                n0 = EVENTS * L + ev_
                hold(e, "q_mm", n0 + 1, "act_passed")
                activation(qT[:, :, t0 * P:t1 * P],
                           psum[6][:, :].rearrange("p (a b) -> p a b", a=2)[:, :, t0 * P:t1 * P], ACT.Copy
                           ).then_inc(s["q_ready"], 1)

            def route_exp(L, ev_, t0, t1):
                hold(e, "bd_ready", EVENTS * L + ev_ + 1, "act_passed")
                activation(ex[:, t0:t1], bd[:, t0:t1], ACT.Exp).then_inc(s["ex_done"], 1)

            def gelu(L, j, par):
                hold(e, "dot_done", L * ROWS + j * PK + PK, "act_passed")
                activation(ga, act[:, par], ACT.Gelu).then_inc(s["gelu_done"], 1)

            def diagonal(L, j, par, k, first=False):
                if k == 0:
                    hold(e, "wk_ready", L * GROUPS + j + 1, "act_passed")
                if L or not first or k >= DR:
                    hold(e, "v_mm", L * ROWS + j * PK + k - DR + 1, "act_passed")
                activation(diag[:, k % DR], ident, ACT.Copy, scale=wk[:, par, k:k + 1]).then_inc(s["diag_ready"], 1)

            def first_step(L):
                gelu(L, 0, 0)
                norm(1 + 2 * L, 1)
                for k in range(PK):
                    diagonal(L, 0, 0, k, first=True)
                    if k == 1:
                        evac_xt(1 + L, 1)
                    if k == 2:
                        route_q(L, 2, 1, 2)
                    if k == 4:
                        route_exp(L, 2, 1, 2)
                        route_q(L, 3, 1, 2)
                    if k == 7:
                        route_exp(L, 3, 1, 2)
                        route_q(L, 4, 0, 2)
                    if k == 11:
                        route_exp(L, 4, 0, 2)

            def step(L, j, par, route_head=None, pool=False, shared=False):
                gelu(L, j, par)
                for k in range(PK):
                    if not (shared and k % VR == VR - 1):
                        diagonal(L, j, par, k)
                    if pool and 3 <= k < 3 + KC // 2:
                        n = k - 3
                        e.wait_ge(s["pool_mm"], n + 1)
                        activation(xnT[:, 2 * n:2 * n + 2, :], psum[4 + n % 4][:, :].rearrange("p (a b) -> p a b", a=2),
                                   ACT.Copy).then_inc(s["pool_ev"], 1)
                    if route_head is not None and k == 4:
                        route_q(L, route_head + 2, 0, 2)
                    if route_head is not None and k == 10:
                        route_exp(L, route_head + 2, 0, 2)

            def evac_acc(L):
                e.wait_ge(s["v_mm"], L * ROWS + PH * PK)
                for n in range(NO):
                    activation(h[:, 0, n * BANK:(n + 1) * BANK], psum[n][:, :], ACT.Copy).then_inc(s["acc_evac"], 1)

            def pooled(q):
                e.wait_ge(s["pool_mm"], KC // 2 + 4 + q + 1)
                activation(xnT[:, 4 * q:4 * q + 4, P:S], psum[4 + q][:, :].rearrange("p (a b) -> p a b", a=4),
                           ACT.Copy).then_inc(s["pool_ev"], 1)

            for L in range(LAYERS):
                if L:
                    norm(2, 1)
                norm(1 + 2 * L, 0)
                if L:
                    for q in range(4):
                        pooled(q)
                evac_xt(1 + L, 0)
                route_q(L, 0, 0, 1)
                route_exp(L, 0, 0, 1)
                route_q(L, 1, 0, 1)
                route_exp(L, 1, 0, 1)
                first_step(L)
                step(L, 1, 1, route_head=3)
                with e.Fori(1, 3) as jj:
                    step(L, 2 * jj, 0, route_head=2 * jj + 2)
                    step(L, 2 * jj + 1, 1, route_head=2 * jj + 3)
                step(L, PH - 2, 0)
                step(L, PH - 1, 1)
                evac_acc(L)
                norm(2 + 2 * L, 0)
                with e.Fori(PH // 2, PH - 1) as jj:
                    step(L, 2 * jj, 0)
                    step(L, 2 * jj + 1, 1)
                step(L, GROUPS - 2, 0, pool=L == 0)
                step(L, GROUPS - 1, 1, shared=True)
            norm(4, 1)

        @block.vector
        def _(v):
            st = Steps()
            vec = nc.vector

            def link(ins):
                st.link(v, ins)

            def norm(o, t):
                one = slice(t, t + 1)
                v.wait_ge(s["sq_done"], TB * o + t + 1)
                vec.tensor_scalar(ms[:, one], ss[:, one], 1.0 / D, EPS, ALU.mult, ALU.add).then_inc(s["ms_done"], 1)
                v.wait_ge(s["root_done"], TB * o + t + 1)
                link(vec.reciprocal(rs[:, one], rt[:, one]))
                v.wait_ge(s["ld_gain"], 16 * (o + 1))
                dst = nrm0[:, t] if o == 0 else h[:, t, :] if o == 4 else xns[t]
                vec.scalar_tensor_tensor(dst, h[:, t, :], rs[:, one], gB[:], ALU.mult, ALU.mult
                                         ).then_inc(s["fin_ready" if o == 4 else "xn_ready"], 1)

            def evac_xt(o, t):
                for q in (1, 3):
                    v.wait_ge(s["tp_done"], 8 * o + 4 * t + q + 1)
                    vec.tensor_copy(xnT[:, 4 * q:4 * q + 4, t * P:(t + 1) * P],
                                    psum[4 + q][:, :].rearrange("p (a b) -> p a b", a=4)).then_inc(s["xt_dve"], 1)

            vec.memset(mqkT[:, :, 0:PAD], 0.0)
            link(vec.memset(mqkT[:, :, PAD + S:], 0.0))
            for t in range(TB):
                norm(0, t)
            for t in range(TB):
                evac_xt(0, t)
            v.wait_ge(s["ld_small"], 6 * 16)
            v.wait_ge(s["gates_mm"], 1)
            g_ps = psum[6][:, 0:TB * 4 * MH].rearrange("p (t c) -> p t c", t=TB)
            vec.tensor_tensor(gsb.rearrange("p t d x m -> p t (d x m)"), g_ps,
                              bgB.unsqueeze(1).to_broadcast([P, TB, 4 * MH]), ALU.add).then_inc(s["gsum"], 1)
            v.wait_ge(s["gsum"], 1)
            v.wait_ge(s["ln_done"], 1)
            for t in range(TB):
                for d in range(2):
                    last = vec.scalar_tensor_tensor(lf[:, t, d], gsb[:, t, d, 1], 0.0, eabs[:, t, d], ALU.min, ALU.subtract)
            last.then_inc(s["lf_ready"], 1)
            v.wait_ge(s["cum_done"], 1)
            w8 = TB * 2 * MH
            cum = psum[7][:, 0:w8].rearrange("p (t d m) -> p t d m", t=TB, d=2)
            tot = psum[7][:, w8:2 * w8].rearrange("p (t d m) -> p t d m", t=TB, d=2)
            vec.tensor_copy(bc, cum)
            vec.tensor_copy(G, tot)
            vec.memset(mprev, 0.0)
            for t in range(TB):
                ins = vec.tensor_tensor(scol[:, t], gsb[:, t, :, 0], cum[:, t], ALU.subtract)
            ins.then_inc(s["scol_ready"], 1)
            v.wait_ge(s["srow_done"], 4)
            for t in range(TB):
                for d in range(2):
                    row = psum[2 * t + d][:, :].rearrange("p (m r) -> p m r", m=MH)
                    ins = vec.tensor_tensor(Em[:, t, d], row, masks[:, d].unsqueeze(1).to_broadcast([P, MH, P]), ALU.add)
                    if t == d:
                        ins = vec.tensor_reduce(smax[:, d], row, X, ALU.max)
            link(ins)
            for t in range(TB):
                for d in range(2):
                    vec.tensor_reduce(Mx[:, t, d], Em[:, t, d], X, ALU.max)
            link(vec.tensor_scalar(c1, smax, 0.0, None, ALU.max))
            for d in range(2):
                ins = vec.tensor_tensor(mprev[:, 1 - d, d], G[:, d, d], c1[:, d], ALU.add)
            link(ins)
            link(vec.tensor_tensor(Mx, Mx, mprev, ALU.max))
            e16 = [expi[:, i * 16:(i + 1) * 16] for i in range(2)]
            vec.tensor_tensor(e16[0], mprev.rearrange("p t d m -> p (t d m)"), Mx.rearrange("p t d m -> p (t d m)"), ALU.subtract)
            vec.scalar_tensor_tensor(e16[1], bc.rearrange("p t d m -> p (t d m)"), -1.0,
                                     Mx.rearrange("p t d m -> p (t d m)"), ALU.mult, ALU.subtract)
            for d in range(2):
                ins = vec.tensor_tensor(expi[:, 32 + 4 * d:36 + 4 * d], scol[:, d, d], c1[:, d], ALU.subtract)
            ins.then_inc(s["expi_ready"], 1)
            em = Em.rearrange("p t d m r -> p (t d m) r")
            vec.tensor_tensor(em, em, Mx.rearrange("p t d m -> p (t d m)").unsqueeze(2).to_broadcast([P, 16, P]),
                              ALU.subtract).then_inc(s["em_sub"], 1)
            v.wait_ge(s["q_sq"], TB * (AKV + AH))
            vec.tensor_scalar(sq1, sq1, 1.0 / AD, EPS, ALU.mult, ALU.add).then_inc(s["q_ms"], 1)
            v.wait_ge(s["q_root"], 1)
            link(vec.reciprocal(sq1, sq1))
            for t in range(TB):
                for i in range(AKV + AH):
                    hv = raw[:, t, R_AK + i * AD:R_AK + (i + 1) * AD]
                    ins = vec.scalar_tensor_tensor(hv, hv, sq1[:, t, i:i + 1], gB_k if i < AKV else gB_q,
                                                   ALU.mult, ALU.mult)
            link(ins)

            def rotate(t):
                n = AKV + AH
                src = raw[:, t, R_AK:R_AK + n * AD].rearrange("p (n a x f) -> p n a x f", n=n, a=2, x=2)
                dst = qkr.rearrange("p (n a x f) -> p n a x f", n=n, a=2, x=2)
                t1, t2 = (rtmp[:, i].rearrange("p (n a f) -> p n a f", n=n, a=2) for i in range(2))
                if t:
                    v.wait_ge(s["atp_mm"], 3)
                cb, sn = ([m[:, t, a].unsqueeze(1).to_broadcast([P, n, 32]) for a in range(2)] for m in (rope_c, rope_s))
                for a in range(2):
                    vec.tensor_tensor(t1[:, :, a], src[:, :, a, 0], cb[a], ALU.mult)
                    ins = vec.tensor_tensor(t2[:, :, a], src[:, :, a, 1], sn[a], ALU.mult)
                link(ins)
                for a in range(2):
                    ins = vec.tensor_tensor(dst[:, :, a, 0], t1[:, :, a], t2[:, :, a], ALU.subtract)
                link(ins)
                for a in range(2):
                    vec.tensor_tensor(t1[:, :, a], src[:, :, a, 1], cb[a], ALU.mult)
                    ins = vec.tensor_tensor(t2[:, :, a], src[:, :, a, 0], sn[a], ALU.mult)
                link(ins)
                for a in range(2):
                    ins = vec.tensor_tensor(dst[:, :, a, 1], t1[:, :, a], t2[:, :, a], ALU.add)
                ins.then_inc(s["rope_done"], 1)
                v.wait_ge(s["rope_done"], t + 1)

            def convolve(c):
                v.wait_ge(s["mqk_evac"], c + 2)
                if c:
                    v.wait_ge(s["silu_done"], c)
                for j in range(CW):
                    for i in range(2):
                        src = mqkT[:, c + i, j:j + S]
                        wc = cvw[:, (c + i) * CW + j:(c + i) * CW + j + 1]
                        if j == 0:
                            ins = vec.tensor_scalar(cv[:, i], src, wc, None, ALU.mult)
                        else:
                            ins = vec.scalar_tensor_tensor(cv[:, i], src, wc, cv[:, i], ALU.mult, ALU.add)
                        if j == CW - 1:
                            ins.then_inc(s["conv_done"], 1)
                    if j < CW - 1:
                        link(ins)

            def attention(i):
                if 1 <= i <= AU:
                    u = i - 1
                    v.wait_ge(s["p_exp"], u + 1)
                    link(vec.reciprocal(prc[:, u % 2:u % 2 + 1], psm[:, u % 2:u % 2 + 1]))
                    vec.tensor_scalar(Pb[:, u % 2], Pb[:, u % 2], prc[:, u % 2:u % 2 + 1], None, ALU.mult
                                      ).then_inc(s["p_ready"], 1)
                if i < AU:
                    v.wait_ge(s["sc_mm"], i + 1)
                    if i >= 2:
                        v.wait_ge(s["p_exp"], i - 1)
                    link(vec.tensor_reduce(mxs[:, i % 2:i % 2 + 1], psum[SC_BANK[i % 2]][:, 0:S], X, ALU.max))
                    vec.tensor_scalar(nmx[:, i % 2:i % 2 + 1], mxs[:, i % 2:i % 2 + 1], -(AD ** -0.5), None, ALU.mult
                                      ).then_inc(s["nmax"], 1)

            for t in range(TB):
                rotate(t)
            for g in range(8 * N_MQK):
                n, hf, i = g // 8, g // 4 % 2, g % 4
                if hf == 0 and n and i % 2 == 1:
                    convolve(4 * (n - 1) + i - 1)
                if 0 <= g - AT0 < AU + 2:
                    attention(g - AT0)
            for c in range(4 * (N_MQK - 1), 4 * N_MQK, 2):
                convolve(c)
            v.wait_ge(s["silu_done"], 4 * N_MQK)
            kk = mqkT[:, MH * MC:2 * MH * MC, PAD:PAD + S]
            vec.tensor_scalar(kk, kk, MD ** -0.5, None, ALU.mult).then_inc(s["kscaled"], 1)
            v.wait_ge(s["em_ready"], 1)
            for i in range(MU + 1):
                if i < MU:
                    hd, t = i // 2, i % 2
                    v.wait_ge(s["s_mm"], i + 1)
                    if i >= 2:
                        v.wait_ge(s["at_mm"], i - 1)
                    vec.tensor_tensor(A[:, i % 2], psum[0][:, 0:P].unsqueeze(1).to_broadcast([P, 2, P]),
                                      Em[:, t, :, hd], ALU.mult).then_inc(s["a_ready"], 1)
                if i:
                    u = i - 1
                    hd, t = u // 2, u % 2
                    first, second = 6 + t, 6 + (1 - t)
                    v.wait_ge(s["i_ready"], u + 1)
                    v.wait_ge(s["n_mm"], 2 * (u + 1))
                    link(vec.tensor_tensor(num2, Isb[:, u % 2], psum[second][:, 0:MD + 1], ALU.add))
                    dens = ((psum[first][:, MD:MD + 1], t), (num2[:, MD:MD + 1], 1 - t))
                    for c, (den, d) in enumerate(dens):
                        w = 16 + (t * 2 + d) * MH + hd
                        ins = vec.scalar_tensor_tensor(dd[:, c:c + 1], den, -1.0, expo[:, w:w + 1], ALU.mult, ALU.max)
                    link(ins)
                    for c, (den, d) in enumerate(dens):
                        ins = vec.tensor_tensor(dd[:, c:c + 1], den, dd[:, c:c + 1], ALU.max)
                    link(ins)
                    link(vec.reciprocal(dr, dd))
                    link(vec.tensor_scalar(hm[:, t, hd], psum[first][:, 0:MD], dr[:, 0:1], None, ALU.mult))
                    vec.scalar_tensor_tensor(hm[:, t, hd], num2[:, 0:MD], dr[:, 1:2], hm[:, t, hd], ALU.mult, ALU.add
                                             ).then_inc(s["comb_done"], 1)
                    v.wait_ge(s["comb_done"], u + 1)
            v.wait_ge(s["y_sq"], TB * MH)
            vec.tensor_scalar(sq2, sq2, 1.0 / MD, EPS, ALU.mult, ALU.add).then_inc(s["y_ms"], 1)
            v.wait_ge(s["y_root"], 1)
            link(vec.reciprocal(sq2, sq2))
            for t in range(TB):
                for hd in range(MH):
                    ins = vec.scalar_tensor_tensor(hm[:, t, hd], hm[:, t, hd], sq2[:, t, hd:hd + 1],
                                                   mlg[:, hd * MD:(hd + 1) * MD], ALU.mult, ALU.mult)
            link(ins)
            v.wait_ge(s["mo_sig"], 1)
            for t in range(TB):
                hf_ = hm[:, t].rearrange("p m c -> p (m c)")
                vec.tensor_tensor(hf_, hf_, raw[:, t, R_MO:RAW], ALU.mult).then_inc(s["hm_ready"], 1)

            for n in range(NO):
                v.wait_ge(s["part_done"], n + 1)
                hv = h[:, 1, n * BANK:(n + 1) * BANK]
                vec.tensor_tensor(hv, psum[4 + n][:, :], hv, ALU.add).then_inc(s["part_added"], 1)

            def add_mixer(t):
                if t:
                    v.wait_ge(s["part_added"], NO)
                for i in range(NO):
                    n = NO - 1 - i if t else i
                    v.wait_ge(s["out_mm"], NO * t + i + 1)
                    hv = h[:, t, n * BANK:(n + 1) * BANK]
                    vec.tensor_tensor(hv, psum[n][:, :], hv, ALU.add).then_inc(s["h_ready"], 1)

            def blocks(t0, t1):
                return range(t0, t1), range(2 * t0, 2 * t1), slice(t0, t1), slice(2 * t0, 2 * t1)

            def route_halves(L, ev_, t0, t1):
                n0 = EVENTS * L + ev_
                ts, qs, tsl, qsl = blocks(t0, t1)
                hold(v, "sc_done", n0 + 1, "dve_passed")
                sc = psum[7][:, :].rearrange("p (q n) -> p q n", q=4)
                for q in qs:
                    ins = vec.max(s16[:, q, 0:8], sc[:, q])
                link(ins)
                for q in qs:
                    vec.match_replace(stmp[:, q], s16[:, q, 0:8], sc[:, q], NEG)
                for q in qs:
                    ins = vec.max_index(i16[:, q, 0:8], s16[:, q, 0:8], sc[:, q])
                ins.then_inc(s["sc_free"], 1)
                hold(v, "sc_free", n0 + 1, "dve_passed")
                for q in qs:
                    ins = vec.max(s16[:, q, 8:16], stmp[:, q])
                link(ins)
                for q in qs:
                    vec.max_index(i16[:, q, 8:16], s16[:, q, 8:16], stmp[:, q])
                for t in ts:
                    ins = vec.tensor_tensor(cand[:, t], s16[:, 2 * t].unsqueeze(2).to_broadcast([P, PK, PK]),
                                            s16[:, 2 * t + 1].unsqueeze(1).to_broadcast([P, PK, PK]), ALU.add)
                link(ins)

            def route_pairs(L, ev_, t0, t1):
                n0 = EVENTS * L + ev_
                ts, qs, tsl, qsl = blocks(t0, t1)
                vec.tensor_copy(i16f[:, qsl], i16[:, qsl])
                cf = cand.rearrange("p t a b -> p t (a b)")
                c2 = cand2.rearrange("p t a b -> p t (a b)")
                for t in ts:
                    ins = vec.max(b16[:, t, 0:8], cf[:, t])
                link(ins)
                for t in ts:
                    vec.match_replace(c2[:, t], b16[:, t, 0:8], cf[:, t], NEG)
                for t in ts:
                    ins = vec.max_index(pos[:, t, 0:8], b16[:, t, 0:8], cf[:, t])
                link(ins)
                for t in ts:
                    ins = vec.max(b16[:, t, 8:16], c2[:, t])
                link(ins)
                for t in ts:
                    vec.max_index(pos[:, t, 8:16], b16[:, t, 8:16], c2[:, t])
                vec.tensor_tensor(bd[:, tsl], b16[:, tsl], b16[:, tsl, 0:1].to_broadcast([P, t1 - t0, PK]), ALU.subtract
                                  ).then_inc(s["bd_ready"], 1)

            def route_experts(L, hd, ev_, t0, t1):
                n0 = EVENTS * L + ev_
                nt = t1 - t0
                ts, qs, tsl, qsl = blocks(t0, t1)
                hold(v, "bd_ready", n0 + 1, "dve_passed")
                vec.tensor_scalar(ab[:, tsl, 0], pos[:, tsl], 4, None, ALU.logical_shift_right)
                link(vec.tensor_scalar(ab[:, tsl, 1], pos[:, tsl], PK - 1, None, ALU.bitwise_and))
                link(vec.tensor_copy(abf[:, qsl], ab[:, tsl].rearrange("p t x k -> p (t x) k")))
                e64 = eq[:, qsl].rearrange("p q k a -> p (q k) a")
                link(vec.tensor_tensor(e64, abf[:, qsl].rearrange("p q k -> p (q k)").unsqueeze(2).to_broadcast([P, 32 * nt, PK]),
                                       iota16.unsqueeze(1).to_broadcast([P, 32 * nt, PK]), ALU.is_equal))
                link(vec.tensor_tensor(eq[:, qsl], eq[:, qsl], i16f[:, qsl].unsqueeze(2).to_broadcast([P, 2 * nt, PK, PK]), ALU.mult))
                link(vec.tensor_reduce(ev[:, tsl].rearrange("p t x k -> p (t x k)"), e64, X, ALU.add))
                link(vec.scalar_tensor_tensor(idx_all[:, :, :].rearrange("p (t g) k -> p t g k", t=TB)[:, tsl, bass.ds(hd, 1)]
                                              .rearrange("p t g k -> p t (g k)"),
                                              ev[:, tsl, 0], float(NK), ev[:, tsl, 1], ALU.mult, ALU.add))
                hold(v, "ex_done", n0 + 1, "dve_passed")
                link(vec.tensor_reduce(exs[:, tsl], ex[:, tsl], X, ALU.add))
                link(vec.reciprocal(exr[:, tsl], exs[:, tsl]))
                link(vec.tensor_tensor(gates.rearrange("p (t g) k -> p t g k", t=TB)[:, tsl, bass.ds(hd, 1)]
                                       .rearrange("p t g k -> p t (g k)"),
                                       ex[:, tsl], exr[:, tsl].unsqueeze(2).to_broadcast([P, nt, PK]), ALU.mult))

            def route(L, hd, ev_, t0, t1):
                route_halves(L, ev_, t0, t1)
                route_pairs(L, ev_, t0, t1)
                route_experts(L, hd, ev_, t0, t1)

            def copy_idx(g, buf, name):
                vec.tensor_copy(buf[:], idx_all[:, bass.ds(g, 1)].rearrange("p g k -> p (g k)")).then_inc(s[name], 1)

            def dot(L, g, par, k, xn):
                v.wait_ge(u_got[k % UR], 16 * (L * ROWS // UR + g * (PK // UR) + k // UR + 1))
                u = U[:, k % UR]
                vec.tensor_tensor_reduce(out=u, in0=u, in1=xn, scale=1.0, scalar=0.0, op0=ALU.mult, op1=ALU.add,
                                         accum_out=act[:, par, k:k + 1]).then_inc(s["dot_done"], 1)

            def weigh(L, g, par):
                hold(v, "gelu_done", L * GROUPS + g + 1, "dve_passed")
                vec.tensor_tensor(wk[:, par], ga, gates[:, bass.ds(g, 1)].rearrange("p g k -> p (g k)"), ALU.mult
                                  ).then_inc(s["wk_ready"], 1)

            def next_v(L, j, par):
                hold(v, "v_mm", L * ROWS + j * PK, "dve_passed")
                copy_idx(j + 1, idxV[1 - par], "idxv_ready")

            def next_u(L, j, par):
                hold(v, "dot_done", L * ROWS + j * PK + PK, "dve_passed")
                copy_idx(j + 2, idxU[par], "idxu_ready")

            def first_step(L):
                norm(1 + 2 * L, 1)
                for k in range(PK):
                    dot(L, 1, 1, k, xn0)
                    if k == 0:
                        weigh(L, 0, 0)
                        evac_xt(1 + L, 1)
                        copy_idx(1, idxV[1], "idxv_ready")
                    if k == 2:
                        route(L, 0, 2, 1, 2)
                    if k == 5:
                        route(L, 1, 3, 1, 2)
                    if k == 8:
                        route_halves(L, 4, 0, 2)
                    if k == 10:
                        route_pairs(L, 4, 0, 2)
                    if k == 11:
                        route_experts(L, 2, 4, 0, 2)
                    if k == 11:
                        next_u(L, 0, 0)

            def step(L, j, par, xn, route_head=None, last=False):
                for k in range(PK):
                    dot(L, j + 1, 1 - par, k, xn)
                    if k == 0:
                        weigh(L, j, par)
                    if k == 4:
                        next_v(L, j, par)
                    if route_head is not None:
                        if k == 5:
                            route_halves(L, route_head + 2, 0, 2)
                        if k == 7:
                            route_pairs(L, route_head + 2, 0, 2)
                        if k == 9:
                            route_experts(L, route_head, route_head + 2, 0, 2)
                    if k == 10 and not last:
                        next_u(L, j, par)

            def add_pooled(t):
                for g in range(4):
                    v.wait_ge(s["py_mm"], 4 * t + g + 1)
                    cols = slice(g * BANK, (g + 1) * BANK)
                    link(vec.tensor_tensor(ytmp[:, g % 2], psum[g][:, :], lsB[:, cols], ALU.mult))
                    vec.tensor_tensor(h[:, t, cols], h[:, t, cols], ytmp[:, g % 2], ALU.add).then_inc(s["h1_ready"], 1)

            def add_last_v(L):
                j = GROUPS - 1
                v.wait_ge(s["wk_ready"], (L + 1) * GROUPS)
                for n, k in enumerate(range(VR - 1, PK, VR)):
                    v.wait_ge(v_got[k % VR], 16 * (L * ROWS // VR + j * (PK // VR) + k // VR + 1))
                    w = wk[:, 1, k:k + 1]
                    if n == 0:
                        ins = vec.tensor_scalar(xn1, V[:, k % VR], w, None, ALU.mult)
                    else:
                        v.wait_ge(s["v_dve"], L * (PK // VR) + n)
                        ins = vec.scalar_tensor_tensor(xn1, V[:, k % VR], w, xn1, ALU.mult, ALU.add)
                    ins.then_inc(s["v_dve"], 1)
                v.wait_ge(s["v_mm"], (L + 1) * ROWS)
                for n in range(NO):
                    cols = slice(n * BANK, (n + 1) * BANK)
                    vec.tensor_tensor(h[:, 1, cols], psum[n][:, :], xn1[:, cols], ALU.add).then_inc(s["acc_evac"], 1)

            add_mixer(0)
            for L in range(LAYERS):
                if L:
                    norm(2, 1)
                    v.wait_ge(s["pool_ev"], KC // 2)
                    for q in range(4):
                        v.wait_ge(s["pool_mm"], KC // 2 + q + 1)
                        xq = xnT[:, 4 * q:4 * q + 4, 0:P]
                        vec.tensor_tensor(xq, psum[4 + q][:, :].rearrange("p (a b) -> p a b", a=4), xq, ALU.add
                                          ).then_inc(s["pool_add"], 1)
                    v.wait_ge(s["ld_scale"], 16)
                    add_pooled(0)
                    v.wait_ge(s["h1_ready"], 4)
                norm(1 + 2 * L, 0)
                evac_xt(1 + L, 0)
                route(L, 0, 0, 0, 1)
                copy_idx(0, idxU[0], "idxu_ready")
                copy_idx(0, idxV[0], "idxv_ready")
                if L:
                    add_pooled(1)
                    v.wait_ge(s["h1_ready"], 4 * TB)
                for k in range(PK):
                    dot(L, 0, 0, k, xn0)
                    if k == 4:
                        route_halves(L, 1, 0, 1)
                    if k == 6:
                        route_pairs(L, 1, 0, 1)
                    if k == 8:
                        route_experts(L, 1, 1, 0, 1)
                        copy_idx(1, idxU[1], "idxu_ready")
                    if k == 12 and L == 0:
                        add_mixer(1)
                first_step(L)
                step(L, 1, 1, xn0, route_head=3)
                n0 = st.n
                with v.Fori(1, 3) as jj:
                    st.base, st.n = n0 + (jj - 1) * (2 * ROUTE), 0
                    step(L, 2 * jj, 0, xn0, route_head=2 * jj + 2)
                    step(L, 2 * jj + 1, 1, xn0, route_head=2 * jj + 3)
                    assert st.n == 2 * ROUTE, st.n
                st.base, st.n = 0, n0 + 2 * 2 * ROUTE
                step(L, PH - 2, 0, xn0)
                step(L, PH - 1, 1, xn1)
                norm(2 + 2 * L, 0)
                with v.Fori(PH // 2, PH - 1) as jj:
                    step(L, 2 * jj, 0, xn1)
                    step(L, 2 * jj + 1, 1, xn1)
                step(L, GROUPS - 2, 0, xn1, last=True)
                weigh(L, GROUPS - 1, 1)
                add_last_v(L)
            norm(4, 1)

        @block.tensor
        def _(pe):
            mm = nc.tensor.matmul
            tr = nc.tensor.transpose

            def transpose_xn(o, norm_o, t, src):
                pe.wait_ge(s["xn_ready"], TB * norm_o + t + 1)
                for q in range(4):
                    if 4 * o + 2 * t:
                        pe.wait_ge(s["xt_act" if q % 2 == 0 else "xt_dve"], 4 * o + 2 * t)
                    for i in range(4):
                        k = 4 * q + i
                        ins = tr(psum[4 + q][:, i * P:(i + 1) * P], src[:, k * P:(k + 1) * P], ident)
                    ins.then_inc(s["tp_done"], 1)

            def straight_half(i, r, hf, middle=None, after=None):
                slot, got = w_half(i)
                pe.wait_ge(w_got[slot], got)
                for t in range(TB):
                    if hf == 0 and r:
                        pe.wait_ge(s["raw_evac"], TB * (r - 1) + t + 1)
                    for k in range(HALF):
                        ins = mm(psum[4 + t][:, :], xnT[:, HALF * hf + k, t * P:(t + 1) * P], wslot[slot][:, k],
                                 start=hf == 0 and k == 0, stop=hf == 1 and k == HALF - 1)
                        if k == HALF // 2 - 1 and middle is not None:
                            middle(t)
                    if hf == 1:
                        ins.then_inc(s["raw_done"], 1)
                    elif t == 1:
                        ins.then_inc(s["w_used"], 1)
                    if after is not None:
                        after(t)

            pe.wait_ge(s["ld_c"], 16)
            for t in range(TB):
                transpose_xn(0, 0, t, nrm0[:, t])
            pe.wait_ge(s["xt_act"], 4)
            pe.wait_ge(s["xt_dve"], 4)
            straight_half(0, 0, 0)
            pe.wait_ge(s["ld_small"], 6 * 16)
            for t in range(TB):
                for k in range(KC):
                    ins = mm(psum[6][:, 4 * MH * t:4 * MH * (t + 1)], xnT[:, k, t * P:(t + 1) * P], wg[:, k],
                             start=k == 0, stop=k == KC - 1)
            ins.then_inc(s["gates_mm"], 1)
            straight_half(1, 0, 1)
            pe.wait_ge(s["lf_ready"], 1)
            for t in range(TB):
                for d, tri in enumerate((tri_f, tri_b)):
                    c = (2 * t + d) * MH
                    mm(psum[7][:, c:c + MH], tri, lf[:, t, d], start=True, stop=True)
                    ins = mm(psum[7][:, 16 + c:16 + c + MH], ones, lf[:, t, d], start=True, stop=True)
            ins.then_inc(s["cum_done"], 1)
            straight_half(2, 1, 0)
            pe.wait_ge(s["scol_ready"], 1)
            for t in range(TB):
                for d in range(2):
                    for m in range(MH):
                        ins = mm(psum[2 * t + d][:, m * P:(m + 1) * P], scol[:, t, d, m:m + 1].to_broadcast([P, P]), ident,
                                 start=True, stop=True)
                    ins.then_inc(s["srow_done"], 1)
            straight_half(3, 1, 1)
            straight_half(4, 2, 0)
            straight_half(5, 2, 1)

            def attention(i):
                if i < AU:
                    hd, t = i // 2, i % 2
                    if i >= 2:
                        pe.wait_ge(s["p_exp"], i - 1)
                    mm(psum[SC_BANK[i % 2]][:, 0:S], aT[:, AKV + hd, t * P:(t + 1) * P], aT[:, hd // (AH // AKV)],
                       start=True, stop=True).then_inc(s["sc_mm"], 1)
                if 1 <= i <= AU:
                    u = i - 1
                    pe.wait_ge(s["p_ready"], u + 1)
                    if u:
                        pe.wait_ge(s["pt_ready"], u)
                    for c in range(2):
                        ins = tr(psum[1][:, c * P:(c + 1) * P], Pb[:, u % 2, c * P:(c + 1) * P], ident)
                    ins.then_inc(s["pt_mm"], 1)
                if i >= 2:
                    u = i - 2
                    kv = u // 2 // (AH // AKV)
                    pe.wait_ge(s["pt_ready"], u + 1)
                    if u:
                        pe.wait_ge(s["yt_ready"], u)
                    for c in range(2):
                        ins = mm(psum[2][:, 0:P], raw[:, c, R_AV + kv * AD:R_AV + (kv + 1) * AD],
                                 PT[:, u % 2, c], start=c == 0, stop=c == 1)
                    ins.then_inc(s["pv_mm"], 1)

            for g in range(8 * N_MQK):
                n, hf, i = g // 8, g // 4 % 2, g % 4
                slot, got = w_half(2 * N_QKV + 2 * n + hf)
                if i == 0:
                    pe.wait_ge(w_got[slot], got)
                if hf == 0:
                    if n == 0:
                        pe.wait_ge(s["raw_evac"], TB * N_QKV)
                        pe.wait_ge(s["scol_ready"], 1)
                    else:
                        pe.wait_ge(s["mqk_evac"], 4 * (n - 1) + i + 1)
                for k in range(HALF):
                    ins = mm(psum[4 + i][:, 0:S], wslot[slot][:, k, i * P:(i + 1) * P], xnT[:, HALF * hf + k, :],
                             start=hf == 0 and k == 0, stop=hf == 1 and k == HALF - 1)
                if hf == 1:
                    ins.then_inc(s["mqk_done"], 1)
                elif i == 3:
                    ins.then_inc(s["w_used"], 1)
                if g in ATP:
                    t = ATP.index(g)
                    pe.wait_ge(s["rope_done"], t + 1)
                    for q in range(3):
                        m = 3 * t + q
                        if m >= 2:
                            pe.wait_ge(s["atp_ready"], m - 1)
                        for c in range(4 * q, min(4 * q + 4, AKV + AH)):
                            ins = tr(psum[2 + m % 2][:, c % 4 * P:(c % 4 + 1) * P], qkr[:, c * P:(c + 1) * P], ident)
                        ins.then_inc(s["atp_mm"], 1)
                if g == AT0:
                    pe.wait_ge(s["atp_ready"], 3 * TB)
                if 0 <= g - AT0 < AU + 2:
                    attention(g - AT0)
            w0 = 2 * (N_QKV + N_MQK)
            pe.wait_ge(s["mqk_evac"], 4 * N_MQK)
            straight_half(w0, N_QKV, 0)
            straight_half(w0 + 1, N_QKV, 1)
            pe.wait_ge(s["kscaled"], 1)
            for t in range(TB):
                for hp in range(2):
                    if t:
                        pe.wait_ge(s["kw_ready"], 2 * hp + 2)
                    for i in range(4):
                        c = MH * MC + 4 * hp + i
                        ins = tr(psum[6 + hp][:, i * P:(i + 1) * P], mqkT[:, c, PAD + t * P:PAD + (t + 1) * P], ident)
                    ins.then_inc(s["ktp_done"], 1)
                if t == 0:
                    straight_half(w0 + 2, N_QKV + 1, 0)
            straight_half(w0 + 3, N_QKV + 1, 1)

            def mlstm(i):
                if i < MU:
                    hd, t = i // 2, i % 2
                    if i:
                        pe.wait_ge(s["a_ready"], i)
                    for c in range(MC):
                        ins = mm(psum[0][:, 0:P], mqkT[:, MC * hd + c, PAD + t * P:PAD + (t + 1) * P],
                                 mqkT[:, MC * (MH + hd) + c, PAD + t * P:PAD + (t + 1) * P], start=c == 0, stop=c == MC - 1)
                    ins.then_inc(s["s_mm"], 1)
                    d = 1 - t
                    if i >= 2:
                        pe.wait_ge(s["i_ready"], i - 1)
                    for c in range(MC):
                        if i:
                            pe.wait_ge(s["c_ready"], MC * (i - 1) + c + 1)
                        kwc = kw[:, d, hd, c * P:(c + 1) * P]
                        mm(psum[2 + c][:, 0:MD], kwc, raw[:, d, R_MV + hd * MD:R_MV + (hd + 1) * MD], start=True, stop=True)
                        mm(psum[2 + c][:, MD:MD + 1], kwc, ones[:, 0:1], start=True, stop=True).then_inc(s["c_mm"], 1)
                if i:
                    u = i - 1
                    hd, t = u // 2, u % 2
                    pe.wait_ge(s["a_ready"], u + 1)
                    if u:
                        pe.wait_ge(s["at_ready"], u)
                    for d in range(2):
                        ins = tr(psum[1][:, d * P:(d + 1) * P], A[:, u % 2, d], ident)
                    ins.then_inc(s["at_mm"], 1)

            def mlstm_sums(i):
                if i > 0:
                    u = i - 1
                    hd, t = u // 2, u % 2
                    pe.wait_ge(s["c_ready"], MC * (u + 1))
                    if i < MU:
                        pe.wait_ge(s["c_ready"], MC * i + 1)
                    else:
                        pe.wait_ge(s["i_ready"], u)
                    for c in range(MC):
                        ins = mm(psum[2][:, 0:MD + 1], mqkT[:, MC * hd + c, PAD + t * P:PAD + (t + 1) * P],
                                 Csb[:, u % 2, c], start=c == 0, stop=c == MC - 1)
                    ins.then_inc(s["i_mm"], 1)
                    pe.wait_ge(s["at_ready"], u + 1)
                    if u:
                        pe.wait_ge(s["comb_done"], u)
                    for d in range(2):
                        mm(psum[6 + d][:, 0:MD], AT[:, u % 2, d], raw[:, t, R_MV + hd * MD:R_MV + (hd + 1) * MD],
                           start=True, stop=True)
                        mm(psum[6 + d][:, MD:MD + 1], AT[:, u % 2, d], ones[:, 0:1], start=True, stop=True
                           ).then_inc(s["n_mm"], 1)

            pe.wait_ge(s["kw_ready"], 2 * MH)
            pe.wait_ge(s["raw_evac"], TB * (N_QKV + N_MV))
            pe.wait_ge(s["em_sub"], 1)
            for g in range(2 * N_MV):
                straight_half(w0 + 2 * N_MV + g, N_QKV + N_MV + g // 2, g % 2,
                              middle=lambda t: mlstm_sums(2 * g + t - 1), after=lambda t: mlstm(2 * g + t))
            mlstm_sums(MU - 1)
            mlstm(MU)
            mlstm_sums(MU)

            def project_attention(n):
                slot, got = w_half(2 * N_IN + n)
                pe.wait_ge(w_got[slot], got)
                for t in range(TB):
                    for k in range(HALF):
                        ins = mm(psum[4 * t + n][:, :], yT[:, k, t * P:(t + 1) * P], wslot[slot][:, k],
                                 start=k == 0, stop=t == 1 and k == HALF - 1)
                ins.then_inc(s["part_done"], 1)

            def project_mlstm(t, n):
                slot, got = w_half(LAST_HALF if t and n == 0 else 2 * N_IN + NO + n)
                pe.wait_ge(w_got[slot], got)
                if t:
                    pe.wait_ge(s["h_ready"], n + 1)
                for k in range(HALF):
                    ins = mm(psum[n][:, :], yT[:, HALF + k, t * P:(t + 1) * P], wslot[slot][:, k],
                             start=t == 1 and k == 0, stop=k == HALF - 1)
                ins.then_inc(s["out_mm"], 1)

            pe.wait_ge(s["comb_done"], MU)
            pe.wait_ge(s["yt_ready"], AU)
            pe.wait_ge(s["raw_evac"], TB * RAW // BANK)
            for n in range(NO - 1):
                project_attention(n)
            pe.wait_ge(s["part_added"], 2)
            for m in range(2 * TB):
                t, q = m // 2, m % 2
                pe.wait_ge(s["hm_ready"], t + 1)
                if t:
                    pe.wait_ge(s["ymt_ready"], q + 1)
                for i in range(4):
                    c = 4 * q + i
                    ins = tr(psum[4 + q][:, i * P:(i + 1) * P], hm[:, t].rearrange("p m c -> p (m c)")[:, c * P:(c + 1) * P], ident)
                ins.then_inc(s["ymt_mm"], 1)
            project_attention(NO - 1)
            pe.wait_ge(s["ymt_ready"], 2 * TB)
            for n in range(NO):
                project_mlstm(0, n)

            def queries(L, hd, par, ev_, t0, t1):
                n0 = EVENTS * L + ev_
                pe.wait_ge(ld_wq[par], 16 * (L * (PH // 2) + (hd - par) // 2 + 1) if isinstance(hd, int) else
                           16 * (L * (PH // 2) + 1) + 8 * (hd - par))
                if n0 if isinstance(n0, int) else True:
                    pe.wait_ge(s["q_ready"], n0)
                for p_ in range(2):
                    for k in range(KC):
                        ins = mm(psum[6][:, p_ * S + t0 * P:p_ * S + t1 * P], wqb[:, par, k, p_ * P:(p_ + 1) * P],
                                 xnT[:, k, t0 * P:t1 * P], start=k == 0, stop=k == KC - 1)
                ins.then_inc(s["q_mm"], 1)

            def scores(L, hd, ev_, t0, t1):
                n0 = EVENTS * L + ev_
                pe.wait_ge(s["q_ready"], n0 + 1)
                if n0 if isinstance(n0, int) else True:
                    pe.wait_ge(s["sc_free"], n0)
                for t in range(t0, t1):
                    for p_ in range(2):
                        ins = mm(psum[7][:, (2 * t + p_) * P:(2 * t + p_ + 1) * P], qT[:, p_, t * P:(t + 1) * P],
                                 keysT[:, bass.ds(2 * hd + p_, 1)].rearrange("p a n -> p (a n)"), start=True, stop=True)
                ins.then_inc(s["sc_done"], 1)

            def pool_block0(n):
                if n >= 4:
                    pe.wait_ge(s["pool_ev"], n - 3)
                for i in range(2):
                    c = 2 * n + i
                    ins = mm(psum[4 + n % 4][:, i * S:(i + 1) * S], xn0[:, c * P:(c + 1) * P], PM[:, c // 4, 0],
                             start=True, stop=True)
                ins.then_inc(s["pool_mm"], 1)

            def project_pooled(t, g):
                if t:
                    pe.wait_ge(s["h1_ready"], g + 1)
                for c in range(4):
                    ins = mm(psum[g][:, :], xnT[:, 4 * g + c, t * P:(t + 1) * P], poolw[:, g, c], start=c == 0, stop=c == 3)
                ins.then_inc(s["py_mm"], 1)

            def add_v(L, j, k, last=False):
                if last == "shared" and k % VR == VR - 1:
                    pe.wait_ge(s["v_mm"], L * ROWS + j * PK + k)
                    pe.wait_ge(s["v_dve"], L * (PK // VR) + k // VR + 1)
                    pe.sem_inc(s["v_mm"], 1)
                    return
                pe.wait_ge(v_got[k % VR], 16 * (L * ROWS // VR + j * (PK // VR) + k // VR + 1))
                pe.wait_ge(s["diag_ready"], L * (ROWS - PK // VR) + j * PK + k + 1 - (k // VR if last == "shared" else 0))
                for n in range(NO):
                    ins = mm(psum[n][:, :], diag[:, k % DR], V[:, k % VR, n * BANK:(n + 1) * BANK],
                             start=False,
                             stop=bool(last) and k == (PK - 2 if last == "shared" else PK - 1))
                ins.then_inc(s["v_mm"], 1)

            def first_step(L):
                for k in range(PK):
                    add_v(L, 0, k)
                    if k == 0:
                        transpose_xn(1 + L, 1 + 2 * L, 1, xn1)
                        pe.wait_ge(s["xt_act"], 4 * (2 + L))
                        pe.wait_ge(s["xt_dve"], 4 * (2 + L))
                    if k == 1:
                        queries(L, 0, 0, 2, 1, 2)
                    if k == 2:
                        scores(L, 0, 2, 1, 2)
                        queries(L, 1, 1, 3, 1, 2)
                    if k == 4:
                        scores(L, 1, 3, 1, 2)
                    if k == 6:
                        queries(L, 2, 0, 4, 0, 2)
                    if k == 8:
                        scores(L, 2, 4, 0, 2)

            def step(L, j, par, route_head=None, last=False, pool=False):
                if pool:
                    pe.wait_ge(s["xn_ready"], 5)
                    pe.wait_ge(s["ld_pm"], 16)
                for k in range(PK):
                    add_v(L, j, k, last)
                    if pool and k < KC // 2:
                        pool_block0(k)
                    if route_head is not None and k == 2:
                        queries(L, route_head, par, route_head + 2, 0, 2)
                    if route_head is not None and k == 4:
                        scores(L, route_head, route_head + 2, 0, 2)

            def seed(L, b):
                for n in range(NO):
                    mm(psum[n][:, :], ident, h[:, b, n * BANK:(n + 1) * BANK], start=True, stop=False)

            for L in range(LAYERS):
                if L:
                    pe.wait_ge(s["xn_ready"], 6)
                    pe.wait_ge(s["pool_ev"], KC // 2)
                    for q in range(4):
                        for i in range(4):
                            c = 4 * q + i
                            ins = mm(psum[4 + q][:, i * P:(i + 1) * P], xn1[:, c * P:(c + 1) * P], PM[:, q, 1, 0:P],
                                     start=True, stop=True)
                        ins.then_inc(s["pool_mm"], 1)
                    pe.wait_ge(s["ld_pool"], 16)
                    pe.wait_ge(s["acc_evac"], TB * NO)
                    for g in range(4):
                        pe.wait_ge(s["pool_add"], g + 1)
                        project_pooled(0, g)
                    for q in range(4):
                        for i in range(4):
                            c = 4 * q + i
                            mm(psum[4 + q][:, i * P:(i + 1) * P], xn1[:, c * P:(c + 1) * P], PM[:, q, 1, P:S],
                               start=i == 0, stop=False)
                        mm(psum[4 + q][:, :], ident, xnT[:, 4 * q:4 * q + 4, P:S], start=False, stop=True
                           ).then_inc(s["pool_mm"], 1)
                    pe.wait_ge(s["pool_ev"], KC // 2 + 4)
                else:
                    project_mlstm(1, 3)
                transpose_xn(1 + L, 1 + 2 * L, 0, xn0)
                pe.wait_ge(s["ld_keys"], 16 * (L + 1))
                pe.wait_ge(s["xt_act"], 4 * (1 + L) + 2)
                pe.wait_ge(s["xt_dve"], 4 * (1 + L) + 2)
                queries(L, 0, 0, 0, 0, 1)
                scores(L, 0, 0, 0, 1)
                if L == 0:
                    project_mlstm(1, 2)
                if L:
                    for g in range(4):
                        project_pooled(1, g)
                queries(L, 1, 1, 1, 0, 1)
                if L == 0:
                    project_mlstm(1, 1)
                scores(L, 1, 1, 0, 1)
                if L == 0:
                    project_mlstm(1, 0)
                    pe.wait_ge(s["h_ready"], TB * NO)
                else:
                    pe.wait_ge(s["h1_ready"], 4 * TB)
                seed(L, 0)
                first_step(L)
                step(L, 1, 1, route_head=3)
                with pe.Fori(1, 3) as jj:
                    step(L, 2 * jj, 0, route_head=2 * jj + 2)
                    step(L, 2 * jj + 1, 1, route_head=2 * jj + 3)
                step(L, PH - 2, 0)
                step(L, PH - 1, 1, last=True)
                pe.wait_ge(s["acc_evac"], TB * NO * L + NO)
                seed(L, 1)
                with pe.Fori(PH // 2, PH - 1) as jj:
                    step(L, 2 * jj, 0)
                    step(L, 2 * jj + 1, 1)
                step(L, GROUPS - 2, 0, pool=L == 0)
                step(L, GROUPS - 1, 1, last="shared")


def _constants(np):
    i = np.arange(P)
    tri = (i[:, None] <= i[None, :]).astype(np.float32)
    ropes = []
    tok = np.arange(S)
    posn = np.stack([tok // 64, tok % 64], -1).astype(np.float32)
    nf = AD // 4
    inv = (10000.0 ** (-np.arange(nf, dtype=np.float32) / nf)).astype(np.float32)
    ang = posn[:, :, None] * inv
    for f in (np.cos, np.sin):
        ropes.append(f(ang).astype(np.float32).reshape(TB, P, 2 * nf).transpose(1, 0, 2).reshape(P, TB * 2 * nf))
    mask = np.where(i[None, :] <= i[:, None], np.float32(0), np.float32(NEG))
    consts = np.concatenate([np.eye(P), tri, tri.T, np.ones((P, P)), mask, mask.T, *ropes,
                             np.broadcast_to(np.arange(PK), (P, PK))], 1).astype(np.float32)
    pool = np.zeros((4, S, S), np.float32)
    for g, w in enumerate(POOLW):
        for t in range(S):
            lo, hi = max(t - w // 2, 0), min(t + w // 2, S)
            pool[g, lo:hi, t] = np.float32(1.0) / np.float32(hi - lo)
            pool[g, t, t] -= 1.0
    pool = pool.reshape(4, TB, P, S).transpose(2, 0, 1, 3).reshape(P, 4 * TB * S)
    return np.ascontiguousarray(consts), np.ascontiguousarray(pool)


def kernel(**inputs):
    import numpy as np
    import concourse.bacc as bacc
    from concourse.bass_utils import run_bass_kernel_spmd

    a = {k: np.asarray(v) for k, v in inputs.items()}

    def tiles(w, halves):
        n = w.shape[1] // BANK
        return w.reshape(halves, KC // halves, P, n, BANK).transpose(3, 0, 2, 1, 4).reshape(n, halves, P, -1)

    w_in = a["w_in"][0]
    aq, ak, av = AH * AD, AH * AD + AKV * AD, AH * AD + 2 * AKV * AD
    mq, mv = av + 2 * MH * MD, av + 3 * MH * MD
    mo = mv + MH * MD
    cols = [w_in[:, aq:ak], w_in[:, :aq], w_in[:, ak:av], w_in[:, av:mq], w_in[:, mq:mv], w_in[:, mv:mo]]
    w_proj = np.concatenate(cols, 1)
    consts, poolm = _constants(np)
    arrays = {
        "x": a["x"][0],
        "consts": consts,
        "poolm": poolm,
        "w_proj": tiles(w_proj, 2),
        "w_gates": w_in[:, mo:].reshape(KC, P, 4 * MH).transpose(1, 0, 2).reshape(P, -1),
        "w_out": tiles(a["w_out"][0], 2).transpose(1, 0, 2, 3).reshape(2 * NO, P, -1),
        "b_gate": a["b_gate"][0],
        "conv_w": a["conv_w"][0].reshape(CW, 4 * MH, P).transpose(2, 1, 0).reshape(P, -1),
        "q_gain": a["q_gain"][0],
        "k_gain": a["k_gain"][0],
        "ml_gain": a["ml_gain"][0],
        "gains": np.stack([a["norm_mix_g"][0], a["norm_ffn_g"][0], a["norm_mix_g"][1], a["norm_ffn_g"][1], a["norm_f"]]),
        "layer_scale": a["layer_scale"][0],
        "pool_w": a["pool_w"][0].reshape(4, 4, P, BANK).transpose(2, 0, 1, 3).reshape(P, -1),
        "wq": a["peer_wq"].reshape(LAYERS, KC, P, PH, 2 * P).transpose(0, 3, 2, 1, 4).reshape(LAYERS, PH, P, -1),
        "keys": a["peer_keys"].reshape(LAYERS, 2 * PH, NK, P).transpose(0, 3, 1, 2).reshape(LAYERS, P, -1),
        "pu0": a["peer_u"][0], "pv0": a["peer_v"][0], "pu1": a["peer_u"][1], "pv1": a["peer_v"][1],
    }
    nc = bacc.Bacc("TRN2", target_bir_lowering=False, num_devices=1)
    args = []
    for name in list(arrays):
        arrays[name] = np.ascontiguousarray(arrays[name])
        args.append(nc.dram_tensor(name, arrays[name].shape, mybir.dt.from_np(arrays[name].dtype),
                                   kind="ExternalInput").ap())
    args.append(nc.dram_tensor("out", (S, D), fp32, kind="ExternalOutput").ap())
    hybrid_encoder(nc, *args)
    r = run_bass_kernel_spmd(nc, [arrays], core_ids=[0])
    return r.results[0]["out"].reshape(1, S, D)
```
